# Optimizing a Trainium2 kernel written in Bass

```python
import jax, jax.numpy as jnp
from jax import lax
import numpy as np
import math

D_MODEL = 1024
BATCH = 1
SEQ = 512
DEPTH = 1

MIX_WIDTH = D_MODEL
CONV_WIDTH = MIX_WIDTH // 2
CONV_GROUPS = 8
CONV_K = 3
RET_WIDTH = MIX_WIDTH - CONV_WIDTH
RET_HEADS = 4
RET_HEAD_DIM = RET_WIDTH // RET_HEADS
RET_CHUNK = 128
ROPE_BASE = 10000.0
D_FF = 4 * D_MODEL
NORM_EPS = 1e-6
IN_COLS = 3 * CONV_WIDTH + 4 * RET_WIDTH


def rms_norm(x, g, eps=NORM_EPS):
    xf = x.astype(jnp.float32)
    y = xf * lax.rsqrt(jnp.mean(xf * xf, axis=-1, keepdims=True) + eps)
    return (y * g.astype(jnp.float32)).astype(x.dtype)

def group_rms_norm(x, g, n_groups, eps=NORM_EPS):
    shp = x.shape
    xg = x.reshape(shp[:-1] + (n_groups, shp[-1] // n_groups)).astype(jnp.float32)
    y = xg * lax.rsqrt(jnp.mean(xg * xg, axis=-1, keepdims=True) + eps)
    return (y.reshape(shp) * g.astype(jnp.float32)).astype(x.dtype)

def rotary(x, positions):
    half = x.shape[-1] // 2
    inv_freq = 1.0 / (ROPE_BASE ** (jnp.arange(half, dtype=jnp.float32) / half))
    ang = positions.astype(jnp.float32)[:, None] * inv_freq[None, :]
    cos = jnp.cos(ang)[None, :, None, :].astype(x.dtype)
    sin = jnp.sin(ang)[None, :, None, :].astype(x.dtype)
    x1, x2 = x[..., :half], x[..., half:]
    return jnp.concatenate([x1 * cos - x2 * sin, x2 * cos + x1 * sin], axis=-1)

def causal_dwconv3(u, w):
    up = jnp.pad(u, ((0, 0), (CONV_K - 1, 0), (0, 0)))
    s = u.shape[1]
    return up[:, 0:s] * w[0] + up[:, 1:s + 1] * w[1] + up[:, 2:s + 2] * w[2]

def chunkwise_retention(q, k, v):
    b, s, h, d = q.shape
    nc = s // RET_CHUNK
    dt = q.dtype
    to_chunks = lambda t: t.reshape(b, nc, RET_CHUNK, h, d).transpose(0, 3, 1, 2, 4)
    qc, kc, vc = to_chunks(q), to_chunks(k), to_chunks(v)

    log_gamma = jnp.log(1.0 - 2.0 ** (-5.0 - jnp.arange(h, dtype=jnp.float32)))
    idx = jnp.arange(RET_CHUNK, dtype=jnp.float32)
    diff = idx[:, None] - idx[None, :]
    intra_decay = jnp.where(diff[None] >= 0,
                            jnp.exp(log_gamma[:, None, None] * jnp.maximum(diff, 0.0)[None]),
                            0.0).astype(dt)
    zeta = jnp.exp(log_gamma[:, None] * (RET_CHUNK - 1 - idx)[None]).astype(dt)
    xi = jnp.exp(log_gamma[:, None] * (idx + 1.0)[None]).astype(dt)
    chunk_decay = jnp.exp(log_gamma * RET_CHUNK).astype(dt)

    scores = jnp.einsum('bhncd,bhnmd->bhncm', qc, kc) * intra_decay[None, :, None]
    o_intra = jnp.einsum('bhncm,bhnme->bhnce', scores, vc)

    kv = jnp.einsum('bhnmd,bhnme->nbhde', kc * zeta[None, :, None, :, None], vc)

    def step(state, kv_n):
        new_state = chunk_decay[None, :, None, None] * state + kv_n
        return new_state, state

    _, s_prev = lax.scan(step, jnp.zeros_like(kv[0]), kv)
    o_cross = jnp.einsum('bhncd,nbhde->bhnce', qc * xi[None, :, None, :, None], s_prev)

    o = o_intra + o_cross
    return o.transpose(0, 2, 3, 1, 4).reshape(b, s, h, d)

def hybrid_mixer(u, w_in, conv_w, conv_norm_g, ret_norm_g, w_out):
    b, s, _ = u.shape
    z = u @ w_in
    c0 = 3 * CONV_WIDTH
    cb, cc, ch = jnp.split(z[..., :c0], 3, axis=-1)
    rq, rk, rv, rg = jnp.split(z[..., c0:], 4, axis=-1)

    y_conv = cb * causal_dwconv3(cc * ch, conv_w)
    y_conv = group_rms_norm(y_conv, conv_norm_g, CONV_GROUPS)

    positions = jnp.arange(s)
    q = rotary(rq.reshape(b, s, RET_HEADS, RET_HEAD_DIM), positions)
    k = rotary(rk.reshape(b, s, RET_HEADS, RET_HEAD_DIM), positions) * (RET_HEAD_DIM ** -0.5)
    v = rv.reshape(b, s, RET_HEADS, RET_HEAD_DIM)
    o = chunkwise_retention(q, k, v).reshape(b, s, RET_WIDTH)
    y_ret = group_rms_norm(o, ret_norm_g, RET_HEADS) * jax.nn.silu(rg)

    return jnp.concatenate([y_conv, y_ret], axis=-1) @ w_out

def sq_relu_mlp(u, w_up, w_down):
    hdn = jax.nn.relu(u @ w_up)
    return (hdn * hdn) @ w_down

def first_inputs(seed: int = 0) -> dict:
    key = jax.random.key(seed)
    ks = jax.random.split(key, 11)
    f32 = jnp.float32
    x = jax.random.normal(ks[0], (BATCH, SEQ, D_MODEL), f32)
    norm1_g = 1.0 + 0.05 * jax.random.normal(ks[1], (D_MODEL,), f32)
    w_in = jax.random.normal(ks[2], (D_MODEL, IN_COLS), f32) * D_MODEL ** -0.5
    conv_w = jax.random.normal(ks[3], (CONV_K, CONV_WIDTH), f32) * CONV_K ** -0.5
    conv_norm_g = 1.0 + 0.05 * jax.random.normal(ks[4], (CONV_WIDTH,), f32)
    ret_norm_g = 1.0 + 0.05 * jax.random.normal(ks[5], (RET_WIDTH,), f32)
    w_out = jax.random.normal(ks[6], (MIX_WIDTH, D_MODEL), f32) * MIX_WIDTH ** -0.5
    norm2_g = 1.0 + 0.05 * jax.random.normal(ks[7], (D_MODEL,), f32)
    w_up = jax.random.normal(ks[8], (D_MODEL, D_FF), f32) * D_MODEL ** -0.5
    w_down = jax.random.normal(ks[9], (D_FF, D_MODEL), f32) * D_FF ** -0.5
    final_norm_g = 1.0 + 0.05 * jax.random.normal(ks[10], (D_MODEL,), f32)
    return {"x": x, "norm1_g": norm1_g, "w_in": w_in, "conv_w": conv_w,
            "conv_norm_g": conv_norm_g, "ret_norm_g": ret_norm_g, "w_out": w_out,
            "norm2_g": norm2_g, "w_up": w_up, "w_down": w_down,
            "final_norm_g": final_norm_g}

def first_block(x, norm1_g, w_in, conv_w, conv_norm_g, ret_norm_g, w_out,
              norm2_g, w_up, w_down, final_norm_g):
    h = x
    for _ in range(DEPTH):
        h = h + hybrid_mixer(rms_norm(h, norm1_g), w_in, conv_w, conv_norm_g, ret_norm_g, w_out)
        h = h + sq_relu_mlp(rms_norm(h, norm2_g), w_up, w_down)
    return rms_norm(h, final_norm_g)


HEAD_DIM = 64
N_FOX_HEADS = 8
N_DSA_HEADS = 8
N_IDX_HEADS = 4
IDX_DIM = 64
TOPK_MAX = 256
Q_BLOCK = 128
N_BUCKETS = 32
MAX_DISTANCE = 128
D_FF_2 = 4 * D_MODEL
EPS = 1e-6

FOX_W = N_FOX_HEADS * HEAD_DIM
DSA_W = N_DSA_HEADS * HEAD_DIM
SPLIT_SIZES = [
    FOX_W, FOX_W, FOX_W,
    N_FOX_HEADS,
    DSA_W, DSA_W, DSA_W,
    N_IDX_HEADS * IDX_DIM,
    IDX_DIM,
    N_IDX_HEADS,
    D_MODEL, D_MODEL,
]
D_IN = int(sum(SPLIT_SIZES))
SPLIT_POINTS = [int(v) for v in np.cumsum(SPLIT_SIZES)[:-1]]


def rmsnorm(x, g):
    xf = x.astype(jnp.float32)
    y = xf * lax.rsqrt(jnp.mean(xf * xf, axis=-1, keepdims=True) + EPS)
    return (y * g.astype(jnp.float32)).astype(x.dtype)

def t5_bucket(dist):
    n = jnp.maximum(dist, 0)
    max_exact = N_BUCKETS // 2
    is_small = n < max_exact
    nf = jnp.maximum(n, 1).astype(jnp.float32)
    large = max_exact + (jnp.log(nf / max_exact) / math.log(MAX_DISTANCE / max_exact)
                         * (N_BUCKETS - max_exact)).astype(jnp.int32)
    large = jnp.minimum(large, N_BUCKETS - 1)
    return jnp.where(is_small, n, large)

def forgetting_attention(q, k, v, cum_logf):
    B, S, H, Dh = q.shape
    n_blocks = S // Q_BLOCK
    scale = Dh ** -0.5
    Ft = jnp.transpose(cum_logf, (0, 2, 1))
    key_pos = jnp.arange(S)

    def block(i):
        start = i * Q_BLOCK
        qb = lax.dynamic_slice_in_dim(q, start, Q_BLOCK, axis=1)
        Fb = lax.dynamic_slice_in_dim(Ft, start, Q_BLOCK, axis=2)
        s = jnp.einsum('bqhd,bkhd->bhqk', qb, k).astype(jnp.float32) * scale
        s = s + Fb[..., :, None] - Ft[:, :, None, :]
        q_pos = start + jnp.arange(Q_BLOCK)
        mask = key_pos[None, :] <= q_pos[:, None]
        s = jnp.where(mask[None, None], s, -jnp.inf)
        p = jax.nn.softmax(s, axis=-1).astype(v.dtype)
        return jnp.einsum('bhqk,bkhd->bqhd', p, v)

    out = lax.map(block, jnp.arange(n_blocks))
    return jnp.transpose(out, (1, 0, 2, 3, 4)).reshape(B, S, H, Dh)

def indexer_sparse_attention(q, k, v, q_idx, k_idx, w_idx, rel_bias):
    B, S, H, Dh = q.shape
    n_blocks = S // Q_BLOCK
    topk = min(TOPK_MAX, S // 4)
    scale = Dh ** -0.5
    idx_scale = IDX_DIM ** -0.5
    key_pos = jnp.arange(S)
    gather = jax.vmap(lambda arr, ids: arr[ids])

    def block(i):
        start = i * Q_BLOCK
        qb = lax.dynamic_slice_in_dim(q, start, Q_BLOCK, axis=1)
        qib = lax.dynamic_slice_in_dim(q_idx, start, Q_BLOCK, axis=1)
        wib = lax.dynamic_slice_in_dim(w_idx, start, Q_BLOCK, axis=1)
        q_pos = start + jnp.arange(Q_BLOCK)
        sc = jnp.einsum('bqhd,bkd->bqhk', qib, k_idx).astype(jnp.float32) * idx_scale
        iscore = jnp.einsum('bqhk,bqh->bqk', jax.nn.relu(sc), wib.astype(jnp.float32))
        causal = key_pos[None, :] <= q_pos[:, None]
        iscore = jnp.where(causal[None], iscore, -jnp.inf)
        _, sel = lax.top_k(iscore, topk)
        kg = gather(k, sel)
        vg = gather(v, sel)
        logits = jnp.einsum('bqhd,bqkhd->bhqk', qb, kg).astype(jnp.float32) * scale
        dist = q_pos[None, :, None] - sel
        valid = dist >= 0
        bias = rel_bias[t5_bucket(dist)].astype(jnp.float32)
        logits = logits + jnp.transpose(bias, (0, 3, 1, 2))
        logits = jnp.where(valid[:, None], logits, -jnp.inf)
        p = jax.nn.softmax(logits, axis=-1).astype(vg.dtype)
        return jnp.einsum('bhqk,bqkhd->bqhd', p, vg)

    out = lax.map(block, jnp.arange(n_blocks))
    return jnp.transpose(out, (1, 0, 2, 3, 4)).reshape(B, S, H, Dh)

def second_inputs(seed: int = 0) -> dict:
    key = jax.random.key(seed)
    ks = jax.random.split(key, 16)
    D = D_MODEL
    nrm = lambda k, shape, s: jax.random.normal(k, shape, jnp.float32) * s
    return {
        "x": nrm(ks[0], (BATCH, SEQ, D), 1.0),
        "c": nrm(ks[1], (BATCH, D), 1.0),
        "w_ada": nrm(ks[2], (D, 6 * D), 0.5 * D ** -0.5),
        "b_ada": nrm(ks[3], (6 * D,), 0.02),
        "g_norm1": 1.0 + nrm(ks[4], (D,), 0.02),
        "w_in": nrm(ks[5], (D, D_IN), D ** -0.5),
        "b_forget": nrm(ks[6], (N_FOX_HEADS,), 0.1),
        "rel_bias": nrm(ks[7], (N_BUCKETS, N_DSA_HEADS), 0.5),
        "w_branch_fox": nrm(ks[8], (FOX_W, D), FOX_W ** -0.5),
        "w_branch_dsa": nrm(ks[9], (DSA_W, D), DSA_W ** -0.5),
        "w_out": nrm(ks[10], (D, D), D ** -0.5),
        "g_norm2": 1.0 + nrm(ks[11], (D,), 0.02),
        "w_mlp1": nrm(ks[12], (D, D_FF_2), D ** -0.5),
        "w_mlp2": nrm(ks[13], (D_FF_2, D), D_FF_2 ** -0.5),
        "g_final": 1.0 + nrm(ks[14], (D,), 0.02),
    }

def second_block(x, c, w_ada, b_ada, g_norm1, w_in, b_forget, rel_bias, w_branch_fox,
              w_branch_dsa, w_out, g_norm2, w_mlp1, w_mlp2, g_final):
    B, S, D = x.shape
    ada = (c @ w_ada + b_ada)[:, None, :]
    shift1, scale1, gate1, shift2, scale2, gate2 = jnp.split(ada, 6, axis=-1)

    for _ in range(DEPTH):
        h = rmsnorm(x, g_norm1) * (1.0 + scale1) + shift1
        proj = h @ w_in
        (q_f, k_f, v_f, f_logit, q_d, k_d, v_d, q_i, k_i, w_i,
         gate_fox, gate_dsa) = jnp.split(proj, SPLIT_POINTS, axis=-1)
        hs = (B, S, -1, HEAD_DIM)
        log_f = jax.nn.log_sigmoid((f_logit + b_forget).astype(jnp.float32))
        cum_logf = jnp.cumsum(log_f, axis=1)
        y_fox = forgetting_attention(q_f.reshape(hs), k_f.reshape(hs), v_f.reshape(hs),
                                     cum_logf).reshape(B, S, FOX_W)
        w_i = w_i * (N_IDX_HEADS ** -0.5)
        y_dsa = indexer_sparse_attention(
            q_d.reshape(hs), k_d.reshape(hs), v_d.reshape(hs),
            q_i.reshape(B, S, N_IDX_HEADS, IDX_DIM), k_i, w_i, rel_bias
        ).reshape(B, S, DSA_W)
        merged = (jax.nn.sigmoid(gate_fox) * (y_fox @ w_branch_fox)
                  + jax.nn.sigmoid(gate_dsa) * (y_dsa @ w_branch_dsa))
        x = x + gate1 * (merged @ w_out)

        h2 = rmsnorm(x, g_norm2) * (1.0 + scale2) + shift2
        x = x + gate2 * (jnp.square(jax.nn.relu(h2 @ w_mlp1)) @ w_mlp2)

    return rmsnorm(x, g_final)


def setup_inputs(seed=0):
    out = dict(first_inputs(seed))
    for name, value in second_inputs(seed + 1).items():
        if name != "x":
            out[name + "_2"] = value
    return out


def reference(
    x, norm1_g, w_in, conv_w, conv_norm_g, ret_norm_g, w_out, norm2_g, w_up, w_down,
    final_norm_g, c_2, w_ada_2, b_ada_2, g_norm1_2, w_in_2, b_forget_2, rel_bias_2,
    w_branch_fox_2, w_branch_dsa_2, w_out_2, g_norm2_2, w_mlp1_2, w_mlp2_2, g_final_2,
):
    x = first_block(
        x, norm1_g, w_in, conv_w, conv_norm_g, ret_norm_g, w_out, norm2_g, w_up, w_down,
        final_norm_g,
    )
    return second_block(
        x, c_2, w_ada_2, b_ada_2, g_norm1_2, w_in_2, b_forget_2, rel_bias_2, w_branch_fox_2,
        w_branch_dsa_2, w_out_2, g_norm2_2, w_mlp1_2, w_mlp2_2, g_final_2,
    )


_drawn_inputs = setup_inputs


def setup_inputs(seed=0):
    import zlib

    import numpy as np

    out = dict(_drawn_inputs(seed))
    spreads = {}
    factors = {'ret_norm_g': 2.887,
     'g_norm1_2': 5.156,
     'b_forget_2': 7.234,
     'g_norm2_2': 3.928,
     'g_final_2': 2.906}
    for name, (base, spread) in spreads.items():
        noise = np.random.default_rng([zlib.crc32(name.encode()), seed]).standard_normal(out[name].shape)
        drawn = base * np.exp(spread * noise) if base else spread * noise
        out[name] = __import__('jax').numpy.asarray(drawn.astype(out[name].dtype))
    for name, factor in factors.items():
        out[name] = (out[name] * factor).astype(out[name].dtype)
    return out
```

```python
from contextlib import ExitStack

import concourse.bass as bass
import numpy as np
from concourse import mybir

F32 = mybir.dt.float32
F32R = mybir.dt.float32r
BF16 = mybir.dt.bfloat16
ALU = mybir.AluOpType
ACT = mybir.ActivationFunctionType

P = 128
T = 512
NT = T // P
D = 1024
KC = D // P
QW = D // 2
NQ = QW // P
DFF = 4 * D
NF = DFF // D
HEADS = 8
HD = 64
IDX_HEADS = 4
TOPK = min(256, T // 4)
EPS = 1e-6
SLOTS = 4
AHEAD = 2
BUCKETS = 32
NREL = T + P
MASKED = -3.0e38
TAKEN = -3.4e38

SA, SB, TR, OU = 4, 5, 6, 7

W1_CB, W1_CC, W1_CH, W1_RQ, W1_RK, W1_RV, W1_RG = [n * QW for n in range(7)]
SPLITS = [QW] * 3 + [HEADS] + [QW] * 3 + [IDX_HEADS * HD, HD, IDX_HEADS, D, D]
(W2_FQ, W2_FK, W2_FV, W2_F, W2_DQ, W2_DK, W2_DV, W2_QI, W2_KI, W2_WI, W2_GF, W2_GD) = [
    sum(SPLITS[:n]) for n in range(12)]

VECS = [("norm1_g", KC), ("conv_w", 3 * NQ), ("conv_norm_g", NQ), ("ret_norm_g", NQ), ("norm2_g", KC),
        ("final_norm_g", KC), ("c_2", KC), ("g_norm1_2", KC), ("g_norm2_2", KC), ("g_final_2", KC),
        ("b_ada_2", 6 * KC)]
VAT = {}
_n = 0
for _name, _rows in VECS:
    VAT[_name] = _n
    _n += _rows
NVEC = _n

NORMS = ["n1", "n2", "nf", "n3", "n4", "n5"]
SPLIT_NORMS = ["n1", "n2", "n3", "n4"]
MLPS = ["mlp", "mlp2"]

TABS = [("ident", P), ("group64", P), ("flip8", P), ("causal", P), ("sel8", HEADS * P), ("onehot", NREL),
        ("cos", T), ("sin", T), ("decay", NQ * T)]
TAT = {}
_n = 0
for _name, _cols in TABS:
    TAT[_name] = _n
    _n += _cols
NTAB = _n
SMALL = TAT["sel8"]


def tables():
    t = np.zeros((P, NTAB), np.float32)
    r = np.arange(P)
    t[:, TAT["ident"]:][:, :P] = np.eye(P)
    t[:, TAT["group64"]:][:, :P] = (r[:, None] // HD) == (r[None, :] // HD)
    t[:, TAT["flip8"]:][:, :P] = 8.0 * np.eye(P)[::-1]
    t[:, TAT["causal"]:][:, :P] = np.where(r[None, :] <= r[:, None], 0.0, MASKED)
    for h in range(HEADS):
        t[h, TAT["sel8"] + h * P:TAT["sel8"] + (h + 1) * P] = -8.0
    n = np.maximum(T - 1 - np.arange(NREL), 0)
    large = 16 + (np.log(np.maximum(n, 1) / 16.0) / np.log(8.0) * 16).astype(np.int64)
    bucket = np.where(n < 16, n, np.minimum(large, BUCKETS - 1))
    t[:BUCKETS, TAT["onehot"]:][:, :NREL] = bucket[None, :] == np.arange(BUCKETS)[:, None]
    half = P // 2
    inv = (1.0 / (np.float32(10000.0) ** (np.arange(half, dtype=np.float32) / half))).astype(np.float32)
    ang = np.arange(T, dtype=np.float32)[None, :] * np.concatenate([inv, inv])[:, None]
    t[:, TAT["cos"]:][:, :T] = np.cos(ang)
    t[:, TAT["sin"]:][:, :T] = np.sin(ang) * np.where(r < half, 1.0, -1.0)[:, None]
    for h in range(NQ):
        gamma = 1.0 - 2.0 ** (-5.0 - h)
        diff = np.arange(T)[None, :] - r[:, None]
        t[:, TAT["decay"] + h * T:][:, :T] = np.where(diff >= 0, gamma ** np.maximum(diff, 0), 0.0) * P ** -0.5
    return t


def before(name):
    return KC * NORMS.index(name)


def split_before(name):
    return KC * SPLIT_NORMS.index(name)


def mlp_before(name):
    return NF * KC * MLPS.index(name)


def wait(eng, sem, n):
    if not isinstance(n, int) or n > 0:
        eng.wait_ge(sem, n)


class Stage:

    def __init__(self, before, n, k, dmas=()):
        self.base = [b + (before.n if before and s < before.k else 0)
                     for s, b in enumerate(before.base if before else [1] * SLOTS)]
        self.raws = [b + (16 * before.n * before.dmas[s] if before and s < before.k else 0)
                     for s, b in enumerate(before.raws if before else [0] * SLOTS)]
        self.n, self.k = n, k
        self.dmas = list(dmas) or [1] * SLOTS

    def turn(self, s, i):
        return self.base[s] + i

    def landed(self, s, i):
        return self.raws[s] + 16 * self.dmas[s] * (i + 1)


def build(nc, tab, x, norm1_g, w_in, conv_w, conv_norm_g, ret_norm_g, w_out, norm2_g, w_up, w_down,
          final_norm_g, c_2, w_ada_2, b_ada_2, g_norm1_2, w_in_2, b_forget_2, rel_bias_2,
          w_branch_fox_2, w_branch_dsa_2, w_out_2, g_norm2_2, w_mlp1_2, w_mlp2_2, g_final_2, out):
    ds = bass.ds
    rows = {"norm1_g": norm1_g, "conv_w": conv_w, "conv_norm_g": conv_norm_g, "ret_norm_g": ret_norm_g,
            "norm2_g": norm2_g, "final_norm_g": final_norm_g, "c_2": c_2, "g_norm1_2": g_norm1_2,
            "g_norm2_2": g_norm2_2, "g_final_2": g_final_2, "b_ada_2": b_ada_2}

    st_ret = Stage(None, NQ, 4)
    st_conv = Stage(st_ret, NQ, 3)
    st_out = Stage(st_conv, KC // 4, 4)
    st_mlp = Stage(st_out, NF * 4, 4)
    st_idx = Stage(st_mlp, 1, 4, [1, 1, 2, 2])
    st_att = Stage(st_idx, 2 * NQ, 3)
    st_bra = Stage(st_att, KC, 3, [1, 1, 2, 1])
    st_out2 = Stage(st_bra, KC // 4, 4)
    st_mlp2 = Stage(st_out2, NF * 4, 4)

    bias_rows = nc.dram_tensor("bias_rows", [HEADS, NREL], F32).ap()

    ctx = ExitStack()
    with ctx:
        def sb(name, shape, dt=F32, where=ctx):
            return where.enter_context(nc.sbuf_tensor(name, shape, dt))

        sems = {}

        def sem(name):
            if name not in sems:
                sems[name] = ctx.enter_context(nc.semaphore(name))
            return sems[name]

        xres = sb("xres", [P, KC, T])
        u_hi, u_lo = sb("u_hi", [P, KC, T], F32R), sb("u_lo", [P, KC, T], F32R)
        y_hi, y_lo = sb("y_hi", [P, KC, T], F32R), sb("y_lo", [P, KC, T], F32R)
        raw = sb("raw", [P, SLOTS, KC * P])
        w_hi, w_lo = sb("w_hi", [P, SLOTS, KC * P], F32R), sb("w_lo", [P, SLOTS, KC * P], F32R)
        small = sb("small", [P, SMALL])
        ident = small[:, TAT["ident"]:TAT["ident"] + P]
        group64 = small[:, TAT["group64"]:TAT["group64"] + P]
        flip8 = small[:, TAT["flip8"]:TAT["flip8"] + P]
        identb, causalb = sb("identb", [P, P], BF16), sb("causalb", [P, P], BF16)
        ones = sb("ones", [P, P])
        epsc = sb("epsc", [P, 1])
        vec = sb("vec", [P, NVEC])
        ada = sb("ada", [P, 6 * KC])
        gain1, gain2 = sb("gain1", [P, KC]), sb("gain2", [P, KC])
        bfor = sb("bfor", [HEADS, 1])
        rowsum, rinv, mneg = sb("rowsum", [P, 8]), sb("rinv", [P, 8]), sb("mneg", [P, 8])
        wtok = sb("wtok", [P, NT * IDX_HEADS])
        top8 = sb("top8", [P, 8])
        nt = sb("nt", [P, 3, T])
        nsq = sb("nsq", [P, 2, T])
        nrs = sb("nrs", [P, T])

        one = ExitStack()
        decay = sb("decay", [P, NQ, T], where=one)
        start = ExitStack()
        xtok = sb("xtok", [P, NT, D], where=start)
        start.close()
        acc = sb("acc", [P, 6 * D], where=one)
        mix = ExitStack()
        rope = sb("rope", [P, 2, T], where=mix)
        cosr, sinr = rope[:, 0, :], rope[:, 1, :]
        vf, vtok = sb("vf", [P, T], where=mix), sb("vtok", [P, NT, P], where=mix)
        qf, kf = sb("qf", [P, T], where=mix), sb("kf", [P, T], where=mix)
        sdec = sb("sdec", [P, NT, T], where=mix)
        osb, sg, silu = sb("osb", [P, T], where=mix), sb("sg", [P, T], where=mix), sb("silu", [P, T], where=mix)
        prod, ycv = sb("prod", [P, T + 2], where=mix), sb("ycv", [P, T], where=mix)
        ccs = vf
        mix.close()
        adaw = sb("adaw", [P, 2, 6 * D // 4], where=one)
        one.close()
        pre = ExitStack()
        vrow = sb("vrow", [NVEC, P], where=pre)
        oneh = sb("oneh", [BUCKETS, NREL], where=pre)
        rbias = sb("rbias", [BUCKETS, HEADS], where=pre)
        fbrow = sb("fbrow", [HEADS, NREL], where=pre)
        pre.close()

        two = ExitStack()
        merge = ExitStack()
        ftab, btab = sb("ftab", [P, HEADS, T], where=merge), sb("btab", [P, HEADS, T], where=merge)
        merge.close()
        m_hi, m_lo = sb("m_hi", [P, KC, T], F32R, where=two), sb("m_lo", [P, KC, T], F32R, where=two)
        qa, ka = sb("qa", [P, T], where=two), sb("ka", [P, T], where=two)
        va, vatok = sb("va", [P, T], where=two), sb("vatok", [P, NT, P], where=two)
        work = sb("work", [P, NT - 1, T], where=two)
        sel = sb("sel", [P, NT, T], BF16, where=two)
        index = ExitStack()
        qi, ki = sb("qi", [P, 2, T], where=index), sb("ki", [P, T], where=index)
        fw = sb("fw", [P, T], where=index)
        sel8 = sb("sel8", [HEADS, HEADS * P], where=index)
        index.close()
        prob = sb("prob", [P, 2, T], where=two)
        probt = sb("probt", [P, NT, T], where=two)
        two.close()
        last = ExitStack()
        otok = sb("otok", [P, 2, D], where=last)
        last.close()

        ps = ctx.enter_context(nc.psum_tensor("ps", [P, 8, T], F32))

        raw_ready = [sem(f"raw_ready{s}") for s in range(SLOTS)]
        hi_ready = [sem(f"hi_ready{s}") for s in range(SLOTS)]
        lo_ready = [sem(f"lo_ready{s}") for s in range(SLOTS)]
        used = [sem(f"used{s}") for s in range(SLOTS)]
        bank_free = [sem(f"bank_free{s}") for s in range(SLOTS)]

        block = ctx.enter_context(nc.Block())

        @block.sync
        def _(sp):
            def load(st, s, i, *pairs):
                if st.raws[s] == 0:
                    sp.wait_ge(sem("x_in0"), 16)
                else:
                    sp.wait_ge(raw_ready[s], st.raws[s])
                wait(sp, lo_ready[s], st.turn(s, i))
                dst = raw[:, s, :].rearrange("p (k m) -> p k m", k=KC)
                for cut, src in pairs:
                    sp.dma_start(cut(dst), src).then_inc(raw_ready[s], 16)

            def whole(dst):
                return dst

            def cols(w, at, n=P):
                return w.rearrange("(k p) n -> p k n", p=P)[:, :, ds(at, n)]

            for i in range(NT):
                sp.dma_start(xtok[:, i, :], x[0, i * P:(i + 1) * P, :]).then_inc(sem(f"x_in{i}"), 16)
                if i == 0:
                    sp.dma_start(small[:], tab[:, 0:SMALL]).then_inc(sem("small_in"), 16)

            with sp.Fori(0, NQ) as j:
                for s, at in enumerate([W1_RV, W1_RQ, W1_RK, W1_RG]):
                    load(st_ret, s, j, (whole, cols(w_in, at + j * P)))
            with sp.Fori(0, NQ) as j:
                for s, at in enumerate([W1_CC, W1_CH, W1_CB]):
                    load(st_conv, s, j, (whole, cols(w_in, at + j * P)))
            with sp.Fori(0, KC // 4) as i:
                for s in range(4):
                    load(st_out, s, i, (whole, cols(w_out, i * 4 * P + s * P)))

            def mlp(st, up, down, with_ada):
                with sp.Fori(0, NF) as q:
                    for d in range(2):
                        with sp.Fori(0, 2) as i:
                            for s in range(4):
                                if d == 0:
                                    src = cols(up, q * D + i * 4 * P + s * P)
                                else:
                                    src = down.rearrange("(q k p) n -> q p k n", q=NF, p=P)[
                                        ds(q, 1), :, :, ds(i * 4 * P + s * P, P)
                                    ].rearrange("q p k n -> p (q k) n")
                                load(st, s, q * 4 + 2 * d + i, (whole, src))
                                if with_ada and s % 2:
                                    b = s // 2
                                    sp.wait_ge(sem(f"ada_used{b}"), q * 4 + 2 * d + i + 1)
                                    sp.wait_ge(sem("mix_done"), 1)
                                    src = w_ada_2.rearrange("(q k p) n -> q k p n", q=NF, p=P)[
                                        ds(q, 1), d, :, ds(i * 3 * D + b * 3 * D // 2, 3 * D // 2)]
                                    sp.dma_start(adaw[:, b, :], src.rearrange("q p n -> p (q n)")
                                                 ).then_inc(sem(f"ada_in{b}"), 16)

            mlp(st_mlp, w_up, w_down, True)

            load(st_idx, 0, 0, (whole, cols(w_in_2, W2_QI)))
            load(st_idx, 1, 0, (whole, cols(w_in_2, W2_QI + P)))
            load(st_idx, 2, 0, (lambda d: d[:, :, 0:HD], cols(w_in_2, W2_KI, HD)),
                 (lambda d: d[:, :, HD:P], cols(w_in_2, W2_KI, HD)))
            load(st_idx, 3, 0, (lambda d: d[:, :, 0:HEADS], cols(w_in_2, W2_F, HEADS)),
                 (lambda d: d[:, :, 32:32 + IDX_HEADS], cols(w_in_2, W2_WI, IDX_HEADS)))
            sp.wait_ge(sem("ada_sum"), 1)
            sp.wait_ge(sem("brow_out"), 16)
            shifted = bass.AP(bias_rows.tensor, 0, [[1, P], [NREL, HEADS], [1, T]])
            sp.dma_start(ftab[:], shifted).then_inc(sem("shifted_in"), 16)
            sp.dma_start(sel8[:], tab[0:HEADS, TAT["sel8"]:TAT["sel8"] + HEADS * P]).then_inc(sem("sel8_in"), 16)
            for base, at3 in ((0, (W2_FV, W2_FQ, W2_FK)), (NQ, (W2_DV, W2_DQ, W2_DK))):
                with sp.Fori(0, NQ) as g:
                    for s, at in enumerate(at3):
                        load(st_att, s, base + g, (whole, cols(w_in_2, at + g * P)))
            with sp.Fori(0, KC) as m:
                load(st_bra, 0, m, (whole, cols(w_in_2, W2_GF + m * P)))
                load(st_bra, 1, m, (whole, cols(w_in_2, W2_GD + m * P)))
                load(st_bra, 2, m, (lambda d: d[:, 0:NQ, :], cols(w_branch_fox_2, m * P)),
                     (lambda d: d[:, NQ:KC, :], cols(w_branch_dsa_2, m * P)))
            with sp.Fori(0, KC // 4) as i:
                for s in range(4):
                    load(st_out2, s, i, (whole, cols(w_out_2, i * 4 * P + s * P)))
            mlp(st_mlp2, w_mlp1_2, w_mlp2_2, False)

            for i in range(NT):
                sp.wait_ge(sem("otok0"), i + 1)
                sp.wait_ge(sem("otok1"), i + 1)
                sp.dma_start(out[0, i * P:(i + 1) * P, :], otok[:, i % 2, :]).then_inc(sem(f"out{i % 2}"), 16)
            sp.wait_ge(sem("out0"), 32)
            sp.wait_ge(sem("out1"), 32)

        @block.gpsimd
        def _(pool):
            for s in range(SLOTS):
                pool.sem_inc(lo_ready[s], 1)
            pool.memset(ones[:], 1.0).then_inc(sem("const"), 1)
            pool.memset(epsc[:], EPS).then_inc(sem("const"), 1)

            def lo(st, s, i):
                pool.wait_ge(hi_ready[s], st.turn(s, i) + 1)
                pool.tensor_tensor(w_lo[:, s, :], raw[:, s, :], w_hi[:, s, :], ALU.subtract
                                   ).then_inc(lo_ready[s], 1)

            for st in (st_ret, st_conv, st_out, st_mlp, st_idx, st_att, st_bra, st_out2, st_mlp2):
                if st.n == 1:
                    for s in range(st.k):
                        lo(st, s, 0)
                else:
                    with pool.Fori(0, st.n) as i:
                        for s in range(st.k):
                            lo(st, s, i)

        @block.tensor
        def _(pe):
            def unit(st, s, i, r_hi, r_lo, chunk_ready=None, part=(0, KC), cols=P, ks=range(KC), bank=None,
                     opens=True, closes=True):
                bank = s if bank is None else bank
                if opens:
                    pe.wait_ge(lo_ready[s], st.turn(s, i) + 1)
                    wait(pe, bank_free[s], st.turn(s, i))
                last = None
                for k in range(*part):
                    if chunk_ready:
                        chunk_ready(k)
                    c = slice(k * P, k * P + cols)
                    for w, r in ((w_hi, r_hi), (w_hi, r_lo), (w_lo, r_hi)):
                        last = pe.matmul(ps[0:cols, bank, :], w[:, s, c], r[:, k, :],
                                         start=(k == ks[0] and w is w_hi and r is r_hi),
                                         stop=(k == ks[-1] and w is w_lo))
                if closes:
                    last.then_inc(used[s], 1)

            def sums(name):
                for m in range(KC):
                    pe.wait_ge(sem("norm_sq"), before(name) + m + 1)
                    pe.matmul(ps[:, SA, :], ones[:], nsq[:, m % 2, :], start=(m == 0), stop=(m == KC - 1)
                              ).then_inc(sem("norm_sum"), 1)

            for s in range(SLOTS):
                pe.sem_inc(used[s], 1)
            pe.wait_ge(sem("small_in"), 16)
            pe.wait_ge(sem("vrow_in"), 16 * len(VECS))
            pe.transpose(ps[:, 3, 0:NVEC], vrow[:], ident[0:NVEC, 0:NVEC]).then_inc(sem("vec_turned"), 1)
            pe.wait_ge(sem("bias_in"), 32)
            pe.matmul(ps[0:HEADS, 1, :], rbias[:], oneh[:, 0:T], start=True, stop=True)
            pe.matmul(ps[0:HEADS, 2, 0:P], rbias[:], oneh[:, T:NREL], start=True, stop=True
                      ).then_inc(sem("brow_done"), 1)
            for m in range(KC):
                if m >= 4:
                    pe.wait_ge(sem("x_ready"), m - 3)
                for i in range(NT):
                    if m == 0:
                        pe.wait_ge(sem(f"x_in{i}"), 16)
                    last = pe.transpose(ps[:, 4 + m % 4, i * P:(i + 1) * P], xtok[:, i, m * P:(m + 1) * P], ident)
                last.then_inc(sem("x_turned"), 1)
            pe.wait_ge(sem("const"), 2)
            pe.wait_ge(sem("x_ready"), KC)
            pe.wait_ge(sem("brow_read"), 2)
            sums("n1")

            def turn_v(src, dst_sem):
                for i in range(NT):
                    last = pe.transpose(ps[:, TR, i * P:(i + 1) * P], src[:, i * P:(i + 1) * P], ident)
                last.then_inc(sem(dst_sem), 1)

            def ret_scores(p):
                pe.wait_ge(sem("qk_ready"), 2 * p + 2)
                for b in range(NT):
                    if b >= 2:
                        pe.wait_ge(sem("sdec_ready"), NT * p + b - 1)
                    pe.matmul(ps[:, SA + b % 2, 0:T - b * P], kf[:, b * P:(b + 1) * P], qf[:, b * P:T],
                              start=True, stop=True).then_inc(sem("ret_s"), 1)

            def ret_out(p):
                pe.wait_ge(sem("vtok_ready"), p + 1)
                for b in range(NT):
                    pe.wait_ge(sem("sdec_ready"), NT * p + b + 1)
                    last = pe.matmul(ps[:, OU, b * P:T], vtok[:, b, :], sdec[:, b, 0:T - b * P],
                                     start=(b == 0), stop=(b == NT - 1))
                last.then_inc(sem("ret_o"), 1)

            def ret_sum(p):
                pe.wait_ge(sem("osq_ready"), p + 1)
                pe.matmul(ps[:, SA, :], ones[:], nsq[:, 0, :], start=True, stop=True).then_inc(sem("ret_sum"), 1)

            def ret(j, p):
                ready = lambda k: pe.wait_ge(sem("norm_u"), before("n1") + k + 1)
                unit(st_ret, 0, j, u_hi, u_lo, ready if p is None else None)
                if p is not None:
                    ret_scores(p)
                unit(st_ret, 1, j, u_hi, u_lo)
                if p is not None:
                    ret_out(p)
                pe.wait_ge(sem("vf_ready"), j + 1)
                turn_v(vf, "vf_turned")
                unit(st_ret, 2, j, u_hi, u_lo)
                if p is not None:
                    ret_sum(p)
                unit(st_ret, 3, j, u_hi, u_lo)
                if p is not None:
                    pe.wait_ge(sem("ret_root"), p + 1)

            ret(0, None)
            with pe.Fori(1, NQ) as j:
                ret(j, j - 1)

            def conv_sum(p):
                pe.wait_ge(sem("csq_ready"), p + 1)
                pe.matmul(ps[:, SB, :], group64, nsq[:, 1, :], start=True, stop=True
                          ).then_inc(sem("conv_sum"), 1)

            unit(st_conv, 0, 0, u_hi, u_lo)
            ret_scores(NQ - 1)
            unit(st_conv, 1, 0, u_hi, u_lo)
            ret_out(NQ - 1)
            unit(st_conv, 2, 0, u_hi, u_lo)
            ret_sum(NQ - 1)
            with pe.Fori(1, NQ) as j:
                unit(st_conv, 0, j, u_hi, u_lo)
                unit(st_conv, 1, j, u_hi, u_lo)
                conv_sum(j - 1)
                unit(st_conv, 2, j, u_hi, u_lo)
            conv_sum(NQ - 1)

            def wout(st, r_hi, r_lo, ready):
                with pe.Fori(0, KC // 4) as i:
                    for s in range(4):
                        unit(st, s, i, r_hi, r_lo, ready if s == 0 else None)

            def y_ready(k):
                if k < NQ:
                    pe.wait_ge(sem("ycv_ready"), k + 1)
                else:
                    pe.wait_ge(sem("yret_ready"), k - NQ + 1)

            wout(st_out, y_hi, y_lo, y_ready)

            def mlp(st, name, norm):
                with pe.Fori(0, NF) as q:
                    with pe.Fori(0, 2) as i:
                        for s in range(4):
                            unit(st, s, q * 4 + i, u_hi, u_lo,
                                 (lambda k: pe.wait_ge(sem("norm_u"), before(norm) + k + 1)) if s == 0 else None)
                    with pe.Fori(0, 2) as i:
                        for s in range(4):
                            unit(st, s, q * 4 + 2 + i, y_hi, y_lo,
                                 (lambda k: pe.wait_ge(sem("mlp_h"), q * KC + (mlp_before(name) + k + 1))) if s == 0 else None)

            sums("n2")
            mlp(st_mlp, "mlp", "n2")
            sums("nf")

            pe.wait_ge(sem("acc_done"), 2 * NF * 4 + 1)
            for m in range(6 * KC):
                last = pe.matmul(ps[:, SB, m:m + 1], acc[:, m * P:(m + 1) * P], ones[:, 0:1], start=True, stop=True)
            last.then_inc(sem("ada_sum"), 1)
            sums("n3")

            ready = lambda k: pe.wait_ge(sem("norm_u"), before("n3") + k + 1)
            unit(st_idx, 0, 0, u_hi, u_lo, ready)
            unit(st_idx, 1, 0, u_hi, u_lo)
            unit(st_idx, 2, 0, u_hi, u_lo)
            unit(st_idx, 3, 0, u_hi, u_lo, cols=32 + IDX_HEADS)
            pe.wait_ge(sem("shifted_in"), 16)
            pe.wait_ge(sem("ada_ready"), 1)
            for h in range(HEADS):
                if h >= 2:
                    pe.wait_ge(sem("btab_ready"), h - 1)
                pe.matmul(ps[:, SA + h % 2, :], flip8, ftab[:, h, :], start=True, stop=True
                          ).then_inc(sem("btab_s"), 1)
            pe.wait_ge(sem("fw_ready"), 1)
            for i in range(NT):
                last = pe.transpose(ps[:, TR, i * 64:i * 64 + 32 + IDX_HEADS], fw[0:32 + IDX_HEADS, i * P:(i + 1) * P],
                                    ident[0:32 + IDX_HEADS, 0:32 + IDX_HEADS])
            last.then_inc(sem("wi_turned"), 1)

            def idx_scores(n):
                i, h = n // IDX_HEADS + 1, n % IDX_HEADS
                if n == 0:
                    pe.wait_ge(sem("qi_ready"), 3)
                    pe.wait_ge(sem("btab_ready"), HEADS)
                if n >= 2:
                    pe.wait_ge(sem("relu_ready"), n - 1)
                b = HD * (h % 2)
                pe.matmul(ps[:, SA + n % 2, 0:(i + 1) * P], qi[b:b + HD, h // 2, i * P:(i + 1) * P],
                          ki[b:b + HD, 0:(i + 1) * P], start=True, stop=True).then_inc(sem("idx_s"), 1)

            def s_step(p, n, dsa):
                hh, i = n // NT, n % NT
                b = HD * hh
                if n == 0:
                    pe.wait_ge(sem("att_qk"), 2 * p + 2)
                if n >= 2:
                    pe.wait_ge(sem("att_logit"), 8 * p + n - 1)
                keys = (i + 1) * P
                bank = SA + n % 2
                pe.matmul(ps[:, bank, 0:keys], qa[b:b + HD, i * P:(i + 1) * P], ka[b:b + HD, 0:keys],
                          start=True, stop=False)
                if dsa:
                    last = pe.matmul(ps[:, bank, 0:keys], identb[:], sel[:, i, 0:keys], start=False, stop=True)
                else:
                    last = pe.matmul(ps[:, bank, keys - P:keys], identb[:], causalb[:], start=False, stop=True)
                last.then_inc(sem("att_s"), 1)

            def t_step(p, n):
                i = n % NT
                pe.wait_ge(sem("att_prob"), 8 * p + n + 1)
                if n == 0:
                    pe.wait_ge(sem("vatok_ready"), p + 1)
                else:
                    pe.wait_ge(sem("att_probt"), 8 * p + n)
                for j in range(i + 1):
                    last = pe.transpose(ps[:, TR, j * P:(j + 1) * P], prob[:, n % 2, j * P:(j + 1) * P], ident)
                last.then_inc(sem("att_t"), 1)

            def pv(p, hh):
                pe.wait_ge(sem("att_probt"), 8 * p + 4 * hh + 4)
                if hh == 0:
                    pe.wait_ge(sem("vatok_ready"), p + 1)
                b = HD * hh
                for j in range(NT):
                    last = pe.matmul(ps[b:b + HD, OU, j * P:T], vatok[:, j, b:b + HD], probt[:, j, j * P:T],
                                     start=(j == 0), stop=(j == NT - 1))
                last.then_inc(sem("att_o"), 1)

            def att(st, units, p, dsa):
                def half():
                    if units:
                        units.pop(0)()
                half()
                s_step(p, 0, dsa)
                s_step(p, 1, dsa)
                half()
                for a in range(3):
                    if a == 2:
                        pv(p, 0)
                    t_step(p, 2 * a)
                    s_step(p, 2 * a + 2, dsa)
                    t_step(p, 2 * a + 1)
                    s_step(p, 2 * a + 3, dsa)
                    half()
                t_step(p, 6)
                t_step(p, 7)
                half()
                pv(p, 1)

            def halves(st, g, n=3):
                def one_half(s, h):
                    return lambda: unit(st, s, g, u_hi, u_lo, part=(h * KC // 2, (h + 1) * KC // 2),
                                        opens=(h == 0), closes=(h == 1))
                return [one_half(s, h) for s in range(n) for h in range(2)]

            def turn_va(g):
                pe.wait_ge(sem("va_ready"), g + 1)
                turn_v(va, "va_turned")

            n = 0
            for half in halves(st_att, 0):
                half()
                for _ in range(2):
                    idx_scores(n)
                    n += 1
            pe.wait_ge(sem("relu_ready"), NT * (NT - 1))
            pe.wait_ge(sem("sel8_in"), 16)
            pe.wait_ge(sem("fcum_ready"), 1)
            for h in range(HEADS):
                if h >= 2:
                    pe.wait_ge(sem("ftab_ready"), h - 1)
                pe.matmul(ps[:, SA + h % 2, :], sel8[:, h * P:(h + 1) * P], nt[0:HEADS, 0, :], start=True, stop=True
                          ).then_inc(sem("ftab_s"), 1)
            pe.wait_ge(sem("wtok_ready"), 1)
            turn_va(0)
            pe.wait_ge(sem("ftab_ready"), HEADS)
            with pe.Fori(1, NQ) as g:
                att(st_att, halves(st_att, g), g - 1, False)
                turn_va(g)
            att(st_att, halves(st_att, NQ), NQ - 1, False)
            turn_va(NQ)
            with pe.Fori(NQ + 1, 2 * NQ) as g:
                att(st_att, halves(st_att, g), g - 1, True)
                turn_va(g)

            def branch(m):
                pe.wait_ge(lo_ready[2], st_bra.turn(2, m) + 1)
                wait(pe, bank_free[2], st_bra.turn(2, m))
                for b, k0 in ((2, 0), (SA, NQ)):
                    for k in range(k0, k0 + NQ):
                        pe.wait_ge(sem("att_y"), k + 1)
                        c = slice(k * P, (k + 1) * P)
                        for w, r in ((w_hi, y_hi), (w_hi, y_lo), (w_lo, y_hi)):
                            last = pe.matmul(ps[:, b, :], w[:, 2, c], r[:, k, :],
                                             start=(k == k0 and w is w_hi and r is y_hi),
                                             stop=(k == k0 + NQ - 1 and w is w_lo))
                last.then_inc(used[2], 1)

            att(st_bra, halves(st_bra, 0, 2), 2 * NQ - 1, True)
            branch(0)
            with pe.Fori(1, KC) as m:
                unit(st_bra, 0, m, u_hi, u_lo)
                unit(st_bra, 1, m, u_hi, u_lo)
                branch(m)

            wout(st_out2, m_hi, m_lo, lambda k: pe.wait_ge(sem("m_ready"), k + 1))
            sums("n4")
            mlp(st_mlp2, "mlp2", "n4")
            sums("n5")
            for i in range(NT):
                for c in range(2):
                    n = 2 * i + c
                    if n >= 4:
                        pe.wait_ge(sem(f"otok{c}"), i - 1)
                    if n == 0:
                        pe.wait_ge(sem("norm_u"), before("n5") + KC)
                    for m in range(4):
                        last = pe.transpose(ps[:, 4 + n % 4, m * P:(m + 1) * P],
                                            xres[:, 4 * c + m, i * P:(i + 1) * P], ident)
                    last.then_inc(sem("o_turned"), 1)

        @block.scalar
        def _(act):
            def ahead(st, s, i):
                t = s + AHEAD
                if t >= st.k:
                    t, i = t - st.k, i + 1
                act.wait_ge(raw_ready[t], st.landed(t, i))
                wait(act, used[t], st.turn(t, i))
                act.activation(w_hi[:, t, :], raw[:, t, :], ACT.Copy).then_inc(hi_ready[t], 1)

            def norm(name, x_sem, x0, shift=None, split=True):
                for m in range(KC):
                    act.wait_ge(sem(x_sem), x0 + m + 1)
                    if m >= 2:
                        act.wait_ge(sem("norm_sum"), before(name) + m - 1)
                    act.activation(nsq[:, m % 2, :], xres[:, m, :], ACT.Square).then_inc(sem("norm_sq"), 1)
                act.wait_ge(sem("norm_sum"), before(name) + KC)
                act.activation(nrs[:], ps[:, SA, :], ACT.Sqrt, bias=epsc[:, 0:1], scale=1.0 / D
                               ).then_inc(sem("norm_root"), 1)
                if split:
                    for m in range(KC):
                        act.wait_ge(sem("norm_t"), split_before(name) + m + 1)
                        if shift is None:
                            act.activation(u_hi[:, m, :], nt[:, m % 3, :], ACT.Copy).then_inc(sem("norm_hi"), 1)
                        else:
                            act.activation(u_hi[:, m, :], nt[:, m % 3, :], ACT.Identity,
                                           bias=ada[:, shift + m:shift + m + 1]).then_inc(sem("norm_hi"), 1)

            for s in range(SLOTS):
                act.sem_inc(hi_ready[s], 1)
            for name, n in VECS:
                src = rows[name]
                if name == "conv_w":
                    src = src.rearrange("t (j p) -> (t j) p", p=P)
                elif name == "c_2":
                    src = src.rearrange("a (j p) -> (a j) p", p=P)
                else:
                    src = src.rearrange("(j p) -> j p", p=P)
                act.dma_start(vrow[VAT[name]:VAT[name] + n, :], src).then_inc(sem("vrow_in"), 16)
            act.dma_start(oneh[:], tab[0:BUCKETS, TAT["onehot"]:TAT["onehot"] + NREL]).then_inc(sem("bias_in"), 16)
            act.dma_start(rbias[:], rel_bias_2).then_inc(sem("bias_in"), 16)
            act.dma_start(bfor[:], b_forget_2.rearrange("(h a) -> h a", a=1)).then_inc(sem("bfor_in"), 16)
            act.dma_start(rope[:], tab[:, TAT["cos"]:TAT["cos"] + 2 * T].rearrange("p (a t) -> p a t", a=2)
                          ).then_inc(sem("rope_in"), 16)

            for s in range(AHEAD):
                act.wait_ge(raw_ready[s], st_ret.landed(s, 0))
                act.activation(w_hi[:, s, :], raw[:, s, :], ACT.Copy).then_inc(hi_ready[s], 1)
            act.wait_ge(sem("brow_done"), 1)
            act.activation(fbrow[:, 0:T], ps[0:HEADS, 1, :], ACT.Copy).then_inc(sem("brow_read"), 1)
            act.activation(fbrow[:, T:NREL], ps[0:HEADS, 2, 0:P], ACT.Copy).then_inc(sem("brow_read"), 1)
            act.wait_ge(sem("brow_read"), 2)
            act.dma_start(bias_rows, fbrow[:]).then_inc(sem("brow_out"), 16)
            act.wait_ge(sem("const"), 2)
            act.wait_ge(sem("vec_turned"), 1)
            act.wait_ge(sem("brow_out"), 16)
            act.dma_start(decay[:], tab[:, TAT["decay"]:TAT["decay"] + NQ * T].rearrange("p (a t) -> p a t", a=NQ)
                          ).then_inc(sem("decay_in"), 16)
            norm("n1", "x_ready", 0)

            def ret_act(j, p):
                ahead(st_ret, 0, j)
                act.wait_ge(used[0], st_ret.turn(0, j) + 1)
                wait(act, sem("vf_turned"), j)
                act.activation(vf[:], ps[:, 0, :], ACT.Copy).then_inc(bank_free[0], 1)
                act.wait_ge(bank_free[0], st_ret.turn(0, j) + 1)
                act.sem_inc(sem("vf_ready"), 1)
            def osq(p):
                act.wait_ge(sem("ret_o"), p + 1)
                act.activation(osb[:], ps[:, OU, :], ACT.Copy).then_inc(sem("osb_ready"), 1)
                act.activation(nsq[:, 0, :], ps[:, OU, :], ACT.Square).then_inc(sem("osq_ready"), 1)
            def ret_root(p):
                act.wait_ge(sem("ret_sum"), p + 1)
                act.activation(nrs[:], ps[:, SA, :], ACT.Sqrt, bias=epsc[:, 0:1], scale=1.0 / P
                               ).then_inc(sem("ret_root"), 1)
            def ret_hi(p):
                act.wait_ge(sem("ret_y"), p + 1)
                act.activation(y_hi[:, ds(NQ + p, 1), :], nt[:, 1:2, :], ACT.Copy).then_inc(sem("ret_hi"), 1)
            def ret(j, p):
                ret_act(j, p)
                ahead(st_ret, 1, j)
                if p is not None:
                    osq(p)
                act.wait_ge(sem("vf_turned"), j + 1)
                act.activation(vtok[:].rearrange("p a b -> p (a b)"), ps[:, TR, :], ACT.Copy
                               ).then_inc(sem("vtok_ready"), 1)
                ahead(st_ret, 2, j)
                if p is not None:
                    ret_root(p)
                ahead(st_ret, 3, j)
                act.wait_ge(used[3], st_ret.turn(3, j) + 1)
                wait(act, sem("silu_ready"), j)
                act.activation(sg[:], ps[:, 3, :], ACT.Sigmoid).then_inc(sem("sg_ready"), 1)
                if p is not None:
                    ret_hi(p)

            ret(0, None)
            with act.Fori(1, NQ) as j:
                ret(j, j - 1)

            def cc(j):
                act.wait_ge(used[0], st_conv.turn(0, j) + 1)
                wait(act, sem("prod_ready"), j)
                act.activation(ccs[:], ps[:, 0, :], ACT.Copy).then_inc(bank_free[0], 1)
            def csq(j):
                act.wait_ge(sem("ycv_done"), j + 1)
                wait(act, sem("conv_sum"), j)
                act.activation(nsq[:, 1, :], ycv[:], ACT.Square).then_inc(sem("csq_ready"), 1)
            def conv_root(p):
                act.wait_ge(sem("conv_sum"), p + 1)
                act.activation(sg[:], ps[:, SB, :], ACT.Sqrt, bias=epsc[:, 0:1], scale=1.0 / HD
                               ).then_inc(sem("conv_root"), 1)
            def conv_hi(p):
                act.wait_ge(sem("conv_t"), p + 1)
                act.activation(y_hi[:, ds(p, 1), :], nt[:, 0:1, :], ACT.Copy).then_inc(sem("conv_hi"), 1)

            ahead(st_conv, 0, 0)
            cc(0)
            ahead(st_conv, 1, 0)
            osq(NQ - 1)
            ahead(st_conv, 2, 0)
            ret_root(NQ - 1)
            ret_hi(NQ - 1)
            csq(0)
            with act.Fori(1, NQ) as j:
                ahead(st_conv, 0, j)
                cc(j)
                ahead(st_conv, 1, j)
                conv_root(j - 1)
                conv_hi(j - 1)
                ahead(st_conv, 2, j)
                csq(j)
            conv_root(NQ - 1)
            conv_hi(NQ - 1)

            with act.Fori(0, KC // 4) as i:
                for s in range(4):
                    ahead(st_out, s, i)
            norm("n2", "x_mixed", 0)

            def mlp(st, name, final):
                def up(q, i):
                    for s in range(4):
                        ahead(st, s, q * 4 + i)
                        act.wait_ge(used[s], st.turn(s, q * 4 + i) + 1)
                        if s >= 2:
                            act.wait_ge(sem("mlp_sq"), q * KC + i * 4 + (mlp_before(name) + s - 1))
                        act.activation(nsq[:, s % 2, :], ps[:, s, :], ACT.Relu).then_inc(bank_free[s], 1)
                        act.wait_ge(bank_free[s], st.turn(s, q * 4 + i) + 1)
                        act.activation(y_hi[:, ds(i * 4 + s, 1), :], nsq[:, s % 2:s % 2 + 1, :], ACT.Square
                                       ).then_inc(sem("mlp_hi"), 1)
                    act.wait_ge(sem("mlp_sq"), q * KC + i * 4 + (mlp_before(name) + 4))

                def down(q, i, last=False):
                    for s in range(4):
                        if not (last and s + AHEAD >= 4):
                            ahead(st, s, q * 4 + 2 + i)

                with act.Fori(0, NF - final) as q:
                    with act.Fori(0, 2) as i:
                        up(q, i)
                    with act.Fori(0, 2) as i:
                        down(q, i)
                if final:
                    with act.Fori(0, 2) as i:
                        up(NF - 1, i)
                    down(NF - 1, 0)
                    down(NF - 1, 1, True)

            mlp(st_mlp, "mlp", 0)
            norm("nf", "mlp_x", mlp_before("mlp") + (NF - 1) * KC, split=False)
            norm("n3", "norm_u", before("nf"), shift=0)

            ahead(st_idx, 0, 0)
            for s in range(2):
                act.wait_ge(used[s], st_idx.turn(s, 0) + 1)
                act.activation(qi[:, s, :], ps[:, s, :], ACT.Copy).then_inc(bank_free[s], 1)
                ahead(st_idx, s + 1, 0)
            act.wait_ge(used[2], st_idx.turn(2, 0) + 1)
            act.activation(ki[:], ps[:, 2, :], ACT.Copy).then_inc(bank_free[2], 1)
            for s in range(3):
                act.wait_ge(bank_free[s], st_idx.turn(s, 0) + 1)
                act.sem_inc(sem("qi_ready"), 1)
            ahead(st_idx, 3, 0)
            act.wait_ge(used[3], st_idx.turn(3, 0) + 1)
            act.activation(fw[0:36, :], ps[0:36, 3, :], ACT.Copy).then_inc(sem("fw_ready"), 1)
            act.wait_ge(sem("fw_ready"), 1)
            act.sem_inc(bank_free[3], 1)
            act.wait_ge(sem("fgate_abs"), 1)
            act.activation(nt[0:HEADS, 1, :], nt[0:HEADS, 1, :], ACT.Exp, scale=-1.0).then_inc(sem("fgate_exp"), 1)
            act.wait_ge(sem("fgate_exp"), 1)
            act.activation(nt[0:HEADS, 1, :], nt[0:HEADS, 1, :], ACT.Ln, bias=ones[0:HEADS, 0:1]
                           ).then_inc(sem("fgate_ln"), 1)

            def relu(n):
                i = n // IDX_HEADS + 1
                act.wait_ge(sem("idx_s"), n + 1)
                if n >= 2:
                    act.wait_ge(sem("idx_acc"), n - 1)
                act.activation(nsq[:, n % 2, 0:(i + 1) * P], ps[:, SA + n % 2, 0:(i + 1) * P], ACT.Relu,
                               scale=HD ** -0.5).then_inc(sem("relu_ready"), 1)

            def va_evac(g):
                act.wait_ge(used[0], st_att.turn(0, g) + 1)
                wait(act, sem("va_turned"), g)
                act.activation(va[:], ps[:, 0, :], ACT.Copy).then_inc(sem("va_ready"), 1)
                act.wait_ge(sem("va_ready"), g + 1)
                act.sem_inc(bank_free[0], 1)
            def qk_evac(s, g):
                act.wait_ge(used[s], st_att.turn(s, g) + 1)
                wait(act, sem("att_s"), 8 * g)
                act.activation((qa, ka)[s - 1][:], ps[:, s, :], ACT.Copy).then_inc(sem("att_qk"), 1)
                act.wait_ge(sem("att_qk"), 2 * g + s)
                act.sem_inc(bank_free[s], 1)
            def vatok_evac(g):
                act.wait_ge(sem("va_turned"), g + 1)
                act.activation(vatok[:].rearrange("p a b -> p (a b)"), ps[:, TR, :], ACT.Copy
                               ).then_inc(sem("vatok_ready"), 1)
            def exps(p, a):
                for n in (2 * a, 2 * a + 1):
                    keys = (n % NT + 1) * P
                    act.wait_ge(sem("att_logit"), 8 * p + n + 1)
                    act.activation(prob[:, n % 2, 0:keys], prob[:, n % 2, 0:keys], ACT.Exp, bias=mneg[:, n:n + 1],
                                   scale=-1.0, accum_out=rowsum[:, n:n + 1]).then_inc(sem("att_exp"), 1)
            def y_evac(p):
                act.wait_ge(sem("att_o"), 2 * p + 2)
                act.activation(y_hi[:, ds(p, 1), :], ps[:, OU:OU + 1, :], ACT.Copy).then_inc(sem("att_hi"), 1)

            n = 0
            for s in range(3):
                ahead(st_att, s, 0)
                for _ in range(4):
                    relu(n)
                    n += 1
                if s == 0:
                    va_evac(0)
                else:
                    qk_evac(s, 0)
            for h in range(HEADS):
                act.wait_ge(sem("ftab_s"), h + 1)
                if h == 0:
                    act.wait_ge(sem("btab_s"), HEADS)
                act.activation(ftab[:, h, :], ps[:, SA + h % 2, :], ACT.Copy).then_inc(sem("ftab_ready"), 1)
            vatok_evac(0)

            def att_group(g):
                p = g - 1
                ahead(st_att, 0, g)
                exps(p, 0)
                va_evac(g)
                exps(p, 1)
                ahead(st_att, 1, g)
                exps(p, 2)
                exps(p, 3)
                ahead(st_att, 2, g)
                qk_evac(1, g)
                y_evac_late = p
                qk_evac(2, g)
                y_evac(y_evac_late)
                vatok_evac(g)

            with act.Fori(1, NQ) as g:
                att_group(g)
            att_group(NQ)
            with act.Fori(NQ + 1, 2 * NQ) as g:
                att_group(g)

            def gate(s, m):
                act.wait_ge(used[s], st_bra.turn(s, m) + 1)
                wait(act, sem("merged"), m)
                act.activation(nsq[:, s, :], ps[:, s, :], ACT.Sigmoid).then_inc(sem("gate_ready"), 1)
                act.wait_ge(sem("gate_ready"), 2 * m + s + 1)
                act.sem_inc(bank_free[s], 1)
            def m_round(m):
                act.wait_ge(sem("merged"), m + 1)
                act.activation(m_hi[:, ds(m, 1), :], nt[:, 2:3, :], ACT.Copy).then_inc(sem("m_hi"), 1)

            p = 2 * NQ - 1
            exps(p, 0)
            ahead(st_bra, 0, 0)
            exps(p, 1)
            exps(p, 2)
            ahead(st_bra, 1, 0)
            exps(p, 3)
            y_evac(p)
            gate(0, 0)
            gate(1, 0)
            ahead(st_bra, 2, 0)
            m_round(0)
            with act.Fori(1, KC) as m:
                ahead(st_bra, 0, m)
                gate(0, m)
                ahead(st_bra, 1, m)
                gate(1, m)
                ahead(st_bra, 2, m)
                m_round(m)
            with act.Fori(0, KC // 4) as i:
                for s in range(4):
                    ahead(st_out2, s, i)
            norm("n4", "x_mixed2", 0, shift=3 * KC)
            mlp(st_mlp2, "mlp2", 1)
            norm("n5", "mlp_x", mlp_before("mlp2") + (NF - 1) * KC, split=False)
            for n in range(1, 2 * NT, 2):
                i = n // 2
                act.wait_ge(sem("o_turned"), n + 1)
                if i >= 2:
                    act.wait_ge(sem(f"out{i % 2}"), 16)
                act.activation(otok[:, i % 2, T:D], ps[:, 4 + n % 4, :], ACT.Copy).then_inc(sem("otok1"), 1)

        @block.vector
        def _(dve):
            def norm(name, gain, dst=True, shift=None):
                dve.wait_ge(sem("norm_root"), NORMS.index(name) + 1)
                dve.reciprocal(nrs[:], nrs[:]).then_inc(sem("norm_rinv"), 1)
                dve.wait_ge(sem("norm_rinv"), NORMS.index(name) + 1)

                def lo(m):
                    dve.wait_ge(sem("norm_hi"), split_before(name) + m + 1)
                    if shift is None:
                        dve.tensor_tensor(u_lo[:, m, :], nt[:, m % 3, :], u_hi[:, m, :], ALU.subtract
                                          ).then_inc(sem("norm_u"), 1)
                    else:
                        dve.scalar_tensor_tensor(u_lo[:, m, :], nt[:, m % 3, :], ada[:, shift + m:shift + m + 1],
                                                 u_hi[:, m, :], ALU.add, ALU.subtract).then_inc(sem("norm_u"), 1)

                for m in range(KC):
                    if not dst:
                        dve.scalar_tensor_tensor(xres[:, m, :], xres[:, m, :], gain(m), nrs[:], ALU.mult, ALU.mult
                                                 ).then_inc(sem("norm_u"), 1)
                        continue
                    if m >= 3:
                        dve.wait_ge(sem("norm_u"), before(name) + m - 2)
                    dve.scalar_tensor_tensor(nt[:, m % 3, :], xres[:, m, :], gain(m), nrs[:], ALU.mult, ALU.mult
                                             ).then_inc(sem("norm_t"), 1)
                    if m >= 1:
                        lo(m - 1)
                if dst:
                    lo(KC - 1)

            def col(name):
                return lambda m: vec[:, VAT[name] + m:VAT[name] + m + 1]

            for s in range(SLOTS):
                dve.sem_inc(bank_free[s], 1)
            for b in range(2):
                dve.sem_inc(sem(f"ada_used{b}"), 1)
            dve.sem_inc(sem("acc_done"), 1)
            dve.wait_ge(sem("small_in"), 16)
            dve.tensor_copy(identb[:], ident).then_inc(sem("masks"), 1)
            dve.tensor_copy(causalb[:], small[:, TAT["causal"]:TAT["causal"] + P]).then_inc(sem("masks"), 1)
            dve.wait_ge(sem("vec_turned"), 1)
            dve.tensor_copy(vec[:], ps[:, 3, 0:NVEC]).then_inc(sem("vec_ready"), 1)
            dve.memset(prod[:, 0:2], 0.0).then_inc(sem("prod_zero"), 1)
            for m in range(KC):
                dve.wait_ge(sem("x_turned"), m + 1)
                dve.tensor_copy(xres[:, m, :], ps[:, 4 + m % 4, :]).then_inc(sem("x_ready"), 1)
            dve.wait_ge(sem("x_ready"), KC)
            dve.wait_ge(sem("brow_out"), 16)
            dve.memset(acc[:], 0.0).then_inc(sem("acc_zero"), 1)
            dve.wait_ge(sem("vec_ready"), 1)
            norm("n1", col("norm1_g"))
            dve.wait_ge(sem("rope_in"), 16)
            dve.wait_ge(sem("decay_in"), 16)

            def rotate(s, j, dst):
                dve.wait_ge(used[s], st_ret.turn(s, j) + 1)
                h = P // 2
                dve.wait_ge(sem("rotated"), 2 * j + s - 1) if not (isinstance(j, int) and 2 * j + s - 1 <= 0) else None
                dve.tensor_tensor(nt[0:h, 2, :], ps[h:P, s, :], sinr[h:P, :], ALU.mult).then_inc(sem("swapped"), 1)
                dve.tensor_tensor(nt[h:P, 2, :], ps[0:h, s, :], sinr[0:h, :], ALU.mult).then_inc(sem("swapped"), 1)
                dve.tensor_tensor(dst[:], ps[:, s, :], cosr, ALU.mult).then_inc(bank_free[s], 1)
                dve.wait_ge(sem("swapped"), 4 * j + 2 * s)
                dve.wait_ge(bank_free[s], st_ret.turn(s, j) + 1)
                dve.tensor_tensor(dst[:], dst[:], nt[:, 2, :], ALU.add).then_inc(sem("rotated"), 1)
                dve.wait_ge(sem("rotated"), 2 * j + s)
                dve.sem_inc(sem("qk_ready"), 1)

            def ret_decay(p):
                for b in range(NT):
                    dve.wait_ge(sem("ret_s"), NT * p + b + 1)
                    n = T - b * P
                    dve.tensor_tensor(sdec[:, b:b + 1, 0:n], ps[:, SA + b % 2:SA + b % 2 + 1, 0:n],
                                      decay[:, ds(p, 1), 0:n], ALU.mult).then_inc(sem("sdec_ready"), 1)

            def ret_norm(p):
                dve.wait_ge(sem("ret_root"), p + 1)
                dve.reciprocal(nrs[:], nrs[:]).then_inc(sem("ret_rinv"), 1)
                dve.wait_ge(sem("ret_rinv"), p + 1)
                dve.wait_ge(sem("osb_ready"), p + 1)
                dve.scalar_tensor_tensor(nt[:, 0, :], osb[:], vec[:, ds(VAT["ret_norm_g"] + p, 1)], nrs[:],
                                         ALU.mult, ALU.mult).then_inc(sem("ret_t"), 1)
                dve.wait_ge(sem("ret_t"), p + 1)
                dve.wait_ge(sem("silu_ready"), p + 1)
                dve.tensor_tensor(nt[:, 1, :], nt[:, 0, :], silu[:], ALU.mult).then_inc(sem("ret_y"), 1)

            def ret_lo(p):
                dve.wait_ge(sem("ret_hi"), p + 1)
                dve.tensor_tensor(y_lo[:, ds(NQ + p, 1), :], nt[:, 1:2, :], y_hi[:, ds(NQ + p, 1), :], ALU.subtract
                                  ).then_inc(sem("yret_ready"), 1)

            def silus(j):
                dve.wait_ge(sem("sg_ready"), j + 1)
                wait(dve, sem("ret_y"), j)
                dve.tensor_tensor(silu[:], ps[:, 3, :], sg[:], ALU.mult).then_inc(sem("silu_ready"), 1)
                dve.wait_ge(sem("silu_ready"), j + 1)
                dve.sem_inc(bank_free[3], 1)

            rotate(1, 0, qf)
            rotate(2, 0, kf)
            silus(0)
            with dve.Fori(1, NQ) as j:
                ret_decay(j - 1)
                rotate(1, j, qf)
                rotate(2, j, kf)
                ret_norm(j - 1)
                silus(j)
                ret_lo(j - 1)

            def conv(j):
                dve.wait_ge(used[1], st_conv.turn(1, j) + 1)
                dve.wait_ge(bank_free[0], st_conv.turn(0, j) + 1)
                wait(dve, sem("conv_y3"), j)
                dve.tensor_tensor(prod[:, 2:T + 2], ps[:, 1, :], ccs[:], ALU.mult).then_inc(sem("prod_ready"), 1)
                dve.wait_ge(sem("prod_ready"), j + 1)
                dve.sem_inc(bank_free[1], 1)
                taps = [vec[:, ds(VAT["conv_w"] + t * NQ + j, 1)] for t in range(3)]
                wait(dve, sem("conv_t"), j)
                dve.tensor_scalar(ycv[:], prod[:, 2:T + 2], taps[2], None, ALU.mult).then_inc(sem("conv_y1"), 1)
                dve.wait_ge(sem("conv_y1"), j + 1)
                dve.scalar_tensor_tensor(ycv[:], prod[:, 1:T + 1], taps[1], ycv[:], ALU.mult, ALU.add
                                         ).then_inc(sem("conv_y2"), 1)
                dve.wait_ge(sem("conv_y2"), j + 1)
                dve.scalar_tensor_tensor(ycv[:], prod[:, 0:T], taps[0], ycv[:], ALU.mult, ALU.add
                                         ).then_inc(sem("conv_y3"), 1)
                dve.wait_ge(sem("conv_y3"), j + 1)
                dve.wait_ge(used[2], st_conv.turn(2, j) + 1)
                dve.tensor_tensor(ycv[:], ps[:, 2, :], ycv[:], ALU.mult).then_inc(sem("ycv_done"), 1)
                dve.wait_ge(sem("ycv_done"), j + 1)
                dve.sem_inc(bank_free[2], 1)

            def conv_norm(p):
                dve.wait_ge(sem("conv_root"), p + 1)
                dve.reciprocal(sg[:], sg[:]).then_inc(sem("conv_rinv"), 1)
                dve.wait_ge(sem("conv_rinv"), p + 1)
                dve.scalar_tensor_tensor(nt[:, 0, :], ycv[:], vec[:, ds(VAT["conv_norm_g"] + p, 1)], sg[:],
                                         ALU.mult, ALU.mult).then_inc(sem("conv_t"), 1)
                dve.wait_ge(sem("conv_hi"), p + 1)
                dve.tensor_tensor(y_lo[:, ds(p, 1), :], nt[:, 0:1, :], y_hi[:, ds(p, 1), :], ALU.subtract
                                  ).then_inc(sem("ycv_ready"), 1)

            ret_decay(NQ - 1)
            ret_norm(NQ - 1)
            ret_lo(NQ - 1)
            dve.wait_ge(sem("prod_zero"), 1)
            conv(0)
            with dve.Fori(1, NQ) as j:
                conv_norm(j - 1)
                conv(j)
            conv_norm(NQ - 1)
            dve.wait_ge(sem("ycv_ready"), NQ)
            dve.sem_inc(sem("mix_done"), 1)

            def add(st, n, s, i, m, scale, done):
                dve.wait_ge(used[s], st.turn(s, n) + 1)
                dve.wait_ge(bank_free[s], st.turn(s, n))
                dve.scalar_tensor_tensor(xres[:, ds(m, 1), :], ps[:, s:s + 1, :], scale, xres[:, ds(m, 1), :],
                                         ALU.mult, ALU.add).then_inc(sem(done), 1)
                dve.wait_ge(sem(done), i + 1)
                dve.sem_inc(bank_free[s], 1)

            def wout(st, scale, done):
                with dve.Fori(0, KC // 4) as i:
                    for s in range(4):
                        add(st, i, s, i * 4 + s, i * 4 + s, scale(i * 4 + s), done)

            wout(st_out, lambda m: 1.0, "x_mixed")
            norm("n2", col("norm2_g"))

            def ada_piece(q, d, i, b):
                n = q * 4 + 2 * d + i
                dve.wait_ge(sem(f"ada_in{b}"), 16 * (n + 1))
                dve.wait_ge(sem("acc_done"), 2 * n + b + 1)
                a = acc[:, ds(i * 3 * D + b * 3 * D // 2, 3 * D // 2)]
                dve.scalar_tensor_tensor(a, adaw[:, b, :], vec[:, ds(VAT["c_2"] + 2 * q + d, 1)], a,
                                         ALU.mult, ALU.add).then_inc(sem("acc_done"), 1)
                dve.wait_ge(sem("acc_done"), 2 * n + b + 2)
                dve.sem_inc(sem(f"ada_used{b}"), 1)

            def mlp(st, name, scale, with_ada):
                with dve.Fori(0, NF) as q:
                    with dve.Fori(0, 2) as i:
                        for s in range(4):
                            dve.wait_ge(bank_free[s], st.turn(s, q * 4 + i) + 1)
                            dve.tensor_tensor(nt[:, s % 2, :], nsq[:, s % 2, :], nsq[:, s % 2, :], ALU.mult
                                              ).then_inc(sem("mlp_sq"), 1)
                            dve.wait_ge(sem("mlp_sq"), q * KC + i * 4 + (mlp_before(name) + s + 1))
                            dve.wait_ge(sem("mlp_hi"), q * KC + i * 4 + (mlp_before(name) + s + 1))
                            m = ds(i * 4 + s, 1)
                            dve.tensor_tensor(y_lo[:, m, :], nt[:, s % 2:s % 2 + 1, :], y_hi[:, m, :], ALU.subtract
                                              ).then_inc(sem("mlp_h"), 1)
                            dve.wait_ge(sem("mlp_h"), q * KC + i * 4 + (mlp_before(name) + s + 1))
                            if with_ada and s % 2:
                                ada_piece(q, 0, i, s // 2)
                    with dve.Fori(0, 2) as i:
                        for s in range(4):
                            add(st, q * 4 + 2 + i, s, q * KC + i * 4 + (mlp_before(name) + s), i * 4 + s,
                                scale(i * 4 + s), "mlp_x")
                            if with_ada and s % 2:
                                ada_piece(q, 1, i, s // 2)

            dve.wait_ge(sem("acc_zero"), 1)
            mlp(st_mlp, "mlp", lambda m: 1.0, True)
            norm("nf", col("final_norm_g"), dst=False)
            dve.wait_ge(sem("ada_sum"), 1)
            dve.tensor_tensor(ada[:], ps[:, SB, 0:6 * KC], vec[:, VAT["b_ada_2"]:VAT["b_ada_2"] + 6 * KC], ALU.add
                              ).then_inc(sem("ada_ready"), 1)
            dve.wait_ge(sem("ada_ready"), 1)
            dve.scalar_tensor_tensor(gain1[:], ada[:, KC:2 * KC], 1.0, vec[:, VAT["g_norm1_2"]:VAT["g_norm1_2"] + KC],
                                     ALU.add, ALU.mult).then_inc(sem("gains"), 1)
            dve.scalar_tensor_tensor(gain2[:], ada[:, 4 * KC:5 * KC], 1.0,
                                     vec[:, VAT["g_norm2_2"]:VAT["g_norm2_2"] + KC], ALU.add, ALU.mult
                                     ).then_inc(sem("gains"), 1)
            dve.wait_ge(sem("gains"), 2)
            dve.wait_ge(sem("norm_u"), before("nf") + KC)
            norm("n3", lambda m: gain1[:, m:m + 1], shift=0)

            dve.wait_ge(sem("bfor_in"), 16)
            dve.wait_ge(sem("masks"), 2)
            dve.tensor_copy(sel[:, 0, 0:P], causalb[:]).then_inc(sem("sel_ready"), 1)
            for h in range(HEADS):
                dve.wait_ge(sem("btab_s"), h + 1)
                dve.tensor_copy(btab[:, h, :], ps[:, SA + h % 2, :]).then_inc(sem("btab_ready"), 1)
            dve.wait_ge(sem("fw_ready"), 1)
            dve.wait_ge(sem("norm_u"), before("n3") + KC)
            f = fw[0:HEADS, :]
            dve.tensor_scalar(nt[0:HEADS, 1, :], f, bfor[:, 0:1], None, ALU.add).then_inc(sem("fgate_z"), 1)
            dve.tensor_scalar(nt[0:HEADS, 2, :], f, bfor[:, 0:1], 0.0, ALU.add, ALU.min).then_inc(sem("fgate_z"), 1)
            dve.wait_ge(sem("fgate_z"), 2)
            dve.scalar_tensor_tensor(nt[0:HEADS, 1, :], nt[0:HEADS, 2, :], -2.0, nt[0:HEADS, 1, :],
                                     ALU.mult, ALU.add).then_inc(sem("fgate_abs"), 1)
            dve.memset(nrs[0:HEADS, :], 1.0).then_inc(sem("fgate_one"), 1)
            dve.wait_ge(sem("wi_turned"), 1)
            for i in range(NT):
                last = dve.tensor_scalar(wtok[:, IDX_HEADS * i:IDX_HEADS * (i + 1)],
                                         ps[:, TR, i * 64 + 32:i * 64 + 32 + IDX_HEADS], IDX_HEADS ** -0.5, None, ALU.mult)
            last.then_inc(sem("wtok_ready"), 1)
            dve.wait_ge(sem("fgate_ln"), 1)
            dve.tensor_tensor(nt[0:HEADS, 2, :], nt[0:HEADS, 2, :], nt[0:HEADS, 1, :], ALU.subtract
                              ).then_inc(sem("fgate_log"), 1)
            dve.wait_ge(sem("fgate_log"), 1)
            dve.wait_ge(sem("fgate_one"), 1)
            dve.tensor_tensor_scan(nt[0:HEADS, 0, :], nrs[0:HEADS, :], nt[0:HEADS, 2, :], 0.0, ALU.mult, ALU.add
                                   ).then_inc(sem("fcum_ready"), 1)
            dve.wait_ge(sem("wtok_ready"), 1)
            for n in range(IDX_HEADS * (NT - 1)):
                i, h = n // IDX_HEADS + 1, n % IDX_HEADS
                keys = (i + 1) * P
                w = wtok[:, IDX_HEADS * i + h:IDX_HEADS * i + h + 1]
                dve.wait_ge(sem("relu_ready"), n + 1)
                wk = work[:, i - 1, 0:keys]
                if h == 0:
                    dve.tensor_scalar(wk, nsq[:, n % 2, 0:keys], w, 0.0, ALU.mult, ALU.add).then_inc(sem("idx_acc"), 1)
                else:
                    dve.wait_ge(sem("idx_acc"), n)
                    dve.scalar_tensor_tensor(wk, nsq[:, n % 2, 0:keys], w, wk, ALU.mult, ALU.add
                                             ).then_inc(sem("idx_acc"), 1)
                if h == IDX_HEADS - 1:
                    dve.wait_ge(sem("idx_acc"), n + 1)
                    d = work[:, i - 1, keys - P:keys]
                    dve.tensor_tensor(d, d, causalb[:], ALU.add).then_inc(sem("iscore"), 1)

            def logits(p, n, tab_at):
                keys = (n % NT + 1) * P
                dve.wait_ge(sem("att_s"), 8 * p + n + 1)
                if n >= 2:
                    dve.wait_ge(sem("att_t"), 8 * p + n - 1)
                else:
                    wait(dve, sem("att_t"), 8 * p)
                dve.tensor_tensor_reduce(prob[:, n % 2, 0:keys], ps[:, SA + n % 2, 0:keys],
                                         tab_at(p, n // NT, keys), -(HD ** -0.5), -MASKED, ALU.add, ALU.min,
                                         mneg[:, n:n + 1]).then_inc(sem("att_logit"), 1)
            def weights(p, n):
                keys = (n % NT + 1) * P
                dve.wait_ge(sem("att_exp"), 8 * p + n + 1)
                dve.reciprocal(rinv[:, n:n + 1], rowsum[:, n:n + 1]).then_inc(sem("att_rinv"), 1)
                dve.wait_ge(sem("att_rinv"), 8 * p + n + 1)
                dve.tensor_scalar(prob[:, n % 2, 0:keys], prob[:, n % 2, 0:keys], rinv[:, n:n + 1], None, ALU.mult
                                  ).then_inc(sem("att_prob"), 1)
            def turned(p, n):
                i = n % NT
                dve.wait_ge(sem("att_t"), 8 * p + n + 1)
                if n == 0:
                    wait(dve, sem("att_o"), 2 * p)
                if n == 4:
                    dve.wait_ge(sem("att_o"), 2 * p + 1)
                dve.tensor_copy(probt[:, 0:i + 1, i * P:(i + 1) * P],
                                ps[:, TR, 0:(i + 1) * P].rearrange("p (a b) -> p a b", b=P)
                                ).then_inc(sem("att_probt"), 1)
            def y_lows(p):
                dve.wait_ge(sem("att_hi"), p + 1)
                dve.tensor_tensor(y_lo[:, ds(p, 1), :], ps[:, OU:OU + 1, :], y_hi[:, ds(p, 1), :], ALU.subtract
                                  ).then_inc(sem("att_y"), 1)
            def fox_tab(p, hh, keys):
                return ftab[:, 2 * p + hh, 0:keys]
            def dsa_tab(p, hh, keys):
                return btab[:, 2 * (p - NQ) + hh, T - keys:T]

            def rounds(i, n0, n1):
                for n in range(n0, n1):
                    wk = work[:, i - 1, 0:(i + 1) * P]
                    dve.max(top8[:], wk).then_inc(sem("top8"), 1)
                    dve.wait_ge(sem("top8"), (TOPK // 8) * (i - 1) + n + 1)
                    dve.match_replace(wk, top8[:], wk, TAKEN).then_inc(sem("taken"), 1)
                    dve.wait_ge(sem("taken"), (TOPK // 8) * (i - 1) + n + 1)

            def att(p, tab_at, select=None):
                for a in range(4):
                    if a > 0:
                        turned(p, 2 * a - 2)
                    logits(p, 2 * a, tab_at)
                    if a > 0:
                        turned(p, 2 * a - 1)
                    logits(p, 2 * a + 1, tab_at)
                    weights(p, 2 * a)
                    weights(p, 2 * a + 1)
                    if select is not None:
                        rounds(select, 3 * a, 3 * a + 3)
                turned(p, 6)
                turned(p, 7)
                if select is not None:
                    rounds(select, 12, TOPK // 8)
                    keys = (select + 1) * P
                    dve.tensor_scalar(sel[:, select, 0:keys], work[:, select - 1, 0:keys],
                                      0.5 * (MASKED + TAKEN), MASKED, ALU.is_gt, ALU.mult
                                      ).then_inc(sem("sel_ready"), 1)
                y_lows(p)

            dve.wait_ge(sem("iscore"), NT - 1)
            for p in range(NQ):
                att(p, fox_tab, p + 1 if p + 1 < NT else None)
            for p in range(NQ, 2 * NQ):
                att(p, dsa_tab)

            def merge_branches(m):
                dve.wait_ge(used[2], st_bra.turn(2, m) + 1)
                dve.wait_ge(sem("gate_ready"), 2 * m + 2)
                dve.tensor_tensor(nt[:, 0, :], ps[:, 2, :], nsq[:, 0, :], ALU.mult).then_inc(sem("gated"), 1)
                dve.tensor_tensor(nt[:, 1, :], ps[:, SA, :], nsq[:, 1, :], ALU.mult).then_inc(sem("gated"), 1)
                dve.wait_ge(sem("gated"), 2 * m + 2)
                dve.sem_inc(bank_free[2], 1)
                dve.tensor_tensor(nt[:, 2, :], nt[:, 0, :], nt[:, 1, :], ALU.add).then_inc(sem("merged"), 1)
                dve.wait_ge(sem("m_hi"), m + 1)
                dve.tensor_tensor(m_lo[:, ds(m, 1), :], nt[:, 2:3, :], m_hi[:, ds(m, 1), :], ALU.subtract
                                  ).then_inc(sem("m_ready"), 1)

            with dve.Fori(0, KC) as m:
                merge_branches(m)
            wout(st_out2, lambda m: ada[:, ds(2 * KC + m, 1)], "x_mixed2")
            norm("n4", lambda m: gain2[:, m:m + 1], shift=3 * KC)
            mlp(st_mlp2, "mlp2", lambda m: ada[:, ds(5 * KC + m, 1)], False)
            norm("n5", col("g_final_2"), dst=False)
            for n in range(0, 2 * NT, 2):
                i = n // 2
                dve.wait_ge(sem("o_turned"), n + 1)
                if i >= 2:
                    dve.wait_ge(sem(f"out{i % 2}"), 16)
                dve.tensor_copy(otok[:, i % 2, 0:T], ps[:, 4 + n % 4, :]).then_inc(sem("otok0"), 1)
    return nc


_INS = ["x", "norm1_g", "w_in", "conv_w", "conv_norm_g", "ret_norm_g", "w_out", "norm2_g", "w_up", "w_down",
        "final_norm_g", "c_2", "w_ada_2", "b_ada_2", "g_norm1_2", "w_in_2", "b_forget_2", "rel_bias_2",
        "w_branch_fox_2", "w_branch_dsa_2", "w_out_2", "g_norm2_2", "w_mlp1_2", "w_mlp2_2", "g_final_2"]


def kernel(**inputs):
    import concourse.bacc as bacc
    from concourse.bass_utils import run_bass_kernel_spmd

    nc = bacc.Bacc("TRN2", target_bir_lowering=False, num_devices=1)
    arrays = {"tab": tables()}
    for name in _INS:
        arrays[name] = np.ascontiguousarray(inputs[name])
    args = {n: nc.dram_tensor(n, a.shape, mybir.dt.from_np(a.dtype), kind="ExternalInput").ap()
            for n, a in arrays.items()}
    args["out"] = nc.dram_tensor("out", (1, T, D), F32, kind="ExternalOutput").ap()
    build(nc, **args)
    r = run_bass_kernel_spmd(nc, [arrays], core_ids=[0])
    return r.results[0]["out"]
```

```python
from contextlib import ExitStack

import concourse.bass as bass
import numpy as np
from concourse import mybir

F32 = mybir.dt.float32
F32R = mybir.dt.float32r
BF16 = mybir.dt.bfloat16
ALU = mybir.AluOpType
ACT = mybir.ActivationFunctionType

P = 128
T = 512
NT = T // P
D = 1024
KC = D // P
QW = D // 2
NQ = QW // P
DFF = 4 * D
NF = DFF // D
HEADS = 8
HD = 64
IDX_HEADS = 4
TOPK = min(256, T // 4)
EPS = 1e-6
SLOTS = 4
AHEAD = 2
BUCKETS = 32
NREL = T + P
MASKED = -3.0e38
TAKEN = -3.4e38

SA, SB, TR, OU = 4, 5, 6, 7
TURNS = (TR, 3)

W1_CB, W1_CC, W1_CH, W1_RQ, W1_RK, W1_RV, W1_RG = [n * QW for n in range(7)]
SPLITS = [QW] * 3 + [HEADS] + [QW] * 3 + [IDX_HEADS * HD, HD, IDX_HEADS, D, D]
(W2_FQ, W2_FK, W2_FV, W2_F, W2_DQ, W2_DK, W2_DV, W2_QI, W2_KI, W2_WI, W2_GF, W2_GD) = [
    sum(SPLITS[:n]) for n in range(12)]

VECS = [("norm1_g", KC), ("conv_w", 3 * NQ), ("conv_norm_g", NQ), ("ret_norm_g", NQ), ("norm2_g", KC),
        ("final_norm_g", KC), ("c_2", KC), ("g_norm1_2", KC), ("g_norm2_2", KC), ("g_final_2", KC),
        ("b_ada_2", 6 * KC)]
VAT = {}
_n = 0
for _name, _rows in VECS:
    VAT[_name] = _n
    _n += _rows
NVEC = _n

NORMS = ["n1", "n2", "n3", "n4", "n5"]
ROOTED = ["n1", "n3", "n4", "n5"]
MLPS = ["mlp", "mlp2"]

TABS = [("ident", P), ("group64", P), ("flip8", P), ("causal", P), ("sel8", HEADS * P), ("onehot", NREL),
        ("cos", T), ("sin", T), ("decay", NQ * T)]
TAT = {}
_n = 0
for _name, _cols in TABS:
    TAT[_name] = _n
    _n += _cols
NTAB = _n
SMALL = TAT["sel8"]


def tables():
    t = np.zeros((P, NTAB), np.float32)
    r = np.arange(P)
    t[:, TAT["ident"]:][:, :P] = np.eye(P)
    t[:, TAT["group64"]:][:, :P] = (r[:, None] // HD) == (r[None, :] // HD)
    t[:, TAT["flip8"]:][:, :P] = 8.0 * np.eye(P)[::-1]
    t[:, TAT["causal"]:][:, :P] = np.where(r[None, :] <= r[:, None], 0.0, MASKED)
    for h in range(HEADS):
        t[h, TAT["sel8"] + h * P:TAT["sel8"] + (h + 1) * P] = -8.0
    n = np.maximum(T - 1 - np.arange(NREL), 0)
    large = 16 + (np.log(np.maximum(n, 1) / 16.0) / np.log(8.0) * 16).astype(np.int64)
    bucket = np.where(n < 16, n, np.minimum(large, BUCKETS - 1))
    t[:BUCKETS, TAT["onehot"]:][:, :NREL] = bucket[None, :] == np.arange(BUCKETS)[:, None]
    half = P // 2
    inv = (1.0 / (np.float32(10000.0) ** (np.arange(half, dtype=np.float32) / half))).astype(np.float32)
    ang = np.arange(T, dtype=np.float32)[None, :] * np.concatenate([inv, inv])[:, None]
    t[:, TAT["cos"]:][:, :T] = np.cos(ang)
    t[:, TAT["sin"]:][:, :T] = np.sin(ang) * np.where(r < half, 1.0, -1.0)[:, None]
    for h in range(NQ):
        gamma = 1.0 - 2.0 ** (-5.0 - h)
        diff = np.arange(T)[None, :] - r[:, None]
        t[:, TAT["decay"] + h * T:][:, :T] = np.where(diff >= 0, gamma ** np.maximum(diff, 0), 0.0) * P ** -0.5
    return t


def selection_plan(parts):
    rounds = [(i, n) for i in range(1, NT) for n in range(TOPK // 8)]
    total = sum(i + 1.5 for i, _ in rounds)
    plan, done = [[] for _ in range(parts)], 0.0
    for i, n in rounds:
        plan[int(done / total * parts)].append((i, n))
        done += i + 1.5
    return plan


def before(name):
    return KC * NORMS.index(name)


def mlp_before(name):
    return NF * KC * MLPS.index(name)


def wait(eng, sem, n):
    if not isinstance(n, int) or n > 0:
        eng.wait_ge(sem, n)


class Stage:

    def __init__(self, before, n, k, dmas=()):
        self.base = [b + (before.n if before and s < before.k else 0)
                     for s, b in enumerate(before.base if before else [1] * SLOTS)]
        self.raws = [b + (16 * before.n * before.dmas[s] if before and s < before.k else 0)
                     for s, b in enumerate(before.raws if before else [0] * SLOTS)]
        self.n, self.k = n, k
        self.dmas = list(dmas) or [1] * SLOTS

    def turn(self, s, i):
        return self.base[s] + i

    def landed(self, s, i):
        return self.raws[s] + 16 * self.dmas[s] * (i + 1)


def build(nc, tab, x, norm1_g, w_in, conv_w, conv_norm_g, ret_norm_g, w_out, norm2_g, w_up, w_down,
          final_norm_g, c_2, w_ada_2, b_ada_2, g_norm1_2, w_in_2, b_forget_2, rel_bias_2,
          w_branch_fox_2, w_branch_dsa_2, w_out_2, g_norm2_2, w_mlp1_2, w_mlp2_2, g_final_2, out):
    ds = bass.ds
    rows = {"norm1_g": norm1_g, "conv_w": conv_w, "conv_norm_g": conv_norm_g, "ret_norm_g": ret_norm_g,
            "norm2_g": norm2_g, "final_norm_g": final_norm_g, "c_2": c_2, "g_norm1_2": g_norm1_2,
            "g_norm2_2": g_norm2_2, "g_final_2": g_final_2, "b_ada_2": b_ada_2}

    st_ret = Stage(None, NQ, 4)
    st_conv = Stage(st_ret, NQ, 3)
    st_out = Stage(st_conv, KC // 4, 4)
    st_mlp = Stage(st_out, NF * 4, 4)
    st_idx = Stage(st_mlp, 1, 4, [1, 1, 2, 2])
    st_att = Stage(st_idx, 2 * NQ, 3)
    st_bra = Stage(st_att, KC, 3, [1, 1, 2, 1])
    st_out2 = Stage(st_bra, KC // 4, 4)
    st_mlp2 = Stage(st_out2, NF * 4, 4)

    bias_rows = nc.dram_tensor("bias_rows", [HEADS, NREL], F32).ap()

    ctx = ExitStack()
    with ctx:
        def sb(name, shape, dt=F32, where=ctx):
            return where.enter_context(nc.sbuf_tensor(name, shape, dt))

        sems = {}

        def sem(name):
            if name not in sems:
                sems[name] = ctx.enter_context(nc.semaphore(name))
            return sems[name]

        xres = sb("xres", [P, KC, T])
        u_hi, u_lo = sb("u_hi", [P, KC, T], F32R), sb("u_lo", [P, KC, T], F32R)
        y_hi, y_lo = sb("y_hi", [P, KC, T], F32R), sb("y_lo", [P, KC, T], F32R)
        raw = sb("raw", [P, SLOTS, KC * P])
        w_hi, w_lo = sb("w_hi", [P, SLOTS, KC * P], F32R), sb("w_lo", [P, SLOTS, KC * P], F32R)
        small = sb("small", [P, SMALL])
        ident = small[:, TAT["ident"]:TAT["ident"] + P]
        group64 = small[:, TAT["group64"]:TAT["group64"] + P]
        flip8 = small[:, TAT["flip8"]:TAT["flip8"] + P]
        identb, causalb = sb("identb", [P, P], BF16), sb("causalb", [P, P], BF16)
        ones = sb("ones", [P, P])
        epsc = sb("epsc", [P, 1])
        vec = sb("vec", [P, NVEC])
        ada = sb("ada", [P, 6 * KC])
        gain1, gain2 = sb("gain1", [P, KC]), sb("gain2", [P, KC])
        gsq = sb("gsq", [P, KC])
        gones = sb("gones", [P, P])
        rootc = sb("rootc", [P, NT])
        bfor = sb("bfor", [HEADS, 1])
        rowsum, rinv, mneg = sb("rowsum", [P, 8]), sb("rinv", [P, 8]), sb("mneg", [P, 8])
        wtok = sb("wtok", [P, NT * IDX_HEADS])
        top8 = sb("top8", [P, 8])
        nt = sb("nt", [P, 3, T])
        nsq = sb("nsq", [P, 2, T])
        nrs = sb("nrs", [P, T])

        one = ExitStack()
        decay = sb("decay", [P, NQ, T], where=one)
        start = ExitStack()
        xtok = sb("xtok", [P, NT, D], where=start)
        start.close()
        acc = sb("acc", [P, 6 * D], where=one)
        mix = ExitStack()
        rope = sb("rope", [P, 2, T], where=mix)
        cosr, sinr = rope[:, 0, :], rope[:, 1, :]
        vf, vtok = sb("vf", [P, T], where=mix), sb("vtok", [P, NT, P], where=mix)
        qf, kf = sb("qf", [P, T], where=mix), sb("kf", [P, T], where=mix)
        sdec = sb("sdec", [P, NT, T], where=mix)
        osb, sg, silu = sb("osb", [P, T], where=mix), sb("sg", [P, T], where=mix), sb("silu", [P, T], where=mix)
        prod, ycv = sb("prod", [P, T + 2], where=mix), sb("ycv", [P, T], where=mix)
        ccs = vf
        mix.close()
        adaw = sb("adaw", [P, 2, 6 * D // 4], where=one)
        one.close()
        pre = ExitStack()
        vrow = sb("vrow", [NVEC, P], where=pre)
        oneh = sb("oneh", [BUCKETS, NREL], where=pre)
        rbias = sb("rbias", [BUCKETS, HEADS], where=pre)
        fbrow = sb("fbrow", [HEADS, NREL], where=pre)
        pre.close()

        two = ExitStack()
        merge = ExitStack()
        ftab, btab = sb("ftab", [P, HEADS, T], where=merge), sb("btab", [P, HEADS, T], where=merge)
        merge.close()
        m_hi, m_lo = sb("m_hi", [P, KC, T], F32R, where=two), sb("m_lo", [P, KC, T], F32R, where=two)
        qa, ka = sb("qa", [P, T], where=two), sb("ka", [P, T], where=two)
        va, vatok = sb("va", [P, T], where=two), sb("vatok", [P, NT, P], where=two)
        work = sb("work", [P, NT - 1, T], where=two)
        sel = sb("sel", [P, NT, T], BF16, where=two)
        index = ExitStack()
        qi, ki = sb("qi", [P, 2, T], where=index), sb("ki", [P, T], where=index)
        fw = sb("fw", [P, T], where=index)
        sel8 = sb("sel8", [HEADS, HEADS * P], where=index)
        index.close()
        prob = sb("prob", [P, 2, T], where=two)
        probt = sb("probt", [P, NT, T], where=two)
        two.close()
        last = ExitStack()
        otok = sb("otok", [P, NT, D], where=last)
        last.close()

        ps = ctx.enter_context(nc.psum_tensor("ps", [P, 8, T], F32))

        raw_ready = [sem(f"raw_ready{s}") for s in range(SLOTS)]
        hi_ready = [sem(f"hi_ready{s}") for s in range(SLOTS)]
        lo_ready = [sem(f"lo_ready{s}") for s in range(SLOTS)]
        used = [sem(f"used{s}") for s in range(SLOTS)]
        bank_free = [sem(f"bank_free{s}") for s in range(SLOTS)]

        block = ctx.enter_context(nc.Block())

        @block.sync
        def _(sp):
            def load(st, s, i, *pairs):
                if st.raws[s] == 0:
                    sp.wait_ge(sem("x_in0"), 16)
                else:
                    sp.wait_ge(raw_ready[s], st.raws[s])
                wait(sp, lo_ready[s], st.turn(s, i))
                dst = raw[:, s, :].rearrange("p (k m) -> p k m", k=KC)
                for cut, src in pairs:
                    sp.dma_start(cut(dst), src).then_inc(raw_ready[s], 16)

            def whole(dst):
                return dst

            def cols(w, at, n=P):
                return w.rearrange("(k p) n -> p k n", p=P)[:, :, ds(at, n)]

            for i in range(NT):
                sp.dma_start(xtok[:, i, :], x[0, i * P:(i + 1) * P, :]).then_inc(sem(f"x_in{i}"), 16)

            with sp.Fori(0, NQ) as j:
                for s, at in enumerate([W1_RV, W1_RQ, W1_RK, W1_RG]):
                    load(st_ret, s, j, (whole, cols(w_in, at + j * P)))
            with sp.Fori(0, NQ) as j:
                for s, at in enumerate([W1_CC, W1_CH, W1_CB]):
                    load(st_conv, s, j, (whole, cols(w_in, at + j * P)))
            with sp.Fori(0, KC // 4) as i:
                for s in range(4):
                    load(st_out, s, i, (whole, cols(w_out, i * 4 * P + s * P)))

            def mlp(st, up, down, with_ada):
                with sp.Fori(0, NF) as q:
                    for d in range(2):
                        with sp.Fori(0, 2) as i:
                            for s in range(4):
                                if d == 0:
                                    src = cols(up, q * D + i * 4 * P + s * P)
                                else:
                                    src = down.rearrange("(q k p) n -> q p k n", q=NF, p=P)[
                                        ds(q, 1), :, :, ds(i * 4 * P + s * P, P)
                                    ].rearrange("q p k n -> p (q k) n")
                                load(st, s, q * 4 + 2 * d + i, (whole, src))
                                if with_ada and s % 2:
                                    b = s // 2
                                    sp.wait_ge(sem(f"ada_used{b}"), q * 4 + 2 * d + i + 1)
                                    sp.wait_ge(sem("mix_done"), 1)
                                    src = w_ada_2.rearrange("(q k p) n -> q k p n", q=NF, p=P)[
                                        ds(q, 1), d, :, ds(i * 3 * D + b * 3 * D // 2, 3 * D // 2)]
                                    sp.dma_start(adaw[:, b, :], src.rearrange("q p n -> p (q n)")
                                                 ).then_inc(sem(f"ada_in{b}"), 16)

            mlp(st_mlp, w_up, w_down, True)

            load(st_idx, 0, 0, (whole, cols(w_in_2, W2_QI)))
            load(st_idx, 1, 0, (whole, cols(w_in_2, W2_QI + P)))
            load(st_idx, 2, 0, (lambda d: d[:, :, 0:HD], cols(w_in_2, W2_KI, HD)),
                 (lambda d: d[:, :, HD:P], cols(w_in_2, W2_KI, HD)))
            load(st_idx, 3, 0, (lambda d: d[:, :, 0:HEADS], cols(w_in_2, W2_F, HEADS)),
                 (lambda d: d[:, :, 32:32 + IDX_HEADS], cols(w_in_2, W2_WI, IDX_HEADS)))
            sp.wait_ge(sem("ada_sum"), 1)
            sp.wait_ge(sem("brow_out"), 16)
            shifted = bass.AP(bias_rows.tensor, 0, [[1, P], [NREL, HEADS], [1, T]])
            sp.dma_start(ftab[:], shifted).then_inc(sem("shifted_in"), 16)
            sp.dma_start(sel8[:], tab[0:HEADS, TAT["sel8"]:TAT["sel8"] + HEADS * P]).then_inc(sem("sel8_in"), 16)
            for base, at3 in ((0, (W2_FV, W2_FQ, W2_FK)), (NQ, (W2_DV, W2_DQ, W2_DK))):
                with sp.Fori(0, NQ) as g:
                    for s, at in enumerate(at3):
                        load(st_att, s, base + g, (whole, cols(w_in_2, at + g * P)))
            with sp.Fori(0, KC) as m:
                load(st_bra, 0, m, (whole, cols(w_in_2, W2_GF + m * P)))
                load(st_bra, 1, m, (whole, cols(w_in_2, W2_GD + m * P)))
                load(st_bra, 2, m, (lambda d: d[:, 0:NQ, :], cols(w_branch_fox_2, m * P)),
                     (lambda d: d[:, NQ:KC, :], cols(w_branch_dsa_2, m * P)))
            with sp.Fori(0, KC // 4) as i:
                for s in range(4):
                    load(st_out2, s, i, (whole, cols(w_out_2, i * 4 * P + s * P)))
            mlp(st_mlp2, w_mlp1_2, w_mlp2_2, False)

            for i in range(NT):
                sp.wait_ge(sem("otok0"), i + 1)
                sp.wait_ge(sem("otok1"), i + 1)
                sp.dma_start(out[0, i * P:(i + 1) * P, :], otok[:, i, :]).then_inc(sem("out"), 16)
            sp.wait_ge(sem("out"), 16 * NT)

        @block.gpsimd
        def _(pool):
            for s in range(SLOTS):
                pool.sem_inc(lo_ready[s], 1)
            pool.memset(ones[:], 1.0).then_inc(sem("const"), 1)
            pool.memset(epsc[:], EPS).then_inc(sem("const"), 1)

            def lo(st, s, i):
                pool.wait_ge(hi_ready[s], st.turn(s, i) + 1)
                pool.tensor_tensor(w_lo[:, s, :], raw[:, s, :], w_hi[:, s, :], ALU.subtract
                                   ).then_inc(lo_ready[s], 1)

            for st in (st_ret, st_conv, st_out, st_mlp, st_idx, st_att, st_bra, st_out2, st_mlp2):
                if st.n == 1:
                    for s in range(st.k):
                        lo(st, s, 0)
                else:
                    with pool.Fori(0, st.n) as i:
                        for s in range(st.k):
                            lo(st, s, i)

        @block.tensor
        def _(pe):
            def unit(st, s, i, r_hi, r_lo, chunk_ready=None, part=(0, KC), cols=P, ks=range(KC), bank=None,
                     opens=True, closes=True):
                bank = s if bank is None else bank
                if opens:
                    pe.wait_ge(lo_ready[s], st.turn(s, i) + 1)
                    wait(pe, bank_free[s], st.turn(s, i))
                last = None
                for k in ks[part[0]:part[1]]:
                    if chunk_ready:
                        chunk_ready(k)
                    c = slice(k * P, k * P + cols)
                    for w, r in ((w_hi, r_hi), (w_hi, r_lo), (w_lo, r_hi)):
                        last = pe.matmul(ps[0:cols, bank, :], w[:, s, c], r[:, k, :],
                                         start=(k == ks[0] and w is w_hi and r is r_hi),
                                         stop=(k == ks[-1] and w is w_lo))
                if closes:
                    last.then_inc(used[s], 1)

            def square_sum(name):
                pe.wait_ge(sem("total"), before(name) - KC + KC)
                pe.matmul(ps[:, SA, :], ones[:], nt[:, 2, :], start=True, stop=False)
                if name == "n3":
                    pe.wait_ge(sem("total_f"), KC)
                    pe.matmul(ps[:, TR, :], ones[:], nt[:, 1, :], start=True, stop=False)
                pe.wait_ge(sem("norm_sq"), before(name) + KC)
                if name == "n3":
                    pe.matmul(ps[:, TR, :], ones[:], nsq[:, (KC - 1) % 2, :], start=False, stop=True
                              ).then_inc(sem("sum_f"), 1)
                    pe.wait_ge(sem("gones"), 1)
                pe.matmul(ps[:, SA, :], gones[:] if name == "n3" else ones[:], nsq[:, (KC - 1) % 2, :],
                          start=False, stop=True).then_inc(sem("norm_sum"), 1)

            def two_units(st, i, r_hi, r_lo, chunk_ready, ks=range(KC), part=(0, KC)):
                for n in range(*part):
                    for s in range(2):
                        unit(st, s, i, r_hi, r_lo, chunk_ready if s == 0 else None, part=(n, n + 1), ks=ks,
                             opens=(n == 0), closes=(n == KC - 1))

            for s in range(SLOTS):
                pe.sem_inc(used[s], 1)
            pe.wait_ge(sem("small_in"), 16)
            for i in range(NT):
                pe.wait_ge(sem(f"x_in{i}"), 16)
                for m in range(KC):
                    t = pe.transpose(ps[:, m, i * P:(i + 1) * P], xtok[:, i, m * P:(m + 1) * P], ident)
                    if i == NT - 1:
                        t.then_inc(sem("x_turned"), 1)
            pe.wait_ge(sem("const"), 2)
            for m in range(KC):
                pe.wait_ge(sem("norm_sq"), m + 1)
                if m == 0:
                    pe.wait_ge(sem("x_ready"), 1)
                last = pe.matmul(ps[:, 0, :], ones[:], nsq[:, m % 2, :], start=(m == 0), stop=(m == KC - 1))
                last.then_inc(sem("n1_added" if m < KC - 1 else "norm_sum"), 1)
                if m == 2:
                    pe.wait_ge(sem("vrow_in"), 16 * len(VECS))
                    pe.wait_ge(sem("x_ready"), 2)
                    pe.transpose(ps[:, 1, 0:NVEC], vrow[:], ident[0:NVEC, 0:NVEC]).then_inc(sem("vec_turned"), 1)

            def bias_rows_made():
                pe.wait_ge(sem("bias_in"), 32)
                pe.matmul(ps[0:HEADS, 2, :], rbias[:], oneh[:, 0:T], start=True, stop=True)
                pe.matmul(ps[0:HEADS, 3, 0:P], rbias[:], oneh[:, T:NREL], start=True, stop=True
                          ).then_inc(sem("brow_done"), 1)

            def turn_v(src, dst_sem):
                for i in range(NT):
                    last = pe.transpose(ps[:, TR, i * P:(i + 1) * P], src[:, i * P:(i + 1) * P], ident)
                last.then_inc(sem(dst_sem), 1)

            def ret_scores(p):
                pe.wait_ge(sem("qk_ready"), 2 * p + 2)
                for b in range(NT):
                    if b >= 2:
                        pe.wait_ge(sem("sdec_ready"), NT * p + b - 1)
                    pe.matmul(ps[:, SA + b % 2, 0:T - b * P], kf[:, b * P:(b + 1) * P], qf[:, b * P:T],
                              start=True, stop=True).then_inc(sem("ret_s"), 1)

            def ret_out(p):
                pe.wait_ge(sem("vtok_ready"), p + 1)
                for b in range(NT):
                    pe.wait_ge(sem("sdec_ready"), NT * p + b + 1)
                    last = pe.matmul(ps[:, OU, b * P:T], vtok[:, b, :], sdec[:, b, 0:T - b * P],
                                     start=(b == 0), stop=(b == NT - 1))
                last.then_inc(sem("ret_o"), 1)

            def ret_sum(p):
                pe.wait_ge(sem("osq_ready"), p + 1)
                pe.matmul(ps[:, SA, :], ones[:], nsq[:, 0, :], start=True, stop=True).then_inc(sem("ret_sum"), 1)

            def ret(j, p):
                if p is None:
                    pe.wait_ge(sem("x_ready"), KC)
                    bias_rows_made()
                    pe.wait_ge(sem("norm_root"), 1)
                    pe.wait_ge(sem("vec_ready"), 1)
                    two_units(st_ret, j, u_hi, u_lo, lambda k: pe.wait_ge(sem("norm_u"), before("n1") + k + 1))
                    pe.wait_ge(sem("brow_read"), 2)
                else:
                    unit(st_ret, 0, j, u_hi, u_lo)
                    ret_scores(p)
                    unit(st_ret, 1, j, u_hi, u_lo)
                if p is not None:
                    ret_out(p)
                pe.wait_ge(sem("vf_ready"), j + 1)
                turn_v(vf, "vf_turned")
                unit(st_ret, 2, j, u_hi, u_lo)
                if p is not None:
                    ret_sum(p)
                unit(st_ret, 3, j, u_hi, u_lo)
                if p is not None:
                    pe.wait_ge(sem("ret_root"), p + 1)

            ret(0, None)
            with pe.Fori(1, NQ) as j:
                ret(j, j - 1)

            def conv_sum(p):
                pe.wait_ge(sem("csq_ready"), p + 1)
                pe.matmul(ps[:, SB, :], group64, nsq[:, 1, :], start=True, stop=True
                          ).then_inc(sem("conv_sum"), 1)

            unit(st_conv, 0, 0, u_hi, u_lo)
            ret_scores(NQ - 1)
            unit(st_conv, 1, 0, u_hi, u_lo)
            ret_out(NQ - 1)
            unit(st_conv, 2, 0, u_hi, u_lo)
            ret_sum(NQ - 1)
            with pe.Fori(1, NQ) as j:
                unit(st_conv, 0, j, u_hi, u_lo)
                unit(st_conv, 1, j, u_hi, u_lo)
                conv_sum(j - 1)
                unit(st_conv, 2, j, u_hi, u_lo)

            def y_ready(k):
                if k < NQ:
                    pe.wait_ge(sem("ycv_ready"), k + 1)
                else:
                    pe.wait_ge(sem("yret_ready"), k - NQ + 1)

            order = [NQ + k for k in range(NQ)] + list(range(NQ))
            two_units(st_out, 0, y_hi, y_lo, y_ready, order, (0, NQ))
            conv_sum(NQ - 1)
            two_units(st_out, 0, y_hi, y_lo, y_ready, order, (NQ, KC))
            for s in range(2, 4):
                unit(st_out, s, 0, y_hi, y_lo)
            for s in range(4):
                unit(st_out, s, 1, y_hi, y_lo)

            def mlp_up(st, norm, q, i, between=None):
                two_units(st, q * 4 + i, u_hi, u_lo, lambda k: pe.wait_ge(sem("norm_u"), before(norm) + k + 1))
                if between:
                    between()
                for s in range(2, 4):
                    unit(st, s, q * 4 + i, u_hi, u_lo)

            def mlp_down(st, name, q, i):
                for s in range(4):
                    unit(st, s, q * 4 + 2 + i, y_hi, y_lo,
                         (lambda k: pe.wait_ge(sem("mlp_h"), q * KC + (mlp_before(name) + k + 1))) if s == 0 else None)

            def mlp_parts(st, name, norm, q0, q1):
                with pe.Fori(q0, q1) as q:
                    with pe.Fori(0, 2) as i:
                        mlp_up(st, norm, q, i)
                    with pe.Fori(0, 2) as i:
                        mlp_down(st, name, q, i)

            mlp_up(st_mlp, "n2", 0, 0, lambda: square_sum("n2"))
            mlp_up(st_mlp, "n2", 0, 1)
            with pe.Fori(0, 2) as i:
                mlp_down(st_mlp, "mlp", 0, i)
            mlp_parts(st_mlp, "mlp", "n2", 1, NF)

            pe.wait_ge(sem("acc_done"), 2 * NF * 4 + 1)
            for m in range(6 * KC):
                last = pe.matmul(ps[:, SB, m:m + 1], acc[:, m * P:(m + 1) * P], ones[:, 0:1], start=True, stop=True)
            last.then_inc(sem("ada_sum"), 1)
            square_sum("n3")

            ready = lambda k: pe.wait_ge(sem("norm_u"), before("n3") + k + 1)
            two_units(st_idx, 0, u_hi, u_lo, ready)
            unit(st_idx, 2, 0, u_hi, u_lo)
            unit(st_idx, 3, 0, u_hi, u_lo, cols=32 + IDX_HEADS)
            pe.wait_ge(sem("shifted_in"), 16)
            pe.wait_ge(sem("ada_ready"), 1)
            for h in range(HEADS):
                if h >= 2:
                    pe.wait_ge(sem("btab_ready"), h - 1)
                pe.matmul(ps[:, SA + h % 2, :], flip8, ftab[:, h, :], start=True, stop=True
                          ).then_inc(sem("btab_s"), 1)
            pe.wait_ge(sem("fw_ready"), 1)
            for i in range(NT):
                last = pe.transpose(ps[:, TR, i * 64:i * 64 + 32 + IDX_HEADS], fw[0:32 + IDX_HEADS, i * P:(i + 1) * P],
                                    ident[0:32 + IDX_HEADS, 0:32 + IDX_HEADS])
            last.then_inc(sem("wi_turned"), 1)

            def idx_scores(n):
                i, h = n // IDX_HEADS + 1, n % IDX_HEADS
                if n == 0:
                    pe.wait_ge(sem("qi_ready"), 3)
                    pe.wait_ge(sem("btab_ready"), HEADS)
                if n >= 2:
                    pe.wait_ge(sem("relu_ready"), n - 1)
                b = HD * (h % 2)
                pe.matmul(ps[:, SA + n % 2, 0:(i + 1) * P], qi[b:b + HD, h // 2, i * P:(i + 1) * P],
                          ki[b:b + HD, 0:(i + 1) * P], start=True, stop=True).then_inc(sem("idx_s"), 1)

            def s_step(p, n, dsa):
                i, hh = n // 2, n % 2
                b = HD * hh
                if n == 0:
                    pe.wait_ge(sem("att_qk"), 2 * p + 2)
                if n >= 2:
                    pe.wait_ge(sem("att_logit"), 8 * p + n - 1)
                keys = (i + 1) * P
                bank = SA + n % 2
                pe.matmul(ps[:, bank, 0:keys], qa[b:b + HD, i * P:(i + 1) * P], ka[b:b + HD, 0:keys],
                          start=True, stop=False)
                if dsa:
                    pe.wait_ge(sem("sel_ready"), i + 1)
                    last = pe.matmul(ps[:, bank, 0:keys], identb[:], sel[:, i, 0:keys], start=False, stop=True)
                else:
                    last = pe.matmul(ps[:, bank, keys - P:keys], identb[:], causalb[:], start=False, stop=True)
                last.then_inc(sem("att_s"), 1)

            def t_step(p, n):
                i = n // 2
                pe.wait_ge(sem("att_prob"), 8 * p + n + 1)
                if n == 0:
                    pe.wait_ge(sem("vatok_ready"), p + 1)
                elif n >= 2:
                    pe.wait_ge(sem("att_probt"), 8 * p + n - 1)
                for j in range(i + 1):
                    last = pe.transpose(ps[:, TURNS[n % 2], j * P:(j + 1) * P], prob[:, n % 2, j * P:(j + 1) * P], ident)
                last.then_inc(sem("att_t"), 1)

            def pv(p, i):
                pe.wait_ge(sem("att_probt"), 8 * p + 2 * i + 2)
                for j in range(i + 1):
                    for hh in range(2):
                        b = HD * hh
                        last = pe.matmul(ps[b:b + HD, OU, i * P:(i + 1) * P], vatok[:, j, b:b + HD],
                                         probt[:, 2 * (i % 2) + hh, j * P:(j + 1) * P], start=(j == 0), stop=(j == i))
                last.then_inc(sem("att_o"), 1)

            def att(st, units, p, dsa):
                def half():
                    if units:
                        units.pop(0)()
                half()
                s_step(p, 0, dsa)
                s_step(p, 1, dsa)
                half()
                for a in range(3):
                    t_step(p, 2 * a)
                    s_step(p, 2 * a + 2, dsa)
                    t_step(p, 2 * a + 1)
                    s_step(p, 2 * a + 3, dsa)
                    if a >= 1:
                        pv(p, a - 1)
                    half()
                t_step(p, 6)
                t_step(p, 7)
                pv(p, 2)
                half()
                pv(p, 3)

            def halves(st, g, n=3):
                def one_half(s, h):
                    return lambda: unit(st, s, g, u_hi, u_lo, part=(h * KC // 2, (h + 1) * KC // 2),
                                        opens=(h == 0), closes=(h == 1))
                return [one_half(s, h) for s in range(n) for h in range(2)]

            def turn_va(g):
                pe.wait_ge(sem("va_ready"), g + 1)
                turn_v(va, "va_turned")

            n = 0
            for half in halves(st_att, 0):
                half()
                for _ in range(2):
                    idx_scores(n)
                    n += 1
            pe.wait_ge(sem("relu_ready"), NT * (NT - 1))
            pe.wait_ge(sem("sel8_in"), 16)
            pe.wait_ge(sem("fcum_ready"), 1)
            for h in range(HEADS):
                if h >= 2:
                    pe.wait_ge(sem("ftab_ready"), h - 1)
                pe.matmul(ps[:, SA + h % 2, :], sel8[:, h * P:(h + 1) * P], nt[0:HEADS, 0, :], start=True, stop=True
                          ).then_inc(sem("ftab_s"), 1)
            pe.wait_ge(sem("wtok_ready"), 1)
            turn_va(0)
            pe.wait_ge(sem("ftab_ready"), HEADS)
            with pe.Fori(1, NQ) as g:
                att(st_att, halves(st_att, g), g - 1, False)
                turn_va(g)
            att(st_att, halves(st_att, NQ), NQ - 1, False)
            turn_va(NQ)
            with pe.Fori(NQ + 1, 2 * NQ) as g:
                att(st_att, halves(st_att, g), g - 1, True)
                turn_va(g)

            def branch(m):
                pe.wait_ge(lo_ready[2], st_bra.turn(2, m) + 1)
                wait(pe, bank_free[2], st_bra.turn(2, m))
                for b, k0 in ((2, 0), (SA, NQ)):
                    for k in range(k0, k0 + NQ):
                        pe.wait_ge(sem("att_y"), k + 1)
                        c = slice(k * P, (k + 1) * P)
                        for w, r in ((w_hi, y_hi), (w_hi, y_lo), (w_lo, y_hi)):
                            last = pe.matmul(ps[:, b, :], w[:, 2, c], r[:, k, :],
                                             start=(k == k0 and w is w_hi and r is y_hi),
                                             stop=(k == k0 + NQ - 1 and w is w_lo))
                last.then_inc(used[2], 1)

            att(st_bra, halves(st_bra, 0, 2), 2 * NQ - 1, True)
            branch(0)
            with pe.Fori(1, KC) as m:
                unit(st_bra, 0, m, u_hi, u_lo)
                unit(st_bra, 1, m, u_hi, u_lo)
                branch(m)

            two_units(st_out2, 0, m_hi, m_lo, lambda k: pe.wait_ge(sem("m_ready"), k + 1))
            for s in range(2, 4):
                unit(st_out2, s, 0, m_hi, m_lo)
            for s in range(4):
                unit(st_out2, s, 1, m_hi, m_lo)
            square_sum("n4")
            mlp_parts(st_mlp2, "mlp2", "n4", 0, NF - 1)
            with pe.Fori(0, 2) as i:
                mlp_up(st_mlp2, "n4", NF - 1, i)
            mlp_down(st_mlp2, "mlp2", NF - 1, 0)

            def turn_out(m, i):
                c = m // 4
                return pe.transpose(ps[:, 4 * (1 - c) + i, (m % 4) * P:(m % 4 + 1) * P],
                                    xres[:, m, i * P:(i + 1) * P], ident)

            for s in range(4):
                unit(st_mlp2, s, NF * 4 - 1, y_hi, y_lo)
                pe.wait_ge(sem("x_gained"), s + 1)
                for i in range(NT):
                    last = turn_out(s, i)
            last.then_inc(sem("o_first"), 1)
            pe.wait_ge(sem("x_gained"), KC - 1)
            for i in range(3):
                for m in range(4, KC - 1):
                    turn_out(m, i)
            pe.wait_ge(sem("total"), before("n5"))
            pe.wait_ge(sem("norm_sq"), before("n5") + KC)
            pe.wait_ge(sem("mlp_x"), 2 * NF * KC)
            for i in range(NT):
                pe.matmul(ps[:, 3, i:i + 1], nt[:, 2, i * P:(i + 1) * P], ones[:, 0:1], start=True, stop=False)
                last = pe.matmul(ps[:, 3, i:i + 1], nsq[:, (KC - 1) % 2, i * P:(i + 1) * P], ones[:, 0:1],
                                 start=False, stop=True)
            last.then_inc(sem("norm_sum"), 1)
            pe.wait_ge(sem("x_gained"), KC)
            for i in range(3):
                turn_out(KC - 1, i).then_inc(sem("o_second"), 1)
            pe.wait_ge(sem("norm_root"), ROOTED.index("n5") + 1)
            for m in range(4, KC):
                last = turn_out(m, 3)
            last.then_inc(sem("o_second"), 1)

        @block.scalar
        def _(act):
            def ahead(st, s, i):
                t = s + AHEAD
                if t >= st.k:
                    t, i = t - st.k, i + 1
                act.wait_ge(raw_ready[t], st.landed(t, i))
                wait(act, used[t], st.turn(t, i))
                act.activation(w_hi[:, t, :], raw[:, t, :], ACT.Copy).then_inc(hi_ready[t], 1)

            def square(name, m, x_sem, x0, n=None):
                n = m if n is None else n
                act.wait_ge(sem(x_sem), x0 + m + 1)
                act.wait_ge(sem("total"), before(name) - KC + m)
                act.activation(nsq[:, n % 2:n % 2 + 1, :], xres[:, ds(m, 1), :], ACT.Square
                               ).then_inc(sem("norm_sq"), 1)

            def norm(name, shift=None, split=True):
                if name == "n3":
                    act.wait_ge(sem("both_sums"), 2)
                    act.activation(nrs[:], nrs[:], ACT.Sqrt).then_inc(sem("norm_root"), 1)
                    act.activation(nsq[:, 0, :], ps[:, TR, :], ACT.Sqrt, bias=epsc[:, 0:1], scale=1.0 / D
                                   ).then_inc(sem("root_f"), 1)
                else:
                    act.wait_ge(sem("norm_sum"), NORMS.index(name) + 1)
                    act.activation(nrs[:], ps[:, 0 if name == "n1" else SA, :], ACT.Sqrt, bias=epsc[:, 0:1], scale=1.0 / D
                                   ).then_inc(sem("norm_root"), 1)
                if split:
                    for m in range(KC):
                        act.wait_ge(sem("norm_t"), KC * ROOTED.index(name) + m + 1)
                        if shift is None:
                            act.activation(u_hi[:, m, :], nt[:, m % 3, :], ACT.Copy).then_inc(sem("norm_hi"), 1)
                        else:
                            act.activation(u_hi[:, m, :], nt[:, m % 3, :], ACT.Identity,
                                           bias=ada[:, shift + m:shift + m + 1]).then_inc(sem("norm_hi"), 1)

            for s in range(SLOTS):
                act.sem_inc(hi_ready[s], 1)
            act.dma_start(small[:], tab[:, 0:SMALL]).then_inc(sem("small_in"), 16)
            for name, n in VECS:
                src = rows[name]
                if name == "conv_w":
                    src = src.rearrange("t (j p) -> (t j) p", p=P)
                elif name == "c_2":
                    src = src.rearrange("a (j p) -> (a j) p", p=P)
                else:
                    src = src.rearrange("(j p) -> j p", p=P)
                act.dma_start(vrow[VAT[name]:VAT[name] + n, :], src).then_inc(sem("vrow_in"), 16)
            act.dma_start(oneh[:], tab[0:BUCKETS, TAT["onehot"]:TAT["onehot"] + NREL]).then_inc(sem("bias_in"), 16)
            act.dma_start(rbias[:], rel_bias_2).then_inc(sem("bias_in"), 16)
            act.dma_start(bfor[:], b_forget_2.rearrange("(h a) -> h a", a=1)).then_inc(sem("bfor_in"), 16)
            act.dma_start(rope[:], tab[:, TAT["cos"]:TAT["cos"] + 2 * T].rearrange("p (a t) -> p a t", a=2)
                          ).then_inc(sem("rope_in"), 16)

            for m in range(KC):
                act.wait_ge(sem("x_turned"), m + 1)
                if m >= 2:
                    act.wait_ge(sem("n1_added"), m - 1)
                act.activation(nsq[:, m % 2, :], ps[:, m, :], ACT.Square).then_inc(sem("norm_sq"), 1)
            for s in range(AHEAD):
                act.wait_ge(raw_ready[s], st_ret.landed(s, 0))
                act.activation(w_hi[:, s, :], raw[:, s, :], ACT.Copy).then_inc(hi_ready[s], 1)
            act.wait_ge(sem("const"), 2)
            norm("n1")
            act.wait_ge(sem("brow_done"), 1)
            act.activation(fbrow[:, 0:T], ps[0:HEADS, 2, :], ACT.Copy).then_inc(sem("brow_read"), 1)
            act.activation(fbrow[:, T:NREL], ps[0:HEADS, 3, 0:P], ACT.Copy).then_inc(sem("brow_read"), 1)
            act.wait_ge(sem("brow_read"), 2)
            act.dma_start(bias_rows, fbrow[:]).then_inc(sem("brow_out"), 16)
            act.wait_ge(sem("vec_turned"), 1)
            act.wait_ge(sem("brow_out"), 16)
            act.dma_start(decay[:], tab[:, TAT["decay"]:TAT["decay"] + NQ * T].rearrange("p (a t) -> p a t", a=NQ)
                          ).then_inc(sem("decay_in"), 16)

            def ret_act(j, p):
                ahead(st_ret, 0, j)
                act.wait_ge(used[0], st_ret.turn(0, j) + 1)
                wait(act, sem("vf_turned"), j)
                act.activation(vf[:], ps[:, 0, :], ACT.Copy).then_inc(bank_free[0], 1)
                act.wait_ge(bank_free[0], st_ret.turn(0, j) + 1)
                act.sem_inc(sem("vf_ready"), 1)
            def osq(p):
                act.wait_ge(sem("ret_o"), p + 1)
                act.activation(osb[:], ps[:, OU, :], ACT.Copy).then_inc(sem("osb_ready"), 1)
                act.activation(nsq[:, 0, :], ps[:, OU, :], ACT.Square).then_inc(sem("osq_ready"), 1)
            def ret_root(p):
                act.wait_ge(sem("ret_sum"), p + 1)
                act.activation(nrs[:], ps[:, SA, :], ACT.Sqrt, bias=epsc[:, 0:1], scale=1.0 / P
                               ).then_inc(sem("ret_root"), 1)
            def ret_hi(p):
                act.wait_ge(sem("ret_y"), p + 1)
                act.activation(y_hi[:, ds(NQ + p, 1), :], nt[:, 1:2, :], ACT.Copy).then_inc(sem("ret_hi"), 1)
            def ret(j, p):
                ret_act(j, p)
                ahead(st_ret, 1, j)
                if p is not None:
                    osq(p)
                act.wait_ge(sem("vf_turned"), j + 1)
                act.activation(vtok[:].rearrange("p a b -> p (a b)"), ps[:, TR, :], ACT.Copy
                               ).then_inc(sem("vtok_ready"), 1)
                ahead(st_ret, 2, j)
                if p is not None:
                    ret_root(p)
                ahead(st_ret, 3, j)
                act.wait_ge(used[3], st_ret.turn(3, j) + 1)
                wait(act, sem("silu_ready"), j)
                act.activation(sg[:], ps[:, 3, :], ACT.Sigmoid).then_inc(sem("sg_ready"), 1)
                if p is not None:
                    ret_hi(p)

            ret(0, None)
            with act.Fori(1, NQ) as j:
                ret(j, j - 1)

            def cc(j):
                act.wait_ge(used[0], st_conv.turn(0, j) + 1)
                wait(act, sem("prod_ready"), j)
                act.activation(ccs[:], ps[:, 0, :], ACT.Copy).then_inc(bank_free[0], 1)
            def csq(j):
                act.wait_ge(sem("ycv_done"), j + 1)
                wait(act, sem("conv_sum"), j)
                act.activation(nsq[:, 1, :], ycv[:], ACT.Square).then_inc(sem("csq_ready"), 1)
            def conv_root(p):
                act.wait_ge(sem("conv_sum"), p + 1)
                act.activation(sg[:], ps[:, SB, :], ACT.Sqrt, bias=epsc[:, 0:1], scale=1.0 / HD
                               ).then_inc(sem("conv_root"), 1)
            def conv_hi(p):
                act.wait_ge(sem("conv_t"), p + 1)
                act.activation(y_hi[:, ds(p, 1), :], nt[:, 0:1, :], ACT.Copy).then_inc(sem("conv_hi"), 1)

            ahead(st_conv, 0, 0)
            cc(0)
            ahead(st_conv, 1, 0)
            osq(NQ - 1)
            ahead(st_conv, 2, 0)
            ret_root(NQ - 1)
            ret_hi(NQ - 1)
            csq(0)
            with act.Fori(1, NQ) as j:
                ahead(st_conv, 0, j)
                cc(j)
                ahead(st_conv, 1, j)
                conv_root(j - 1)
                conv_hi(j - 1)
                ahead(st_conv, 2, j)
                csq(j)
            conv_root(NQ - 1)
            conv_hi(NQ - 1)

            for i in range(KC // 4):
                for s in range(4):
                    ahead(st_out, s, i)
                    act.wait_ge(sem("x_mixed"), i * 4 + s + 1)
                    act.activation(u_hi[:, ds(i * 4 + s, 1), :], xres[:, ds(i * 4 + s, 1), :], ACT.Copy,
                                   scale=vec[:, ds(VAT["norm2_g"] + i * 4 + s, 1)]).then_inc(sem("norm_hi"), 1)
                    square("n2", i * 4 + s, "x_mixed", 0, s)

            def mlp(st, name, next_norm):
                def up(q, i):
                    for s in range(4):
                        ahead(st, s, q * 4 + i)
                        act.wait_ge(used[s], st.turn(s, q * 4 + i) + 1)
                        if s >= 2:
                            act.wait_ge(sem("mlp_sq"), q * KC + i * 4 + (mlp_before(name) + s - 1))
                        if s == 1:
                            act.wait_ge(sem("norm_sum"), NORMS.index(next_norm))
                        act.activation(nsq[:, s % 2, :], ps[:, s, :], ACT.Relu).then_inc(bank_free[s], 1)
                        act.wait_ge(bank_free[s], st.turn(s, q * 4 + i) + 1)
                        act.activation(y_hi[:, ds(i * 4 + s, 1), :], nsq[:, s % 2:s % 2 + 1, :], ACT.Square
                                       ).then_inc(sem("mlp_hi"), 1)
                    act.wait_ge(sem("mlp_sq"), q * KC + i * 4 + (mlp_before(name) + 4))

                def down(q, i, last=False):
                    for s in range(4):
                        if not (last and st is st_mlp2 and s + AHEAD >= 4):
                            ahead(st, s, q * 4 + 2 + i)
                        if last is not False:
                            m = i * 4 + s
                            square(next_norm, m, "mlp_x", mlp_before(name) + (NF - 1) * KC)
                            if next_norm == "n5":
                                act.wait_ge(sem("norm_sq"), before("n5") + m + 1)
                                act.activation(xres[:, m, :], xres[:, m, :], ACT.Copy,
                                               scale=vec[:, VAT["g_final_2"] + m:VAT["g_final_2"] + m + 1]
                                               ).then_inc(sem("x_gained"), 1)

                with act.Fori(0, NF - 1) as q:
                    with act.Fori(0, 2) as i:
                        up(q, i)
                    with act.Fori(0, 2) as i:
                        down(q, i)
                with act.Fori(0, 2) as i:
                    up(NF - 1, i)
                down(NF - 1, 0, 0)
                down(NF - 1, 1, 1)

            mlp(st_mlp, "mlp", "n3")
            norm("n3", shift=0)

            ahead(st_idx, 0, 0)
            for s in range(2):
                act.wait_ge(used[s], st_idx.turn(s, 0) + 1)
                act.activation(qi[:, s, :], ps[:, s, :], ACT.Copy).then_inc(bank_free[s], 1)
                ahead(st_idx, s + 1, 0)
            act.wait_ge(used[2], st_idx.turn(2, 0) + 1)
            act.activation(ki[:], ps[:, 2, :], ACT.Copy).then_inc(bank_free[2], 1)
            for s in range(3):
                act.wait_ge(bank_free[s], st_idx.turn(s, 0) + 1)
                act.sem_inc(sem("qi_ready"), 1)
            ahead(st_idx, 3, 0)
            act.wait_ge(used[3], st_idx.turn(3, 0) + 1)
            act.activation(fw[0:36, :], ps[0:36, 3, :], ACT.Copy).then_inc(sem("fw_ready"), 1)
            act.wait_ge(sem("fw_ready"), 1)
            act.sem_inc(bank_free[3], 1)
            act.wait_ge(sem("fgate_abs"), 1)
            act.activation(nt[0:HEADS, 1, :], nt[0:HEADS, 1, :], ACT.Exp, scale=-1.0).then_inc(sem("fgate_exp"), 1)
            act.wait_ge(sem("fgate_exp"), 1)
            act.activation(nt[0:HEADS, 1, :], nt[0:HEADS, 1, :], ACT.Ln, bias=ones[0:HEADS, 0:1]
                           ).then_inc(sem("fgate_ln"), 1)

            def relu(n):
                i = n // IDX_HEADS + 1
                if n == 0:
                    act.wait_ge(sem("x_final"), KC)
                act.wait_ge(sem("idx_s"), n + 1)
                if n >= 2:
                    act.wait_ge(sem("idx_acc"), n - 1)
                act.activation(nsq[:, n % 2, 0:(i + 1) * P], ps[:, SA + n % 2, 0:(i + 1) * P], ACT.Relu,
                               scale=HD ** -0.5).then_inc(sem("relu_ready"), 1)

            def va_evac(g):
                act.wait_ge(used[0], st_att.turn(0, g) + 1)
                wait(act, sem("va_turned"), g)
                act.activation(va[:], ps[:, 0, :], ACT.Copy).then_inc(sem("va_ready"), 1)
                act.wait_ge(sem("va_ready"), g + 1)
                act.sem_inc(bank_free[0], 1)
            def qk_evac(s, g):
                act.wait_ge(used[s], st_att.turn(s, g) + 1)
                wait(act, sem("att_s"), 8 * g)
                act.activation((qa, ka)[s - 1][:], ps[:, s, :], ACT.Copy).then_inc(sem("att_qk"), 1)
                act.wait_ge(sem("att_qk"), 2 * g + s)
                act.sem_inc(bank_free[s], 1)
            def vatok_evac(g):
                act.wait_ge(sem("va_turned"), g + 1)
                act.activation(vatok[:].rearrange("p a b -> p (a b)"), ps[:, TR, :], ACT.Copy
                               ).then_inc(sem("vatok_ready"), 1)
            def exps(p, a):
                for n in (2 * a, 2 * a + 1):
                    keys = (n // 2 + 1) * P
                    act.wait_ge(sem("att_logit"), 8 * p + n + 1)
                    act.activation(prob[:, n % 2, 0:keys], prob[:, n % 2, 0:keys], ACT.Exp, bias=mneg[:, n:n + 1],
                                   scale=-1.0, accum_out=rowsum[:, n:n + 1]).then_inc(sem("att_exp"), 1)
            def y_evac(p):
                act.wait_ge(sem("att_o"), NT * p + NT)
                act.activation(y_hi[:, ds(p, 1), :], ps[:, OU:OU + 1, :], ACT.Copy).then_inc(sem("att_hi"), 1)

            n = 0
            for s in range(3):
                ahead(st_att, s, 0)
                for _ in range(4):
                    relu(n)
                    n += 1
                if s == 0:
                    va_evac(0)
                else:
                    qk_evac(s, 0)
            for h in range(HEADS):
                act.wait_ge(sem("ftab_s"), h + 1)
                if h == 0:
                    act.wait_ge(sem("btab_s"), HEADS)
                act.activation(ftab[:, h, :], ps[:, SA + h % 2, :], ACT.Copy).then_inc(sem("ftab_ready"), 1)
            vatok_evac(0)

            def att_group(g):
                p = g - 1
                ahead(st_att, 0, g)
                exps(p, 0)
                va_evac(g)
                exps(p, 1)
                ahead(st_att, 1, g)
                exps(p, 2)
                exps(p, 3)
                ahead(st_att, 2, g)
                qk_evac(1, g)
                y_evac_late = p
                qk_evac(2, g)
                y_evac(y_evac_late)
                vatok_evac(g)

            with act.Fori(1, NQ) as g:
                att_group(g)
            att_group(NQ)
            with act.Fori(NQ + 1, 2 * NQ) as g:
                att_group(g)

            def gate(s, m):
                act.wait_ge(used[s], st_bra.turn(s, m) + 1)
                wait(act, sem("merged"), m)
                act.activation(nsq[:, s, :], ps[:, s, :], ACT.Sigmoid).then_inc(sem("gate_ready"), 1)
                act.wait_ge(sem("gate_ready"), 2 * m + s + 1)
                act.sem_inc(bank_free[s], 1)
            def m_round(m):
                act.wait_ge(sem("merged"), m + 1)
                act.activation(m_hi[:, ds(m, 1), :], nt[:, 2:3, :], ACT.Copy).then_inc(sem("m_hi"), 1)

            p = 2 * NQ - 1
            exps(p, 0)
            ahead(st_bra, 0, 0)
            exps(p, 1)
            exps(p, 2)
            ahead(st_bra, 1, 0)
            exps(p, 3)
            y_evac(p)
            gate(0, 0)
            gate(1, 0)
            ahead(st_bra, 2, 0)
            m_round(0)
            with act.Fori(1, KC) as m:
                ahead(st_bra, 0, m)
                gate(0, m)
                ahead(st_bra, 1, m)
                gate(1, m)
                ahead(st_bra, 2, m)
                m_round(m)
            with act.Fori(0, KC // 4) as i:
                for s in range(4):
                    ahead(st_out2, s, i)
                    square("n4", i * 4 + s, "x_mixed2", 0, s)
            norm("n4", shift=3 * KC)
            mlp(st_mlp2, "mlp2", "n5")
            act.wait_ge(sem("norm_sum"), NORMS.index("n5") + 1)
            act.activation(rootc[:], ps[:, 3, 0:NT], ACT.Sqrt, bias=epsc[:, 0:1], scale=1.0 / D
                           ).then_inc(sem("norm_root"), 1)
            act.wait_ge(sem("norm_rinv"), ROOTED.index("n5") + 1)
            for i in range(NT):
                act.wait_ge(sem("o_second"), i + 1)
                act.activation(otok[:, i, T:D], ps[:, i, :], ACT.Copy, scale=rootc[:, i:i + 1]
                               ).then_inc(sem("otok1"), 1)

        @block.vector
        def _(dve):
            def clear_total(name):
                dve.memset(nt[:, 2, :], 0.0).then_inc(sem("total"), 1)
                if name == "n3":
                    dve.memset(nt[:, 1, :], 0.0).then_inc(sem("total_f"), 1)

            def add_square(name, m, n=None):
                n = m if n is None else n
                dve.wait_ge(sem("norm_sq"), before(name) + m + 1)
                dve.wait_ge(sem("total"), before(name) - KC + m + 1)
                sq = nsq[:, n % 2, :]
                if name == "n3":
                    dve.wait_ge(sem("total_f"), m + 1)
                    dve.tensor_tensor(nt[:, 1, :], nt[:, 1, :], sq, ALU.add).then_inc(sem("total_f"), 1)
                    dve.scalar_tensor_tensor(nt[:, 2, :], sq, gsq[:, m:m + 1], nt[:, 2, :], ALU.mult, ALU.add
                                             ).then_inc(sem("total"), 1)
                else:
                    dve.tensor_tensor(nt[:, 2, :], nt[:, 2, :], sq, ALU.add).then_inc(sem("total"), 1)

            def norm(name, gain, dst=True, shift=None):
                if name == "n3":
                    dve.wait_ge(sem("sum_f"), 1)
                    dve.tensor_scalar(nrs[:], ps[:, TR, :], EPS / D, EPS * EPS, ALU.mult, ALU.add
                                      ).then_inc(sem("both_sums"), 1)
                    dve.wait_ge(sem("both_sums"), 1)
                    dve.wait_ge(sem("norm_sum"), NORMS.index(name) + 1)
                    dve.scalar_tensor_tensor(nrs[:], ps[:, SA, :], 1.0 / D, nrs[:], ALU.mult, ALU.add
                                             ).then_inc(sem("both_sums"), 1)
                dve.wait_ge(sem("norm_root"), ROOTED.index(name) + 1)
                dve.reciprocal(nrs[:], nrs[:]).then_inc(sem("norm_rinv"), 1)
                dve.wait_ge(sem("norm_rinv"), ROOTED.index(name) + 1)

                def lo(m):
                    dve.wait_ge(sem("norm_hi"), before(name) + m + 1)
                    if shift is None:
                        dve.tensor_tensor(u_lo[:, m, :], nt[:, m % 3, :], u_hi[:, m, :], ALU.subtract
                                          ).then_inc(sem("norm_u"), 1)
                    else:
                        dve.scalar_tensor_tensor(u_lo[:, m, :], nt[:, m % 3, :], ada[:, shift + m:shift + m + 1],
                                                 u_hi[:, m, :], ALU.add, ALU.subtract).then_inc(sem("norm_u"), 1)

                for m in range(KC):
                    if not dst:
                        dve.scalar_tensor_tensor(xres[:, m, :], xres[:, m, :], gain(m), nrs[:], ALU.mult, ALU.mult
                                                 ).then_inc(sem("norm_u"), 1)
                        continue
                    if m >= 3:
                        dve.wait_ge(sem("norm_u"), before(name) + m - 2)
                    dve.scalar_tensor_tensor(nt[:, m % 3, :], xres[:, m, :], gain(m), nrs[:], ALU.mult, ALU.mult
                                             ).then_inc(sem("norm_t"), 1)
                    if m >= 1:
                        lo(m - 1)
                if dst:
                    lo(KC - 1)

            def col(name):
                return lambda m: vec[:, VAT[name] + m:VAT[name] + m + 1]

            for s in range(SLOTS):
                dve.sem_inc(bank_free[s], 1)
            for b in range(2):
                dve.sem_inc(sem(f"ada_used{b}"), 1)
            dve.sem_inc(sem("acc_done"), 1)
            dve.wait_ge(sem("small_in"), 16)
            dve.tensor_copy(identb[:], ident).then_inc(sem("masks"), 1)
            dve.tensor_copy(causalb[:], small[:, TAT["causal"]:TAT["causal"] + P]).then_inc(sem("masks"), 1)
            dve.memset(prod[:, 0:2], 0.0).then_inc(sem("prod_zero"), 1)
            for m in range(KC):
                dve.wait_ge(sem("x_turned"), m + 1)
                dve.wait_ge(sem("norm_sq"), m + 1)
                dve.tensor_copy(xres[:, m, :], ps[:, m, :]).then_inc(sem("x_ready"), 1)
            dve.wait_ge(sem("vec_turned"), 1)
            dve.tensor_copy(vec[:], ps[:, 1, 0:NVEC]).then_inc(sem("vec_ready"), 1)
            dve.wait_ge(sem("vec_ready"), 1)
            dve.wait_ge(sem("x_ready"), KC)
            norm("n1", col("norm1_g"))
            dve.wait_ge(sem("rope_in"), 16)
            dve.wait_ge(sem("decay_in"), 16)

            def rotate(s, j, dst):
                dve.wait_ge(used[s], st_ret.turn(s, j) + 1)
                h = P // 2
                dve.wait_ge(sem("rotated"), 2 * j + s - 1) if not (isinstance(j, int) and 2 * j + s - 1 <= 0) else None
                dve.tensor_tensor(nt[0:h, 2, :], ps[h:P, s, :], sinr[h:P, :], ALU.mult).then_inc(sem("swapped"), 1)
                dve.tensor_tensor(nt[h:P, 2, :], ps[0:h, s, :], sinr[0:h, :], ALU.mult).then_inc(sem("swapped"), 1)
                dve.tensor_tensor(dst[:], ps[:, s, :], cosr, ALU.mult).then_inc(bank_free[s], 1)
                dve.wait_ge(sem("swapped"), 4 * j + 2 * s)
                dve.wait_ge(bank_free[s], st_ret.turn(s, j) + 1)
                dve.tensor_tensor(dst[:], dst[:], nt[:, 2, :], ALU.add).then_inc(sem("rotated"), 1)
                dve.wait_ge(sem("rotated"), 2 * j + s)
                dve.sem_inc(sem("qk_ready"), 1)

            def ret_decay(p):
                for b in range(NT):
                    dve.wait_ge(sem("ret_s"), NT * p + b + 1)
                    n = T - b * P
                    dve.tensor_tensor(sdec[:, b:b + 1, 0:n], ps[:, SA + b % 2:SA + b % 2 + 1, 0:n],
                                      decay[:, ds(p, 1), 0:n], ALU.mult).then_inc(sem("sdec_ready"), 1)

            def ret_norm(p):
                dve.wait_ge(sem("ret_root"), p + 1)
                dve.reciprocal(nrs[:], nrs[:]).then_inc(sem("ret_rinv"), 1)
                dve.wait_ge(sem("ret_rinv"), p + 1)
                dve.wait_ge(sem("osb_ready"), p + 1)
                dve.scalar_tensor_tensor(nt[:, 0, :], osb[:], vec[:, ds(VAT["ret_norm_g"] + p, 1)], nrs[:],
                                         ALU.mult, ALU.mult).then_inc(sem("ret_t"), 1)
                dve.wait_ge(sem("ret_t"), p + 1)
                dve.wait_ge(sem("silu_ready"), p + 1)
                dve.tensor_tensor(nt[:, 1, :], nt[:, 0, :], silu[:], ALU.mult).then_inc(sem("ret_y"), 1)

            def ret_lo(p):
                dve.wait_ge(sem("ret_hi"), p + 1)
                dve.tensor_tensor(y_lo[:, ds(NQ + p, 1), :], nt[:, 1:2, :], y_hi[:, ds(NQ + p, 1), :], ALU.subtract
                                  ).then_inc(sem("yret_ready"), 1)

            def silus(j):
                dve.wait_ge(sem("sg_ready"), j + 1)
                wait(dve, sem("ret_y"), j)
                dve.tensor_tensor(silu[:], ps[:, 3, :], sg[:], ALU.mult).then_inc(sem("silu_ready"), 1)
                dve.wait_ge(sem("silu_ready"), j + 1)
                dve.sem_inc(bank_free[3], 1)

            rotate(1, 0, qf)
            rotate(2, 0, kf)
            silus(0)
            dve.wait_ge(sem("brow_out"), 16)
            dve.memset(acc[:], 0.0).then_inc(sem("acc_zero"), 1)
            with dve.Fori(1, NQ) as j:
                ret_decay(j - 1)
                rotate(1, j, qf)
                rotate(2, j, kf)
                ret_norm(j - 1)
                silus(j)
                ret_lo(j - 1)

            def conv(j):
                dve.wait_ge(used[1], st_conv.turn(1, j) + 1)
                dve.wait_ge(bank_free[0], st_conv.turn(0, j) + 1)
                wait(dve, sem("conv_y3"), j)
                dve.tensor_tensor(prod[:, 2:T + 2], ps[:, 1, :], ccs[:], ALU.mult).then_inc(sem("prod_ready"), 1)
                dve.wait_ge(sem("prod_ready"), j + 1)
                dve.sem_inc(bank_free[1], 1)
                taps = [vec[:, ds(VAT["conv_w"] + t * NQ + j, 1)] for t in range(3)]
                wait(dve, sem("conv_t"), j)
                dve.tensor_scalar(ycv[:], prod[:, 2:T + 2], taps[2], None, ALU.mult).then_inc(sem("conv_y1"), 1)
                dve.wait_ge(sem("conv_y1"), j + 1)
                dve.scalar_tensor_tensor(ycv[:], prod[:, 1:T + 1], taps[1], ycv[:], ALU.mult, ALU.add
                                         ).then_inc(sem("conv_y2"), 1)
                dve.wait_ge(sem("conv_y2"), j + 1)
                dve.scalar_tensor_tensor(ycv[:], prod[:, 0:T], taps[0], ycv[:], ALU.mult, ALU.add
                                         ).then_inc(sem("conv_y3"), 1)
                dve.wait_ge(sem("conv_y3"), j + 1)
                dve.wait_ge(used[2], st_conv.turn(2, j) + 1)
                dve.tensor_tensor(ycv[:], ps[:, 2, :], ycv[:], ALU.mult).then_inc(sem("ycv_done"), 1)
                dve.wait_ge(sem("ycv_done"), j + 1)
                dve.sem_inc(bank_free[2], 1)

            def conv_norm(p):
                dve.wait_ge(sem("conv_root"), p + 1)
                dve.reciprocal(sg[:], sg[:]).then_inc(sem("conv_rinv"), 1)
                dve.wait_ge(sem("conv_rinv"), p + 1)
                dve.scalar_tensor_tensor(nt[:, 0, :], ycv[:], vec[:, ds(VAT["conv_norm_g"] + p, 1)], sg[:],
                                         ALU.mult, ALU.mult).then_inc(sem("conv_t"), 1)
                dve.wait_ge(sem("conv_hi"), p + 1)
                dve.tensor_tensor(y_lo[:, ds(p, 1), :], nt[:, 0:1, :], y_hi[:, ds(p, 1), :], ALU.subtract
                                  ).then_inc(sem("ycv_ready"), 1)

            ret_decay(NQ - 1)
            ret_norm(NQ - 1)
            ret_lo(NQ - 1)
            dve.wait_ge(sem("prod_zero"), 1)
            conv(0)
            with dve.Fori(1, NQ) as j:
                conv_norm(j - 1)
                conv(j)
            conv_norm(NQ - 1)
            dve.wait_ge(sem("ycv_ready"), NQ)
            dve.sem_inc(sem("mix_done"), 1)

            def add(st, n, s, i, m, scale, done):
                dve.wait_ge(used[s], st.turn(s, n) + 1)
                dve.wait_ge(bank_free[s], st.turn(s, n))
                dve.scalar_tensor_tensor(xres[:, ds(m, 1), :], ps[:, s:s + 1, :], scale, xres[:, ds(m, 1), :],
                                         ALU.mult, ALU.add).then_inc(sem(done), 1)
                dve.wait_ge(sem(done), i + 1)
                dve.sem_inc(bank_free[s], 1)

            def wout(st, scale, done, next_norm, gained=False):
                clear_total(next_norm)
                for i in range(KC // 4):
                    for s in range(4):
                        m = i * 4 + s
                        add(st, i, s, m, m, scale(m), done)
                        if gained:
                            dve.wait_ge(sem("norm_hi"), before("n2") + m + 1)
                            dve.scalar_tensor_tensor(u_lo[:, m, :], xres[:, m, :], col("norm2_g")(m), u_hi[:, m, :],
                                                     ALU.mult, ALU.subtract).then_inc(sem("norm_u"), 1)
                        if i * 4 + s < KC - 1:
                            add_square(next_norm, i * 4 + s)

            wout(st_out, lambda m: 1.0, "x_mixed", "n2", gained=True)

            def ada_piece(q, d, i, b):
                n = q * 4 + 2 * d + i
                dve.wait_ge(sem(f"ada_in{b}"), 16 * (n + 1))
                dve.wait_ge(sem("acc_done"), 2 * n + b + 1)
                a = acc[:, ds(i * 3 * D + b * 3 * D // 2, 3 * D // 2)]
                dve.scalar_tensor_tensor(a, adaw[:, b, :], vec[:, ds(VAT["c_2"] + 2 * q + d, 1)], a,
                                         ALU.mult, ALU.add).then_inc(sem("acc_done"), 1)
                dve.wait_ge(sem("acc_done"), 2 * n + b + 2)
                dve.sem_inc(sem(f"ada_used{b}"), 1)

            def mlp(st, name, scale, with_ada, next_norm, factor=None):
                def up(q):
                    with dve.Fori(0, 2) as i:
                        for s in range(4):
                            if factor is not None and s == 0:
                                wait(dve, sem("mlp_x"), q * KC + mlp_before(name))
                            dve.wait_ge(bank_free[s], st.turn(s, q * 4 + i) + 1)
                            dve.tensor_tensor(nt[:, s % 2, :], nsq[:, s % 2, :], nsq[:, s % 2, :], ALU.mult
                                              ).then_inc(sem("mlp_sq"), 1)
                            dve.wait_ge(sem("mlp_sq"), q * KC + i * 4 + (mlp_before(name) + s + 1))
                            dve.wait_ge(sem("mlp_hi"), q * KC + i * 4 + (mlp_before(name) + s + 1))
                            m = ds(i * 4 + s, 1)
                            dve.tensor_tensor(y_lo[:, m, :], nt[:, s % 2:s % 2 + 1, :], y_hi[:, m, :], ALU.subtract
                                              ).then_inc(sem("mlp_h"), 1)
                            dve.wait_ge(sem("mlp_h"), q * KC + i * 4 + (mlp_before(name) + s + 1))
                            if with_ada and s % 2:
                                ada_piece(q, 0, i, s // 2)

                def down(q, i, last=False):
                    for s in range(4):
                        if with_ada and s % 2:
                            ada_piece(q, 1, i, s // 2)
                        n, m = q * KC + i * 4 + (mlp_before(name) + s), i * 4 + s
                        if factor is None:
                            add(st, q * 4 + 2 + i, s, n, m, scale(m), "mlp_x")
                        else:
                            dve.wait_ge(used[s], st.turn(s, q * 4 + 2 + i) + 1)
                            wait(dve, sem("mlp_x"), n)
                            dve.tensor_tensor(nt[:, 0, :], ps[:, s, :], factor[:], ALU.mult
                                              ).then_inc(bank_free[s], 1)
                            dve.wait_ge(bank_free[s], st.turn(s, q * 4 + 2 + i) + 1)
                            dve.tensor_tensor(xres[:, ds(m, 1), :], nt[:, 0:1, :], xres[:, ds(m, 1), :], ALU.add
                                              ).then_inc(sem("mlp_x"), 1)
                        if last and i * 4 + s < KC - 1:
                            add_square(next_norm, i * 4 + s)

                if factor is None:
                    first = 0
                else:
                    first = 1
                    up(0)
                    dve.wait_ge(sem("norm_sum"), NORMS.index("n2") + 1)
                    dve.tensor_scalar(factor[:], ps[:, SA, :], 1.0 / D, EPS, ALU.mult, ALU.add
                                      ).then_inc(sem("mean_sq"), 1)
                    dve.wait_ge(sem("mean_sq"), 1)
                    dve.reciprocal(factor[:], factor[:]).then_inc(sem("factor"), 1)
                    dve.wait_ge(sem("factor"), 1)
                    with dve.Fori(0, 2) as i:
                        down(0, i)
                with dve.Fori(first, NF - 1) as q:
                    up(q)
                    with dve.Fori(0, 2) as i:
                        down(q, i)
                up(NF - 1)
                clear_total(next_norm)
                for i in range(2):
                    down(NF - 1, i, True)

            dve.wait_ge(sem("acc_zero"), 1)
            dve.tensor_tensor(gsq[:], vec[:, VAT["final_norm_g"]:VAT["final_norm_g"] + KC],
                              vec[:, VAT["final_norm_g"]:VAT["final_norm_g"] + KC], ALU.mult).then_inc(sem("gsq"), 1)
            dve.wait_ge(sem("gsq"), 1)
            dve.tensor_scalar(gones[:], ones[:], gsq[:, KC - 1:KC], None, ALU.mult).then_inc(sem("gones"), 1)
            mlp(st_mlp, "mlp", None, True, "n3", factor=nrs)
            dve.wait_ge(sem("ada_sum"), 1)
            dve.tensor_tensor(ada[:], ps[:, SB, 0:6 * KC], vec[:, VAT["b_ada_2"]:VAT["b_ada_2"] + 6 * KC], ALU.add
                              ).then_inc(sem("ada_ready"), 1)
            dve.wait_ge(sem("ada_ready"), 1)
            dve.scalar_tensor_tensor(gain1[:], ada[:, KC:2 * KC], 1.0, vec[:, VAT["g_norm1_2"]:VAT["g_norm1_2"] + KC],
                                     ALU.add, ALU.mult).then_inc(sem("gains"), 1)
            dve.scalar_tensor_tensor(gain2[:], ada[:, 4 * KC:5 * KC], 1.0,
                                     vec[:, VAT["g_norm2_2"]:VAT["g_norm2_2"] + KC], ALU.add, ALU.mult
                                     ).then_inc(sem("gains"), 1)
            dve.wait_ge(sem("gains"), 2)
            dve.tensor_tensor(gain1[:], gain1[:], vec[:, VAT["final_norm_g"]:VAT["final_norm_g"] + KC], ALU.mult
                              ).then_inc(sem("gains"), 1)
            dve.wait_ge(sem("gains"), 3)
            norm("n3", lambda m: gain1[:, m:m + 1], shift=0)
            dve.wait_ge(sem("root_f"), 1)
            dve.reciprocal(nsq[:, 0, :], nsq[:, 0, :]).then_inc(sem("rinv_f"), 1)
            dve.wait_ge(sem("rinv_f"), 1)
            for m in range(KC):
                g = VAT["final_norm_g"] + m
                dve.scalar_tensor_tensor(xres[:, m, :], xres[:, m, :], vec[:, g:g + 1], nsq[:, 0, :],
                                         ALU.mult, ALU.mult).then_inc(sem("x_final"), 1)

            dve.wait_ge(sem("bfor_in"), 16)
            dve.wait_ge(sem("masks"), 2)
            dve.tensor_copy(sel[:, 0, 0:P], causalb[:]).then_inc(sem("sel_ready"), 1)
            for h in range(HEADS):
                dve.wait_ge(sem("btab_s"), h + 1)
                dve.tensor_copy(btab[:, h, :], ps[:, SA + h % 2, :]).then_inc(sem("btab_ready"), 1)
            dve.wait_ge(sem("fw_ready"), 1)
            dve.wait_ge(sem("norm_u"), before("n3") + KC)
            f = fw[0:HEADS, :]
            dve.tensor_scalar(nt[0:HEADS, 1, :], f, bfor[:, 0:1], None, ALU.add).then_inc(sem("fgate_z"), 1)
            dve.tensor_scalar(nt[0:HEADS, 2, :], f, bfor[:, 0:1], 0.0, ALU.add, ALU.min).then_inc(sem("fgate_z"), 1)
            dve.wait_ge(sem("fgate_z"), 2)
            dve.scalar_tensor_tensor(nt[0:HEADS, 1, :], nt[0:HEADS, 2, :], -2.0, nt[0:HEADS, 1, :],
                                     ALU.mult, ALU.add).then_inc(sem("fgate_abs"), 1)
            dve.memset(nrs[0:HEADS, :], 1.0).then_inc(sem("fgate_one"), 1)
            dve.wait_ge(sem("wi_turned"), 1)
            for i in range(NT):
                last = dve.tensor_scalar(wtok[:, IDX_HEADS * i:IDX_HEADS * (i + 1)],
                                         ps[:, TR, i * 64 + 32:i * 64 + 32 + IDX_HEADS], IDX_HEADS ** -0.5, None, ALU.mult)
            last.then_inc(sem("wtok_ready"), 1)
            dve.wait_ge(sem("fgate_ln"), 1)
            dve.tensor_tensor(nt[0:HEADS, 2, :], nt[0:HEADS, 2, :], nt[0:HEADS, 1, :], ALU.subtract
                              ).then_inc(sem("fgate_log"), 1)
            dve.wait_ge(sem("fgate_log"), 1)
            dve.wait_ge(sem("fgate_one"), 1)
            dve.tensor_tensor_scan(nt[0:HEADS, 0, :], nrs[0:HEADS, :], nt[0:HEADS, 2, :], 0.0, ALU.mult, ALU.add
                                   ).then_inc(sem("fcum_ready"), 1)
            dve.wait_ge(sem("wtok_ready"), 1)
            for n in range(IDX_HEADS * (NT - 1)):
                i, h = n // IDX_HEADS + 1, n % IDX_HEADS
                keys = (i + 1) * P
                w = wtok[:, IDX_HEADS * i + h:IDX_HEADS * i + h + 1]
                dve.wait_ge(sem("relu_ready"), n + 1)
                wk = work[:, i - 1, 0:keys]
                if h == 0:
                    dve.tensor_scalar(wk, nsq[:, n % 2, 0:keys], w, 0.0, ALU.mult, ALU.add).then_inc(sem("idx_acc"), 1)
                else:
                    dve.wait_ge(sem("idx_acc"), n)
                    dve.scalar_tensor_tensor(wk, nsq[:, n % 2, 0:keys], w, wk, ALU.mult, ALU.add
                                             ).then_inc(sem("idx_acc"), 1)
                if h == IDX_HEADS - 1:
                    dve.wait_ge(sem("idx_acc"), n + 1)
                    d = work[:, i - 1, keys - P:keys]
                    dve.tensor_tensor(d, d, causalb[:], ALU.add).then_inc(sem("iscore"), 1)

            def logits(p, n, tab_at):
                keys = (n // 2 + 1) * P
                dve.wait_ge(sem("att_s"), 8 * p + n + 1)
                if n >= 2:
                    dve.wait_ge(sem("att_t"), 8 * p + n - 1)
                else:
                    wait(dve, sem("att_t"), 8 * p)
                dve.tensor_tensor_reduce(prob[:, n % 2, 0:keys], ps[:, SA + n % 2, 0:keys],
                                         tab_at(p, n % 2, keys), -(HD ** -0.5), -MASKED, ALU.add, ALU.min,
                                         mneg[:, n:n + 1]).then_inc(sem("att_logit"), 1)
            def weights(p, n):
                keys = (n // 2 + 1) * P
                dve.wait_ge(sem("att_exp"), 8 * p + n + 1)
                dve.reciprocal(rinv[:, n:n + 1], rowsum[:, n:n + 1]).then_inc(sem("att_rinv"), 1)
                dve.wait_ge(sem("att_rinv"), 8 * p + n + 1)
                dve.tensor_scalar(prob[:, n % 2, 0:keys], prob[:, n % 2, 0:keys], rinv[:, n:n + 1], None, ALU.mult
                                  ).then_inc(sem("att_prob"), 1)
            def turned(p, n):
                i, keys = n // 2, (n // 2 + 1) * P
                dve.wait_ge(sem("att_t"), 8 * p + n + 1)
                if n % 2 == 0:
                    wait(dve, sem("att_o"), NT * p + i - 1)
                dve.tensor_copy(probt[:, 2 * (i % 2) + n % 2, 0:keys], ps[:, TURNS[n % 2], 0:keys]
                                ).then_inc(sem("att_probt"), 1)
            def y_lows(p):
                dve.wait_ge(sem("att_hi"), p + 1)
                dve.tensor_tensor(y_lo[:, ds(p, 1), :], ps[:, OU:OU + 1, :], y_hi[:, ds(p, 1), :], ALU.subtract
                                  ).then_inc(sem("att_y"), 1)
            def fox_tab(p, hh, keys):
                return ftab[:, 2 * p + hh, 0:keys]
            def dsa_tab(p, hh, keys):
                return btab[:, 2 * (p - NQ) + hh, T - keys:T]

            plan = selection_plan(4 * NQ)

            def rounds(part):
                for i, n in plan[part]:
                    wk = work[:, i - 1, 0:(i + 1) * P]
                    dve.max(top8[:], wk).then_inc(sem("top8"), 1)
                    dve.wait_ge(sem("top8"), (TOPK // 8) * (i - 1) + n + 1)
                    dve.match_replace(wk, top8[:], wk, TAKEN).then_inc(sem("taken"), 1)
                    dve.wait_ge(sem("taken"), (TOPK // 8) * (i - 1) + n + 1)
                    if n == TOPK // 8 - 1:
                        dve.tensor_scalar(sel[:, i, 0:(i + 1) * P], wk, 0.5 * (MASKED + TAKEN), MASKED,
                                          ALU.is_gt, ALU.mult).then_inc(sem("sel_ready"), 1)

            def att(p, tab_at, select=False):
                for a in range(4):
                    if a > 0:
                        turned(p, 2 * a - 2)
                    logits(p, 2 * a, tab_at)
                    if a > 0:
                        turned(p, 2 * a - 1)
                    logits(p, 2 * a + 1, tab_at)
                    weights(p, 2 * a)
                    weights(p, 2 * a + 1)
                    if select:
                        rounds(4 * p + a)
                turned(p, 6)
                turned(p, 7)
                y_lows(p)

            dve.wait_ge(sem("iscore"), NT - 1)
            for p in range(NQ):
                att(p, fox_tab, True)
            for p in range(NQ, 2 * NQ):
                att(p, dsa_tab)

            def merge_branches(m):
                dve.wait_ge(used[2], st_bra.turn(2, m) + 1)
                dve.wait_ge(sem("gate_ready"), 2 * m + 2)
                dve.tensor_tensor(nt[:, 0, :], ps[:, 2, :], nsq[:, 0, :], ALU.mult).then_inc(sem("gated"), 1)
                dve.tensor_tensor(nt[:, 1, :], ps[:, SA, :], nsq[:, 1, :], ALU.mult).then_inc(sem("gated"), 1)
                dve.wait_ge(sem("gated"), 2 * m + 2)
                dve.sem_inc(bank_free[2], 1)
                dve.tensor_tensor(nt[:, 2, :], nt[:, 0, :], nt[:, 1, :], ALU.add).then_inc(sem("merged"), 1)
                dve.wait_ge(sem("m_hi"), m + 1)
                dve.tensor_tensor(m_lo[:, ds(m, 1), :], nt[:, 2:3, :], m_hi[:, ds(m, 1), :], ALU.subtract
                                  ).then_inc(sem("m_ready"), 1)

            with dve.Fori(0, KC) as m:
                merge_branches(m)
            dve.wait_ge(sem("m_ready"), KC)
            wout(st_out2, lambda m: ada[:, ds(2 * KC + m, 1)], "x_mixed2", "n4")
            norm("n4", lambda m: gain2[:, m:m + 1], shift=3 * KC)
            mlp(st_mlp2, "mlp2", lambda m: ada[:, ds(5 * KC + m, 1)], False, "n5")
            dve.wait_ge(sem("norm_root"), ROOTED.index("n5") + 1)
            dve.reciprocal(rootc[:], rootc[:]).then_inc(sem("norm_rinv"), 1)
            dve.wait_ge(sem("norm_rinv"), ROOTED.index("n5") + 1)
            dve.wait_ge(sem("o_first"), 1)
            for i in range(NT):
                dve.tensor_scalar(otok[:, i, 0:T], ps[:, 4 + i, :], rootc[:, i:i + 1], None, ALU.mult
                                  ).then_inc(sem("otok0"), 1)
    return nc


_INS = ["x", "norm1_g", "w_in", "conv_w", "conv_norm_g", "ret_norm_g", "w_out", "norm2_g", "w_up", "w_down",
        "final_norm_g", "c_2", "w_ada_2", "b_ada_2", "g_norm1_2", "w_in_2", "b_forget_2", "rel_bias_2",
        "w_branch_fox_2", "w_branch_dsa_2", "w_out_2", "g_norm2_2", "w_mlp1_2", "w_mlp2_2", "g_final_2"]


def kernel(**inputs):
    import concourse.bacc as bacc
    from concourse.bass_utils import run_bass_kernel_spmd

    nc = bacc.Bacc("TRN2", target_bir_lowering=False, num_devices=1)
    arrays = {"tab": tables()}
    for name in _INS:
        arrays[name] = np.ascontiguousarray(inputs[name])
    args = {n: nc.dram_tensor(n, a.shape, mybir.dt.from_np(a.dtype), kind="ExternalInput").ap()
            for n, a in arrays.items()}
    args["out"] = nc.dram_tensor("out", (1, T, D), F32, kind="ExternalOutput").ap()
    build(nc, **args)
    r = run_bass_kernel_spmd(nc, [arrays], core_ids=[0])
    return r.results[0]["out"]
```

```python
from contextlib import ExitStack

import concourse.bass as bass
import numpy as np
from concourse import mybir

F32 = mybir.dt.float32
F32R = mybir.dt.float32r
BF16 = mybir.dt.bfloat16
ALU = mybir.AluOpType
ACT = mybir.ActivationFunctionType

P = 128
T = 512
NT = T // P
D = 1024
KC = D // P
QW = D // 2
NQ = QW // P
DFF = 4 * D
NF = DFF // D
HEADS = 8
HD = 64
IDX_HEADS = 4
TOPK = min(256, T // 4)
EPS = 1e-6
SLOTS = 4
AHEAD = 2
BUCKETS = 32
NREL = T + P
MASKED = -3.0e38
TAKEN = -3.4e38

SA, SB, TR, OU = 4, 5, 6, 7
TURNS = (TR, 3)

W1_CB, W1_CC, W1_CH, W1_RQ, W1_RK, W1_RV, W1_RG = [n * QW for n in range(7)]
SPLITS = [QW] * 3 + [HEADS] + [QW] * 3 + [IDX_HEADS * HD, HD, IDX_HEADS, D, D]
(W2_FQ, W2_FK, W2_FV, W2_F, W2_DQ, W2_DK, W2_DV, W2_QI, W2_KI, W2_WI, W2_GF, W2_GD) = [
    sum(SPLITS[:n]) for n in range(12)]

VECS = [("norm1_g", KC), ("conv_w", 3 * NQ), ("conv_norm_g", NQ), ("ret_norm_g", NQ), ("norm2_g", KC),
        ("final_norm_g", KC), ("c_2", KC), ("g_norm1_2", KC), ("g_norm2_2", KC), ("g_final_2", KC),
        ("b_ada_2", 6 * KC)]
VAT = {}
_n = 0
for _name, _rows in VECS:
    VAT[_name] = _n
    _n += _rows
NVEC = _n

NORMS = ["n1", "n2", "n3", "n4", "n5"]
INVERTED = ["n1", "n3", "n5"]
SHIFTED = ["n3", "n4"]
ROOTED = ["n1", "n3", "n4", "n5"]
MLPS = ["mlp", "mlp2"]

TABS = [("ident", P), ("group64", P), ("causal", P), ("onehot", NREL),
        ("cos", T), ("sin", T), ("decay", NQ * T)]
TAT = {}
_n = 0
for _name, _cols in TABS:
    TAT[_name] = _n
    _n += _cols
NTAB = _n
SMALL = TAT["onehot"]


def tables():
    t = np.zeros((P, NTAB), np.float32)
    r = np.arange(P)
    t[:, TAT["ident"]:][:, :P] = np.eye(P)
    t[:, TAT["group64"]:][:, :P] = (r[:, None] // HD) == (r[None, :] // HD)
    t[:, TAT["causal"]:][:, :P] = np.where(r[None, :] <= r[:, None], 0.0, MASKED)
    n = np.maximum(T - 1 - np.arange(NREL), 0)
    large = 16 + (np.log(np.maximum(n, 1) / 16.0) / np.log(8.0) * 16).astype(np.int64)
    bucket = np.where(n < 16, n, np.minimum(large, BUCKETS - 1))
    t[:BUCKETS, TAT["onehot"]:][:, :NREL] = bucket[None, :] == np.arange(BUCKETS)[:, None]
    half = P // 2
    inv = (1.0 / (np.float32(10000.0) ** (np.arange(half, dtype=np.float32) / half))).astype(np.float32)
    ang = np.arange(T, dtype=np.float32)[None, :] * np.concatenate([inv, inv])[:, None]
    t[:, TAT["cos"]:][:, :T] = np.cos(ang)
    t[:, TAT["sin"]:][:, :T] = np.sin(ang) * np.where(r < half, 1.0, -1.0)[:, None]
    for h in range(NQ):
        gamma = 1.0 - 2.0 ** (-5.0 - h)
        diff = np.arange(T)[None, :] - r[:, None]
        t[:, TAT["decay"] + h * T:][:, :T] = np.where(diff >= 0, gamma ** np.maximum(diff, 0), 0.0) * P ** -0.5
    return t


def selection_plan(shares):
    rounds = [(i, n) for i in range(1, NT) for n in range(TOPK // 8)]
    total = sum(i + 1.5 for i, _ in rounds)
    plan, done, part, upto = [[] for _ in shares], 0.0, 0, shares[0]
    for i, n in rounds:
        while part < len(shares) - 1 and done / total * sum(shares) >= upto:
            part += 1
            upto += shares[part]
        plan[part].append((i, n))
        done += i + 1.5
    return plan


def before(name):
    return KC * NORMS.index(name)


def mlp_before(name):
    return NF * KC * MLPS.index(name)


def wait(eng, sem, n):
    if not isinstance(n, int) or n > 0:
        eng.wait_ge(sem, n)


class Stage:

    def __init__(self, before, n, k, dmas=()):
        self.base = [b + (before.n if before and s < before.k else 0)
                     for s, b in enumerate(before.base if before else [1] * SLOTS)]
        self.raws = [b + (16 * before.n * before.dmas[s] if before and s < before.k else 0)
                     for s, b in enumerate(before.raws if before else [0] * SLOTS)]
        self.n, self.k = n, k
        self.dmas = list(dmas) or [1] * SLOTS

    def turn(self, s, i):
        return self.base[s] + i

    def landed(self, s, i):
        return self.raws[s] + 16 * self.dmas[s] * (i + 1)


def build(nc, tab, x, norm1_g, w_in, conv_w, conv_norm_g, ret_norm_g, w_out, norm2_g, w_up, w_down,
          final_norm_g, c_2, w_ada_2, b_ada_2, g_norm1_2, w_in_2, b_forget_2, rel_bias_2,
          w_branch_fox_2, w_branch_dsa_2, w_out_2, g_norm2_2, w_mlp1_2, w_mlp2_2, g_final_2, out):
    ds = bass.ds
    rows = {"norm1_g": norm1_g, "conv_w": conv_w, "conv_norm_g": conv_norm_g, "ret_norm_g": ret_norm_g,
            "norm2_g": norm2_g, "final_norm_g": final_norm_g, "c_2": c_2, "g_norm1_2": g_norm1_2,
            "g_norm2_2": g_norm2_2, "g_final_2": g_final_2, "b_ada_2": b_ada_2}

    st_ret = Stage(None, NQ, 4)
    st_conv = Stage(st_ret, NQ, 3)
    st_out = Stage(st_conv, KC // 4, 4)
    st_mlp = Stage(st_out, NF * 4, 4)
    st_idx = Stage(st_mlp, 1, 3, [1, 1, 3])
    st_att = Stage(st_idx, 2 * NQ, 3)
    st_bra = Stage(st_att, KC, 3, [1, 1, 2, 1])
    st_out2 = Stage(st_bra, KC // 4, 4)
    st_mlp2 = Stage(st_out2, NF * 4, 4)

    bias_rows = nc.dram_tensor("bias_rows", [HEADS, P, NREL], F32).ap()
    forget_rows = nc.dram_tensor("forget_rows", [HEADS, T], F32).ap()

    ctx = ExitStack()
    with ctx:
        def sb(name, shape, dt=F32, where=ctx):
            return where.enter_context(nc.sbuf_tensor(name, shape, dt))

        sems = {}

        def sem(name):
            if name not in sems:
                sems[name] = ctx.enter_context(nc.semaphore(name))
            return sems[name]

        xres = sb("xres", [P, KC, T])
        u_hi, u_lo = sb("u_hi", [P, KC, T], F32R), sb("u_lo", [P, KC, T], F32R)
        y_hi, y_lo = sb("y_hi", [P, KC, T], F32R), sb("y_lo", [P, KC, T], F32R)
        raw = sb("raw", [P, SLOTS, KC * P])
        w_hi, w_lo = sb("w_hi", [P, SLOTS, KC * P], F32R), sb("w_lo", [P, SLOTS, KC * P], F32R)
        small = sb("small", [P, SMALL])
        ident = small[:, TAT["ident"]:TAT["ident"] + P]
        group64 = small[:, TAT["group64"]:TAT["group64"] + P]
        identb, causalb = sb("identb", [P, P], BF16), sb("causalb", [P, P], BF16)
        ones = sb("ones", [P, P])
        epsc, spare = sb("epsc", [P, 1]), sb("spare", [P, 1])
        vec = sb("vec", [P, NVEC])
        ada = sb("ada", [P, 6 * KC])
        gain1, gain2 = sb("gain1", [P, KC]), sb("gain2", [P, KC])
        gsq = sb("gsq", [P, KC])
        rootc = sb("rootc", [P, NT])
        bfor = sb("bfor", [HEADS, 1])
        rowsum, rinv, mneg = sb("rowsum", [P, 8]), sb("rinv", [P, 8]), sb("mneg", [P, 8])
        wtok = sb("wtok", [P, NT * IDX_HEADS])
        top8 = sb("top8", [P, 8])
        nt = sb("nt", [P, 3, T])
        nsq = sb("nsq", [P, 2, T])
        nrs = sb("nrs", [P, T])

        one = ExitStack()
        decay = sb("decay", [P, NQ, T], where=one)
        rows_made = ExitStack()
        fbrow = sb("fbrow", [HEADS, NREL], where=rows_made)
        rows_made.close()
        start = ExitStack()
        xtok = sb("xtok", [P, NT, D], where=start)
        start.close()
        acc = sb("acc", [P, 6 * D], where=one)
        mix = ExitStack()
        rope = sb("rope", [P, 2, T], where=mix)
        cosr, sinr = rope[:, 0, :], rope[:, 1, :]
        vf, vtok = sb("vf", [P, T], where=mix), sb("vtok", [P, NT, P], where=mix)
        qf, kf = sb("qf", [P, T], where=mix), sb("kf", [P, T], where=mix)
        sdec = sb("sdec", [P, NT, T], where=mix)
        osb, sg, silu = sb("osb", [P, T], where=mix), sb("sg", [P, T], where=mix), sb("silu", [P, T], where=mix)
        prod, ycv = sb("prod", [P, T + 2], where=mix), sb("ycv", [P, T], where=mix)
        r1 = sb("r1", [P, T], where=mix)
        ccs, r1sq = vf, qf
        mix.close()
        adaw = sb("adaw", [P, 2, 6 * D // 4], where=one)
        gones = sb("gones", [P, P], where=one)
        one.close()
        pre = ExitStack()
        vrow = sb("vrow", [NVEC, P], where=pre)
        oneh = sb("oneh", [BUCKETS, NREL], where=pre)
        rbias = sb("rbias", [BUCKETS, HEADS], where=pre)
        pre.close()

        two = ExitStack()
        merge = ExitStack()
        ftab, btab = sb("ftab", [P, HEADS, T], where=merge), sb("btab", [P, HEADS, T], where=merge)
        merge.close()
        m_hi, m_lo = sb("m_hi", [P, KC, T], F32R, where=two), sb("m_lo", [P, KC, T], F32R, where=two)
        qa, ka = sb("qa", [P, T], where=two), sb("ka", [P, T], where=two)
        va, vatok = sb("va", [P, T], where=two), sb("vatok", [P, NT, P], where=two)
        work = sb("work", [P, NT - 1, T], where=two)
        sel = sb("sel", [P, NT, T], BF16, where=two)
        index = ExitStack()
        qi, ki = sb("qi", [P, 2, T], where=index), sb("ki", [P, T], where=index)
        fw = sb("fw", [P, T], where=index)
        index.close()
        prob = sb("prob", [P, 2, T], where=two)
        probt = sb("probt", [P, NT, T], where=two)
        two.close()
        last = ExitStack()
        otok = sb("otok", [P, NT, D], where=last)
        last.close()

        ps = ctx.enter_context(nc.psum_tensor("ps", [P, 8, T], F32))

        raw_ready = [sem(f"raw_ready{s}") for s in range(SLOTS)]
        hi_ready = [sem(f"hi_ready{s}") for s in range(SLOTS)]
        lo_ready = [sem(f"lo_ready{s}") for s in range(SLOTS)]
        used = [sem(f"used{s}") for s in range(SLOTS)]
        bank_free = [sem(f"bank_free{s}") for s in range(SLOTS)]

        block = ctx.enter_context(nc.Block())

        @block.sync
        def _(sp):
            def load(st, s, i, *pairs):
                if st.raws[s] == 0:
                    sp.wait_ge(sem("x_in0"), 16)
                else:
                    sp.wait_ge(raw_ready[s], st.raws[s])
                wait(sp, lo_ready[s], st.turn(s, i))
                dst = raw[:, s, :].rearrange("p (k m) -> p k m", k=KC)
                for cut, src in pairs:
                    sp.dma_start(cut(dst), src).then_inc(raw_ready[s], 16)

            def whole(dst):
                return dst

            def cols(w, at, n=P):
                return w.rearrange("(k p) n -> p k n", p=P)[:, :, ds(at, n)]

            for i in range(NT):
                sp.dma_start(xtok[:, i, :], x[0, i * P:(i + 1) * P, :]).then_inc(sem(f"x_in{i}"), 16)

            def ret_loads(j):
                for s, at in enumerate([W1_RV, W1_RQ, W1_RK, W1_RG]):
                    load(st_ret, s, j, (whole, cols(w_in, at + j * P)))

            def brow_copies(j):
                sp.wait_ge(sem("brow_read"), 2)
                sp.dma_start(bias_rows[:, ds(j * (P // NQ), P // NQ), :],
                             bass.AP(fbrow[:].tensor, fbrow[:].offset, [fbrow[:].ap[0], [0, P // NQ], [1, NREL]])
                             ).then_inc(sem("brow_out"), 16)

            ret_loads(0)
            for name, n in VECS[1:]:
                src = rows[name]
                if name == "conv_w":
                    src = src.rearrange("t (j p) -> (t j) p", p=P)
                elif name == "c_2":
                    src = src.rearrange("a (j p) -> (a j) p", p=P)
                else:
                    src = src.rearrange("(j p) -> j p", p=P)
                sp.dma_start(vrow[VAT[name]:VAT[name] + n, :], src
                              ).then_inc(sem("vrow_in"), 16)
            sp.dma_start(oneh[:], tab[0:BUCKETS, TAT["onehot"]:TAT["onehot"] + NREL]).then_inc(sem("bias_in"), 16)
            sp.dma_start(rbias[:], rel_bias_2).then_inc(sem("bias_in"), 16)
            sp.dma_start(bfor[:], b_forget_2.rearrange("(h a) -> h a", a=1)).then_inc(sem("bfor_in"), 16)
            sp.dma_start(rope[:], tab[:, TAT["cos"]:TAT["cos"] + 2 * T].rearrange("p (a t) -> p a t", a=2)
                          ).then_inc(sem("rope_in"), 16)
            with sp.Fori(1, NQ) as j:
                ret_loads(j)
                brow_copies(j - 1)
            brow_copies(NQ - 1)
            with sp.Fori(0, NQ) as j:
                for s, at in enumerate([W1_CC, W1_CH, W1_CB]):
                    load(st_conv, s, j, (whole, cols(w_in, at + j * P)))
            with sp.Fori(0, KC // 4) as i:
                for s in range(4):
                    load(st_out, s, i, (whole, cols(w_out, i * 4 * P + s * P)))

            def mlp(st, up, down, with_ada):
                with sp.Fori(0, NF) as q:
                    for d in range(2):
                        with sp.Fori(0, 2) as i:
                            for s in range(4):
                                if d == 0:
                                    src = cols(up, q * D + i * 4 * P + s * P)
                                else:
                                    src = down.rearrange("(q k p) n -> q p k n", q=NF, p=P)[
                                        ds(q, 1), :, :, ds(i * 4 * P + s * P, P)
                                    ].rearrange("q p k n -> p (q k) n")
                                load(st, s, q * 4 + 2 * d + i, (whole, src))
                                if with_ada and s % 2:
                                    b = s // 2
                                    sp.wait_ge(sem(f"ada_used{b}"), q * 4 + 2 * d + i + 1)
                                    sp.wait_ge(sem("mix_done"), 1)
                                    src = w_ada_2.rearrange("(q k p) n -> q k p n", q=NF, p=P)[
                                        ds(q, 1), d, :, ds(i * 3 * D + b * 3 * D // 2, 3 * D // 2)]
                                    sp.dma_start(adaw[:, b, :], src.rearrange("q p n -> p (q n)")
                                                 ).then_inc(sem(f"ada_in{b}"), 16)

            mlp(st_mlp, w_up, w_down, True)

            load(st_idx, 0, 0, (whole, cols(w_in_2, W2_QI)))
            load(st_idx, 1, 0, (whole, cols(w_in_2, W2_QI + P)))
            load(st_idx, 2, 0, (lambda d: d[:, :, 0:HD], cols(w_in_2, W2_KI, HD)),
                 (lambda d: d[:, :, HD:HD + HEADS], cols(w_in_2, W2_F, HEADS)),
                 (lambda d: d[:, :, HD + 32:HD + 32 + IDX_HEADS], cols(w_in_2, W2_WI, IDX_HEADS)))
            sp.wait_ge(sem("ada_sum"), 2)
            sp.wait_ge(sem("brow_out"), 16 * NQ)
            sp.dma_start(btab[:], bass.AP(bias_rows.tensor, P - 1, [[NREL - 1, P], [P * NREL, HEADS], [1, T]])
                         ).then_inc(sem("btab_in"), 16)

            def att_loads(g, at3, n, slots=range(3)):
                for s in slots:
                    load(st_att, s, n, (whole, cols(w_in_2, at3[s] + g * P)))

            att_loads(0, (W2_FV, W2_FQ, W2_FK), 0)
            att_loads(1, (W2_FV, W2_FQ, W2_FK), 1, (0, 1))
            sp.wait_ge(sem("forget_out"), 16)
            sp.dma_start(ftab[:], bass.AP(forget_rows.tensor, 0, [[0, P], [T, HEADS], [1, T]])
                         ).then_inc(sem("ftab_in"), 16)
            att_loads(1, (W2_FV, W2_FQ, W2_FK), 1, (2,))
            with sp.Fori(2, NQ) as g:
                att_loads(g, (W2_FV, W2_FQ, W2_FK), g)
            with sp.Fori(0, NQ) as g:
                att_loads(g, (W2_DV, W2_DQ, W2_DK), NQ + g)
            with sp.Fori(0, KC) as m:
                load(st_bra, 0, m, (whole, cols(w_in_2, W2_GF + m * P)))
                load(st_bra, 1, m, (whole, cols(w_in_2, W2_GD + m * P)))
                load(st_bra, 2, m, (lambda d: d[:, 0:NQ, :], cols(w_branch_fox_2, m * P)),
                     (lambda d: d[:, NQ:KC, :], cols(w_branch_dsa_2, m * P)))
            with sp.Fori(0, KC // 4) as i:
                for s in range(4):
                    load(st_out2, s, i, (whole, cols(w_out_2, i * 4 * P + s * P)))
            mlp(st_mlp2, w_mlp1_2, w_mlp2_2, False)

            for i in range(NT):
                sp.wait_ge(sem("otok0"), i + 1)
                sp.wait_ge(sem("otok1"), i + 1)
                sp.dma_start(out[0, i * P:(i + 1) * P, :], otok[:, i, :]).then_inc(sem("out"), 16)
            sp.wait_ge(sem("out"), 16 * NT)

        @block.gpsimd
        def _(pool):
            for s in range(SLOTS):
                pool.sem_inc(lo_ready[s], 1)
            pool.memset(ones[:], 1.0).then_inc(sem("const"), 1)
            pool.memset(epsc[:], EPS).then_inc(sem("const"), 1)

            def lo(st, s, i):
                pool.wait_ge(hi_ready[s], st.turn(s, i) + 1)
                pool.tensor_tensor(w_lo[:, s, :], raw[:, s, :], w_hi[:, s, :], ALU.subtract
                                   ).then_inc(lo_ready[s], 1)

            for st in (st_ret, st_conv, st_out, st_mlp, st_idx, st_att, st_bra, st_out2, st_mlp2):
                if st.n == 1:
                    for s in range(st.k):
                        lo(st, s, 0)
                else:
                    with pool.Fori(0, st.n) as i:
                        for s in range(st.k):
                            lo(st, s, i)

        @block.tensor
        def _(pe):
            def unit(st, s, i, r_hi, r_lo, chunk_ready=None, part=(0, KC), cols=P, ks=range(KC), bank=None,
                     opens=True, closes=True):
                bank = s if bank is None else bank
                if opens:
                    pe.wait_ge(lo_ready[s], st.turn(s, i) + 1)
                    wait(pe, bank_free[s], st.turn(s, i))
                last = None
                for k in ks[part[0]:part[1]]:
                    if chunk_ready:
                        chunk_ready(k)
                    c = slice(k * P, k * P + cols)
                    for w, r in ((w_hi, r_hi), (w_hi, r_lo), (w_lo, r_hi)):
                        last = pe.matmul(ps[0:cols, bank, :], w[:, s, c], r[:, k, :],
                                         start=(k == ks[0] and w is w_hi and r is r_hi),
                                         stop=(k == ks[-1] and w is w_lo))
                if closes:
                    last.then_inc(used[s], 1)

            def square_sum(name):
                pe.wait_ge(sem("total"), before(name) + KC)
                pe.matmul(ps[:, SA, :], ones[:], nt[:, 2, :], start=True, stop=False)
                if name == "n3":
                    pe.wait_ge(sem("total_f"), KC)
                    pe.matmul(ps[:, TR, :], ones[:], nt[:, 1, :], start=True, stop=False)
                pe.wait_ge(sem("norm_sq"), before(name) + KC)
                if name == "n3":
                    pe.matmul(ps[:, TR, :], ones[:], nsq[:, (KC - 1) % 2, :], start=False, stop=True
                              ).then_inc(sem("sum_f"), 1)
                    pe.wait_ge(sem("gones"), 1)
                pe.matmul(ps[:, SA, :], gones[:] if name == "n3" else ones[:], nsq[:, (KC - 1) % 2, :],
                          start=False, stop=True).then_inc(sem("norm_sum"), 1)

            def two_units(st, i, r_hi, r_lo, chunk_ready, ks=range(KC), part=(0, KC), lag=0):
                for step in range(part[0], part[1] + lag):
                    for s in range(2):
                        n = step - lag * s
                        if part[0] <= n < part[1]:
                            unit(st, s, i, r_hi, r_lo, chunk_ready if s == 0 else None, part=(n, n + 1), ks=ks,
                                 opens=(n == 0), closes=(n == KC - 1))

            for s in range(SLOTS):
                pe.sem_inc(used[s], 1)
            pe.wait_ge(sem("small_in"), 16)
            def turn_in(i, m):
                return pe.transpose(ps[:, m, i * P:(i + 1) * P], xtok[:, i, m * P:(m + 1) * P], ident)

            pe.wait_ge(sem("gain_in"), 16)
            pe.transpose(ps[:, KC - 1, 0:KC], vrow[0:KC, :], ident[0:KC, 0:KC]).then_inc(sem("gain_turned"), 1)
            for i in range(NT):
                pe.wait_ge(sem(f"x_in{i}"), 16)
                for m in range(KC):
                    if i == 0 and m == KC - 1:
                        pe.wait_ge(sem("gain_ready"), 1)
                    t = turn_in(i, m)
                    if i == NT - 1:
                        t.then_inc(sem("x_turned"), 1)

            def bias_rows_made():
                pe.wait_ge(sem("bias_in"), 32)
                pe.matmul(ps[0:HEADS, SB, :], rbias[:], oneh[:, 0:T], start=True, stop=True)
                pe.matmul(ps[0:HEADS, OU, 0:P], rbias[:], oneh[:, T:NREL], start=True, stop=True
                          ).then_inc(sem("brow_done"), 1)
                pe.wait_ge(sem("vrow_in"), 16 * (len(VECS) - 1))
                pe.transpose(ps[:, OU, P:P + NVEC], vrow[:], ident[0:NVEC, 0:NVEC]).then_inc(sem("vec_turned"), 1)

            def turn_v(src, dst_sem):
                for i in range(NT):
                    last = pe.transpose(ps[:, TR, i * P:(i + 1) * P], src[:, i * P:(i + 1) * P], ident)
                last.then_inc(sem(dst_sem), 1)

            def ret_scores(p):
                pe.wait_ge(sem("qk_ready"), 2 * p + 2)
                for b in range(NT):
                    if b >= 2:
                        pe.wait_ge(sem("sdec_ready"), NT * p + b - 1)
                    pe.matmul(ps[:, SA + b % 2, 0:T - b * P], kf[:, b * P:(b + 1) * P], qf[:, b * P:T],
                              start=True, stop=True).then_inc(sem("ret_s"), 1)

            def ret_out(p):
                pe.wait_ge(sem("vtok_ready"), p + 1)
                for b in range(NT):
                    pe.wait_ge(sem("sdec_ready"), NT * p + b + 1)
                    last = pe.matmul(ps[:, OU, b * P:T], vtok[:, b, :], sdec[:, b, 0:T - b * P],
                                     start=(b == 0), stop=(b == NT - 1))
                last.then_inc(sem("ret_o"), 1)

            def ret_sum(p):
                pe.wait_ge(sem("osq_ready"), p + 1)
                pe.matmul(ps[:, SA, :], ones[:], nsq[:, 0, :], start=True, stop=True).then_inc(sem("ret_sum"), 1)

            def ret(j, p):
                unit(st_ret, 0, j, u_hi, u_lo)
                ret_scores(p)
                unit(st_ret, 1, j, u_hi, u_lo)
                ret_out(p)
                pe.wait_ge(sem("vf_ready"), j + 1)
                turn_v(vf, "vf_turned")
                unit(st_ret, 2, j, u_hi, u_lo)
                ret_sum(p)
                unit(st_ret, 3, j, u_hi, u_lo)
                pe.wait_ge(sem("ret_root"), p + 1)

            pe.wait_ge(sem("x_ready"), 2)
            two_units(st_ret, 0, u_hi, u_lo, lambda k: pe.wait_ge(sem("norm_u"), before("n1") + k + 1), lag=2)
            pe.wait_ge(sem("x_ready"), KC)
            unit(st_ret, 2, 0, u_hi, u_lo, part=(0, NQ), closes=False)
            pe.wait_ge(sem("const"), 2)
            square_sum("n1")
            unit(st_ret, 2, 0, u_hi, u_lo, part=(NQ, KC), opens=False)
            bias_rows_made()
            unit(st_ret, 3, 0, u_hi, u_lo)
            pe.wait_ge(sem("vf_ready"), 1)
            turn_v(vf, "vf_turned")
            pe.wait_ge(sem("brow_read"), 2)
            pe.wait_ge(sem("vec_ready"), 1)
            with pe.Fori(1, NQ) as j:
                ret(j, j - 1)

            def conv_sum(p):
                pe.wait_ge(sem("csq_ready"), p + 1)
                pe.matmul(ps[:, SB, :], group64, nsq[:, 1, :], start=True, stop=True
                          ).then_inc(sem("conv_sum"), 1)

            unit(st_conv, 0, 0, u_hi, u_lo)
            ret_scores(NQ - 1)
            unit(st_conv, 1, 0, u_hi, u_lo)
            ret_out(NQ - 1)
            unit(st_conv, 2, 0, u_hi, u_lo)
            ret_sum(NQ - 1)
            with pe.Fori(1, NQ) as j:
                unit(st_conv, 0, j, u_hi, u_lo)
                unit(st_conv, 1, j, u_hi, u_lo)
                conv_sum(j - 1)
                unit(st_conv, 2, j, u_hi, u_lo)

            def y_ready(k):
                if k < NQ:
                    pe.wait_ge(sem("ycv_ready"), k + 1)
                else:
                    pe.wait_ge(sem("yret_ready"), k - NQ + 1)

            order = [NQ + k for k in range(NQ)] + list(range(NQ))
            two_units(st_out, 0, y_hi, y_lo, y_ready, order, (0, NQ))
            conv_sum(NQ - 1)
            two_units(st_out, 0, y_hi, y_lo, y_ready, order, (NQ, KC - 1))
            unit(st_out, 2, 0, y_hi, y_lo, ks=order, part=(0, KC - 1), closes=False)
            two_units(st_out, 0, y_hi, y_lo, y_ready, order, (KC - 1, KC))
            unit(st_out, 2, 0, y_hi, y_lo, ks=order, part=(KC - 1, KC), opens=False)
            unit(st_out, 3, 0, y_hi, y_lo)
            for s in range(4):
                unit(st_out, s, 1, y_hi, y_lo)

            def mlp_up(st, norm, q, i, between=None):
                two_units(st, q * 4 + i, u_hi, u_lo, lambda k: pe.wait_ge(sem("norm_u"), before(norm) + k + 1))
                if between:
                    between()
                for s in range(2, 4):
                    unit(st, s, q * 4 + i, u_hi, u_lo)

            def mlp_down(st, name, q, i):
                for s in range(4):
                    unit(st, s, q * 4 + 2 + i, y_hi, y_lo,
                         (lambda k: pe.wait_ge(sem("mlp_h"), q * KC + (mlp_before(name) + k + 1))) if s == 0 else None)

            def mlp_parts(st, name, norm, q0, q1):
                with pe.Fori(q0, q1) as q:
                    with pe.Fori(0, 2) as i:
                        mlp_up(st, norm, q, i)
                    with pe.Fori(0, 2) as i:
                        mlp_down(st, name, q, i)

            mlp_up(st_mlp, "n2", 0, 0, lambda: square_sum("n2"))
            mlp_up(st_mlp, "n2", 0, 1)
            with pe.Fori(0, 2) as i:
                mlp_down(st_mlp, "mlp", 0, i)
            mlp_parts(st_mlp, "mlp", "n2", 1, NF - 1)
            with pe.Fori(0, 2) as i:
                mlp_up(st_mlp, "n2", NF - 1, i)
            mlp_down(st_mlp, "mlp", NF - 1, 0)

            def ada_columns(m0, m1, done):
                for m in range(m0, m1):
                    last = pe.matmul(ps[:, SB, m:m + 1], acc[:, m * P:(m + 1) * P], ones[:, 0:1], start=True, stop=True)
                if done:
                    last.then_inc(sem("ada_sum"), 1)

            for s in range(4):
                unit(st_mlp, s, NF * 4 - 1, y_hi, y_lo)
                if s == 1:
                    pe.wait_ge(sem("acc_done"), 2 * (NF * 4 - 1) + 1)
                    ada_columns(0, 3 * KC // 2, False)
                if s == 2:
                    ada_columns(3 * KC // 2, 3 * KC, True)

            square_sum("n3")
            pe.wait_ge(sem("acc_done"), 2 * NF * 4 + 1)
            pe.wait_ge(sem("ada_ready"), 1)
            ada_columns(3 * KC, 6 * KC, True)

            ready = lambda k: pe.wait_ge(sem("norm_u"), before("n3") + k + 1)
            two_units(st_idx, 0, u_hi, u_lo, ready)
            unit(st_idx, 2, 0, u_hi, u_lo)

            def turn_wi():
                pe.wait_ge(sem("fw_ready"), 1)
                for i in range(NT):
                    last = pe.transpose(ps[:, TR, i * 64:i * 64 + 32 + IDX_HEADS],
                                        fw[0:32 + IDX_HEADS, i * P:(i + 1) * P],
                                        ident[0:32 + IDX_HEADS, 0:32 + IDX_HEADS])
                last.then_inc(sem("wi_turned"), 1)

            def idx_scores(n):
                i, h = n // IDX_HEADS + 1, n % IDX_HEADS
                if n == 0:
                    pe.wait_ge(sem("qi_ready"), 3)
                    pe.wait_ge(sem("ada_ready"), 2)
                if n >= 2:
                    pe.wait_ge(sem("relu_ready"), n - 1)
                b = HD * (h % 2)
                pe.matmul(ps[:, SA + n % 2, 0:(i + 1) * P], qi[b:b + HD, h // 2, i * P:(i + 1) * P],
                          ki[b:b + HD, 0:(i + 1) * P], start=True, stop=True).then_inc(sem("idx_s"), 1)

            def s_step(p, n, dsa):
                i, hh = n // 2, n % 2
                b = HD * hh
                if n == 0:
                    pe.wait_ge(sem("att_qk"), 2 * p + 2)
                if n >= 2:
                    pe.wait_ge(sem("att_logit"), 8 * p + n - 1)
                keys = (i + 1) * P
                bank = SA + n % 2
                pe.matmul(ps[:, bank, 0:keys], qa[b:b + HD, i * P:(i + 1) * P], ka[b:b + HD, 0:keys],
                          start=True, stop=False)
                if dsa:
                    pe.wait_ge(sem("sel_ready"), i + 1)
                    last = pe.matmul(ps[:, bank, 0:keys], identb[:], sel[:, i, 0:keys], start=False, stop=True)
                else:
                    last = pe.matmul(ps[:, bank, keys - P:keys], identb[:], causalb[:], start=False, stop=True)
                last.then_inc(sem("att_s"), 1)

            def t_step(p, n):
                i = n // 2
                pe.wait_ge(sem("att_prob"), 8 * p + n + 1)
                if n == 0:
                    pe.wait_ge(sem("vatok_ready"), p + 1)
                elif n >= 2:
                    pe.wait_ge(sem("att_probt"), 8 * p + n - 1)
                for j in range(i + 1):
                    last = pe.transpose(ps[:, TURNS[n % 2], j * P:(j + 1) * P], prob[:, n % 2, j * P:(j + 1) * P], ident)
                last.then_inc(sem("att_t"), 1)

            def pv(p, i):
                pe.wait_ge(sem("att_probt"), 8 * p + 2 * i + 2)
                for j in range(i + 1):
                    for hh in range(2):
                        b = HD * hh
                        last = pe.matmul(ps[b:b + HD, OU, i * P:(i + 1) * P], vatok[:, j, b:b + HD],
                                         probt[:, 2 * (i % 2) + hh, j * P:(j + 1) * P], start=(j == 0), stop=(j == i))
                last.then_inc(sem("att_o"), 1)

            def att(st, units, p, dsa):
                def half():
                    if units:
                        units.pop(0)()
                half()
                s_step(p, 0, dsa)
                s_step(p, 1, dsa)
                half()
                for a in range(3):
                    t_step(p, 2 * a)
                    s_step(p, 2 * a + 2, dsa)
                    t_step(p, 2 * a + 1)
                    s_step(p, 2 * a + 3, dsa)
                    if a >= 1:
                        pv(p, a - 1)
                    half()
                t_step(p, 6)
                t_step(p, 7)
                pv(p, 2)
                half()
                pv(p, 3)

            def halves(st, g, n=3):
                def one_half(s, h):
                    return lambda: unit(st, s, g, u_hi, u_lo, part=(h * KC // 2, (h + 1) * KC // 2),
                                        opens=(h == 0), closes=(h == 1))
                return [one_half(s, h) for s in range(n) for h in range(2)]

            def turn_va(g):
                pe.wait_ge(sem("va_ready"), g + 1)
                turn_v(va, "va_turned")

            n = 0
            for a, half in enumerate(halves(st_att, 0)):
                half()
                if a == 0:
                    turn_wi()
                for _ in range(2):
                    idx_scores(n)
                    n += 1
            pe.wait_ge(sem("wtok_ready"), 1)
            turn_va(0)
            pe.wait_ge(sem("relu_ready"), NT * (NT - 1))
            with pe.Fori(1, NQ) as g:
                att(st_att, halves(st_att, g), g - 1, False)
                turn_va(g)
            att(st_att, halves(st_att, NQ), NQ - 1, False)
            turn_va(NQ)
            with pe.Fori(NQ + 1, 2 * NQ) as g:
                att(st_att, halves(st_att, g), g - 1, True)
                turn_va(g)

            def branch(m):
                pe.wait_ge(lo_ready[2], st_bra.turn(2, m) + 1)
                wait(pe, bank_free[2], st_bra.turn(2, m))
                for b, k0 in ((2, 0), (SA, NQ)):
                    for k in range(k0, k0 + NQ):
                        pe.wait_ge(sem("att_y"), k + 1)
                        c = slice(k * P, (k + 1) * P)
                        for w, r in ((w_hi, y_hi), (w_hi, y_lo), (w_lo, y_hi)):
                            last = pe.matmul(ps[:, b, :], w[:, 2, c], r[:, k, :],
                                             start=(k == k0 and w is w_hi and r is y_hi),
                                             stop=(k == k0 + NQ - 1 and w is w_lo))
                last.then_inc(used[2], 1)

            att(st_bra, halves(st_bra, 0, 2), 2 * NQ - 1, True)
            branch(0)
            with pe.Fori(1, KC) as m:
                unit(st_bra, 0, m, u_hi, u_lo)
                unit(st_bra, 1, m, u_hi, u_lo)
                branch(m)

            two_units(st_out2, 0, m_hi, m_lo, lambda k: pe.wait_ge(sem("m_ready"), k + 1))
            for s in range(2, 4):
                unit(st_out2, s, 0, m_hi, m_lo)
            for s in range(4):
                unit(st_out2, s, 1, m_hi, m_lo)
            square_sum("n4")
            mlp_parts(st_mlp2, "mlp2", "n4", 0, NF - 1)
            with pe.Fori(0, 2) as i:
                mlp_up(st_mlp2, "n4", NF - 1, i)
            mlp_down(st_mlp2, "mlp2", NF - 1, 0)

            def turn_out(m, i):
                c = m // 4
                return pe.transpose(ps[:, 4 * (1 - c) + i, (m % 4) * P:(m % 4 + 1) * P],
                                    xres[:, m, i * P:(i + 1) * P], ident)

            for s in range(4):
                unit(st_mlp2, s, NF * 4 - 1, y_hi, y_lo)
                pe.wait_ge(sem("x_gained"), s + 1)
                for i in range(NT):
                    last = turn_out(s, i)
            last.then_inc(sem("o_first"), 1)
            pe.wait_ge(sem("x_gained"), KC - 1)
            for i in range(3):
                for m in range(4, KC - 1):
                    turn_out(m, i)
            pe.wait_ge(sem("total"), before("n5"))
            pe.wait_ge(sem("mlp_x"), 2 * NF * KC)
            for i in range(NT):
                pe.matmul(ps[:, 3, i:i + 1], nt[:, 2, i * P:(i + 1) * P], ones[:, 0:1], start=(i == 0), stop=False)
            pe.wait_ge(sem("norm_sq"), before("n5") + KC)
            for i in range(NT):
                last = pe.matmul(ps[:, 3, i:i + 1], nsq[:, (KC - 1) % 2, i * P:(i + 1) * P], ones[:, 0:1],
                                 start=False, stop=(i == NT - 1))
            last.then_inc(sem("norm_sum"), 1)
            pe.wait_ge(sem("x_gained"), KC)
            for i in range(3):
                turn_out(KC - 1, i).then_inc(sem("o_second"), 1)
            pe.wait_ge(sem("norm_root"), ROOTED.index("n5") + 1)
            for m in range(4, KC):
                last = turn_out(m, 3)
            last.then_inc(sem("o_second"), 1)

        @block.scalar
        def _(act):
            def ahead(st, s, i):
                t = s + AHEAD
                if t >= st.k:
                    t, i = t - st.k, i + 1
                act.wait_ge(raw_ready[t], st.landed(t, i))
                wait(act, used[t], st.turn(t, i))
                act.activation(w_hi[:, t, :], raw[:, t, :], ACT.Copy).then_inc(hi_ready[t], 1)

            def fetch_sqrt():
                act.activation(spare[:], epsc[:], ACT.Sqrt)

            def square(name, m, x_sem, x0, n=None):
                n = m if n is None else n
                act.wait_ge(sem(x_sem), x0 + m + 1)
                wait(act, sem("total"), before(name) + m)
                act.activation(nsq[:, n % 2:n % 2 + 1, :], xres[:, ds(m, 1), :], ACT.Square
                               ).then_inc(sem("norm_sq"), 1)

            def norm(name, shift):
                if name == "n3":
                    act.wait_ge(sem("both_sums"), 2)
                    act.activation(nrs[:], nrs[:], ACT.Sqrt).then_inc(sem("norm_root"), 1)
                    act.activation(nsq[:, 0, :], ps[:, TR, :], ACT.Sqrt, bias=epsc[:, 0:1], scale=1.0 / D
                                   ).then_inc(sem("root_f"), 1)
                else:
                    act.wait_ge(sem("norm_sum"), NORMS.index(name) + 1)
                    act.activation(nrs[:], ps[:, SA, :], ACT.Sqrt, bias=epsc[:, 0:1], scale=1.0 / D
                                   ).then_inc(sem("norm_root"), 1)
                    act.wait_ge(sem("norm_root"), ROOTED.index(name) + 1)

                    def shifts(m):
                        if m >= 2:
                            act.wait_ge(sem("norm_t"), KC * SHIFTED.index(name) + m - 1)
                        act.activation(nsq[:, m % 2, :], nrs[:], ACT.Copy, scale=ada[:, shift + m:shift + m + 1]
                                       ).then_inc(sem("norm_shift"), 1)

                    shifts(0)
                    for m in range(KC):
                        if m + 1 < KC:
                            shifts(m + 1)
                        act.wait_ge(sem("norm_t"), KC * SHIFTED.index(name) + m + 1)
                        act.activation(u_hi[:, m, :], nt[:, m % 3, :], ACT.Copy).then_inc(sem("norm_hi"), 1)
                    return
                for m in range(KC):
                    act.wait_ge(sem("norm_t"), KC * SHIFTED.index(name) + m + 1)
                    act.activation(u_hi[:, m, :], nt[:, m % 3, :], ACT.Identity,
                                   bias=ada[:, shift + m:shift + m + 1]).then_inc(sem("norm_hi"), 1)

            for s in range(SLOTS):
                act.sem_inc(hi_ready[s], 1)
            act.dma_start(small[:], tab[:, 0:SMALL]).then_inc(sem("small_in"), 16)
            act.dma_start(vrow[0:KC, :], norm1_g.rearrange("(j p) -> j p", p=P)).then_inc(sem("gain_in"), 16)

            act.wait_ge(sem("const"), 2)
            fetch_sqrt()

            def first_hi(s):
                act.wait_ge(raw_ready[s], st_ret.landed(s, 0))
                act.activation(w_hi[:, s, :], raw[:, s, :], ACT.Copy).then_inc(hi_ready[s], 1)

            first_hi(0)
            act.wait_ge(sem("gain_ready"), 1)
            for m in range(KC):
                act.wait_ge(sem("x_ready"), m + 1)
                act.activation(u_hi[:, m, :], xres[:, m, :], ACT.Copy,
                               scale=vec[:, VAT["norm1_g"] + m:VAT["norm1_g"] + m + 1]).then_inc(sem("norm_hi"), 1)
                if m == 1:
                    first_hi(1)
            ahead(st_ret, 0, 0)
            for m in range(KC):
                square("n1", m, "x_ready", 0)
                if m == 3:
                    ahead(st_ret, 1, 0)
            act.wait_ge(sem("const"), 2)
            act.wait_ge(sem("norm_sum"), 1)
            act.activation(r1[:], ps[:, SA, :], ACT.Sqrt, bias=epsc[:, 0:1], scale=1.0 / D
                           ).then_inc(sem("norm_root"), 1)
            act.wait_ge(sem("brow_done"), 1)
            act.activation(fbrow[:, 0:T], ps[0:HEADS, SB, :], ACT.Copy, scale=HD ** 0.5).then_inc(sem("brow_read"), 1)
            act.wait_ge(sem("vec_turned"), 1)
            act.activation(fbrow[:, T:NREL], ps[0:HEADS, OU, 0:P], ACT.Copy, scale=HD ** 0.5).then_inc(sem("brow_read"), 1)
            act.activation(vec[:, KC:NVEC], ps[:, OU, P + KC:P + NVEC], ACT.Copy).then_inc(sem("vec_ready"), 1)
            act.dma_start(decay[:], tab[:, TAT["decay"]:TAT["decay"] + NQ * T].rearrange("p (a t) -> p a t", a=NQ)
                          ).then_inc(sem("decay_in"), 16)

            def osq(p):
                act.wait_ge(sem("ret_o"), p + 1)
                act.activation(osb[:], ps[:, OU, :], ACT.Copy).then_inc(sem("osb_ready"), 1)
                act.activation(nsq[:, 0, :], ps[:, OU, :], ACT.Square).then_inc(sem("osq_ready"), 1)
            def ret_root(p):
                act.wait_ge(sem("ret_sum"), p + 1)
                act.activation(nrs[:], ps[:, SA, :], ACT.Sqrt, bias=epsc[:, 0:1], scale=1.0 / P
                               ).then_inc(sem("ret_root"), 1)
            def ret_hi(p):
                act.wait_ge(sem("ret_y"), p + 1)
                act.activation(y_hi[:, ds(NQ + p, 1), :], nt[:, 1:2, :], ACT.Copy).then_inc(sem("ret_hi"), 1)
            def vtok_evac(j):
                act.wait_ge(sem("vf_turned"), j + 1)
                act.activation(vtok[:].rearrange("p a b -> p (a b)"), ps[:, TR, :], ACT.Copy
                               ).then_inc(sem("vtok_ready"), 1)
            def sigmoid(j):
                act.wait_ge(sem("gate_in"), j + 1)
                wait(act, sem("silu_ready"), j)
                act.activation(sg[:], silu[:], ACT.Sigmoid).then_inc(sem("sg_ready"), 1)
            def ret(j, p):
                ahead(st_ret, 0, j)
                ahead(st_ret, 1, j)
                osq(p)
                vtok_evac(j)
                ahead(st_ret, 2, j)
                ret_root(p)
                ahead(st_ret, 3, j)
                sigmoid(j)
                ret_hi(p)

            ahead(st_ret, 2, 0)
            ahead(st_ret, 3, 0)
            vtok_evac(0)
            sigmoid(0)
            with act.Fori(1, NQ) as j:
                ret(j, j - 1)

            def csq(j):
                act.wait_ge(sem("ycv_done"), j + 1)
                wait(act, sem("conv_sum"), j)
                act.activation(nsq[:, 1, :], ycv[:], ACT.Square).then_inc(sem("csq_ready"), 1)
            def conv_root(p):
                act.wait_ge(sem("conv_sum"), p + 1)
                act.activation(sg[:], ps[:, SB, :], ACT.Sqrt, bias=epsc[:, 0:1], scale=1.0 / HD
                               ).then_inc(sem("conv_root"), 1)
            def conv_hi(p):
                act.wait_ge(sem("conv_t"), p + 1)
                act.activation(y_hi[:, ds(p, 1), :], nt[:, 0:1, :], ACT.Copy).then_inc(sem("conv_hi"), 1)

            ahead(st_conv, 0, 0)
            ahead(st_conv, 1, 0)
            osq(NQ - 1)
            ahead(st_conv, 2, 0)
            ret_root(NQ - 1)
            ret_hi(NQ - 1)
            with act.Fori(1, NQ) as j:
                ahead(st_conv, 0, j)
                csq(j - 1)
                ahead(st_conv, 1, j)
                conv_root(j - 1)
                ahead(st_conv, 2, j)
                conv_hi(j - 1)
            csq(NQ - 1)
            conv_root(NQ - 1)
            ahead(st_out, 0, 0)
            ahead(st_out, 1, 0)
            conv_hi(NQ - 1)

            for i in range(KC // 4):
                for s in range(4):
                    if i > 0 or s >= AHEAD:
                        ahead(st_out, s, i)
                    act.wait_ge(sem("x_mixed"), i * 4 + s + 1)
                    act.wait_ge(sem("vec_ready"), 1)
                    act.activation(u_hi[:, ds(i * 4 + s, 1), :], xres[:, ds(i * 4 + s, 1), :], ACT.Copy,
                                   scale=vec[:, ds(VAT["norm2_g"] + i * 4 + s, 1)]).then_inc(sem("norm_hi"), 1)
                    square("n2", i * 4 + s, "x_mixed", 0, s)

            def mlp(st, name, next_norm):
                def up(q, i):
                    for s in range(4):
                        ahead(st, s, q * 4 + i)
                        act.wait_ge(used[s], st.turn(s, q * 4 + i) + 1)
                        if s >= 2:
                            act.wait_ge(sem("mlp_sq"), q * KC + i * 4 + (mlp_before(name) + s - 1))
                        if s == 1:
                            act.wait_ge(sem("norm_sum"), NORMS.index(next_norm))
                        act.activation(nsq[:, s % 2, :], ps[:, s, :], ACT.Relu).then_inc(bank_free[s], 1)
                        act.wait_ge(bank_free[s], st.turn(s, q * 4 + i) + 1)
                        act.activation(y_hi[:, ds(i * 4 + s, 1), :], nsq[:, s % 2:s % 2 + 1, :], ACT.Square
                                       ).then_inc(sem("mlp_hi"), 1)
                    act.wait_ge(sem("mlp_sq"), q * KC + i * 4 + (mlp_before(name) + 4))

                def down(q, i, last=False):
                    for s in range(4):
                        if not (last and st is st_mlp2 and s + AHEAD >= 4):
                            ahead(st, s, q * 4 + 2 + i)
                        if last is not False:
                            m = i * 4 + s
                            square(next_norm, m, "mlp_x", mlp_before(name) + (NF - 1) * KC)
                            if next_norm == "n5":
                                act.wait_ge(sem("norm_sq"), before("n5") + m + 1)
                                act.activation(xres[:, m, :], xres[:, m, :], ACT.Copy,
                                               scale=vec[:, VAT["g_final_2"] + m:VAT["g_final_2"] + m + 1]
                                               ).then_inc(sem("x_gained"), 1)

                with act.Fori(0, NF - 1) as q:
                    with act.Fori(0, 2) as i:
                        up(q, i)
                    with act.Fori(0, 2) as i:
                        down(q, i)
                with act.Fori(0, 2) as i:
                    up(NF - 1, i)
                down(NF - 1, 0, 0)
                down(NF - 1, 1, 1)

            mlp(st_mlp, "mlp", "n3")
            norm("n3", shift=0)

            ahead(st_idx, 0, 0)
            for s in range(2):
                act.wait_ge(used[s], st_idx.turn(s, 0) + 1)
                act.activation(qi[:, s, :], ps[:, s, :], ACT.Copy).then_inc(bank_free[s], 1)
                ahead(st_idx, s + 1, 0)
            act.wait_ge(used[2], st_idx.turn(2, 0) + 1)
            act.activation(fw[0:HD, :], ps[HD:P, 2, :], ACT.Copy).then_inc(sem("fw_ready"), 1)
            act.activation(ki[0:HD, :], ps[0:HD, 2, :], ACT.Copy).then_inc(sem("ki_ready"), 1)
            act.activation(ki[HD:P, :], ps[0:HD, 2, :], ACT.Copy).then_inc(sem("ki_ready"), 1)
            act.wait_ge(sem("fw_ready"), 1)
            act.wait_ge(sem("ki_ready"), 2)
            act.sem_inc(bank_free[2], 1)
            for s in range(3):
                act.wait_ge(bank_free[s], st_idx.turn(s, 0) + 1)
                act.sem_inc(sem("qi_ready"), 1)
            act.wait_ge(sem("fgate_abs"), 1)
            act.activation(nt[0:HEADS, 1, :], nt[0:HEADS, 1, :], ACT.Exp, scale=-1.0).then_inc(sem("fgate_exp"), 1)
            act.wait_ge(sem("fgate_exp"), 1)
            act.activation(nt[0:HEADS, 1, :], nt[0:HEADS, 1, :], ACT.Ln, bias=ones[0:HEADS, 0:1]
                           ).then_inc(sem("fgate_ln"), 1)

            def relu(n):
                i = n // IDX_HEADS + 1
                if n == 0:
                    act.wait_ge(sem("x_final"), KC)
                act.wait_ge(sem("idx_s"), n + 1)
                if n >= 2:
                    act.wait_ge(sem("idx_acc"), n - 1)
                act.activation(nsq[:, n % 2, 0:(i + 1) * P], ps[:, SA + n % 2, 0:(i + 1) * P], ACT.Relu,
                               scale=HD ** -0.5).then_inc(sem("relu_ready"), 1)

            def va_evac(g):
                act.wait_ge(used[0], st_att.turn(0, g) + 1)
                wait(act, sem("va_turned"), g)
                act.activation(va[:], ps[:, 0, :], ACT.Copy).then_inc(sem("va_ready"), 1)
                act.wait_ge(sem("va_ready"), g + 1)
                act.sem_inc(bank_free[0], 1)
            def qk_evac(s, g):
                act.wait_ge(used[s], st_att.turn(s, g) + 1)
                wait(act, sem("att_s"), 8 * g)
                act.activation((qa, ka)[s - 1][:], ps[:, s, :], ACT.Copy).then_inc(sem("att_qk"), 1)
                act.wait_ge(sem("att_qk"), 2 * g + s)
                act.sem_inc(bank_free[s], 1)
            def vatok_evac(g):
                act.wait_ge(sem("va_turned"), g + 1)
                act.activation(vatok[:].rearrange("p a b -> p (a b)"), ps[:, TR, :], ACT.Copy
                               ).then_inc(sem("vatok_ready"), 1)
            def exps(p, a):
                for n in (2 * a, 2 * a + 1):
                    keys = (n // 2 + 1) * P
                    act.wait_ge(sem("att_logit"), 8 * p + n + 1)
                    act.activation(prob[:, n % 2, 0:keys], prob[:, n % 2, 0:keys], ACT.Exp, bias=mneg[:, n:n + 1],
                                   scale=-1.0, accum_out=rowsum[:, n:n + 1]).then_inc(sem("att_exp"), 1)
            def y_evac(p):
                act.wait_ge(sem("att_o"), NT * p + NT)
                act.activation(y_hi[:, ds(p, 1), :], ps[:, OU:OU + 1, :], ACT.Copy).then_inc(sem("att_hi"), 1)

            n = 0
            for s in range(3):
                ahead(st_att, s, 0)
                for _ in range(4):
                    relu(n)
                    n += 1
                    if n == 2:
                        act.wait_ge(sem("forget_ready"), 1)
                        act.dma_start(forget_rows, nt[0:HEADS, 1, :]).then_inc(sem("forget_out"), 16)
                if s == 0:
                    va_evac(0)
                else:
                    qk_evac(s, 0)
            vatok_evac(0)

            def att_group(g):
                p = g - 1
                ahead(st_att, 0, g)
                exps(p, 0)
                va_evac(g)
                exps(p, 1)
                ahead(st_att, 1, g)
                exps(p, 2)
                exps(p, 3)
                ahead(st_att, 2, g)
                qk_evac(1, g)
                qk_evac(2, g)
                y_evac(p)
                vatok_evac(g)

            with act.Fori(1, NQ) as g:
                att_group(g)
            att_group(NQ)
            with act.Fori(NQ + 1, 2 * NQ) as g:
                att_group(g)

            def gate(s, m):
                act.wait_ge(used[s], st_bra.turn(s, m) + 1)
                wait(act, sem("merged"), m)
                act.activation(nsq[:, s, :], ps[:, s, :], ACT.Sigmoid).then_inc(sem("gate_ready"), 1)
                act.wait_ge(sem("gate_ready"), 2 * m + s + 1)
                act.sem_inc(bank_free[s], 1)
            def m_round(m):
                act.wait_ge(sem("merged"), m + 1)
                act.activation(m_hi[:, ds(m, 1), :], nt[:, 2:3, :], ACT.Copy).then_inc(sem("m_hi"), 1)

            p = 2 * NQ - 1
            exps(p, 0)
            ahead(st_bra, 0, 0)
            exps(p, 1)
            exps(p, 2)
            ahead(st_bra, 1, 0)
            exps(p, 3)
            y_evac(p)
            gate(0, 0)
            gate(1, 0)
            ahead(st_bra, 2, 0)
            m_round(0)
            with act.Fori(1, KC) as m:
                ahead(st_bra, 0, m)
                gate(0, m)
                ahead(st_bra, 1, m)
                gate(1, m)
                ahead(st_bra, 2, m)
                m_round(m)
            fetch_sqrt()
            with act.Fori(0, KC // 4) as i:
                for s in range(4):
                    ahead(st_out2, s, i)
                    square("n4", i * 4 + s, "x_mixed2", 0, s)
            norm("n4", shift=3 * KC)
            mlp(st_mlp2, "mlp2", "n5")
            act.wait_ge(sem("norm_sum"), NORMS.index("n5") + 1)
            act.activation(rootc[:], ps[:, 3, 0:NT], ACT.Sqrt, bias=epsc[:, 0:1], scale=1.0 / D
                           ).then_inc(sem("norm_root"), 1)
            act.wait_ge(sem("norm_rinv"), INVERTED.index("n5") + 1)
            for i in range(NT):
                act.wait_ge(sem("o_second"), i + 1)
                act.activation(otok[:, i, T:D], ps[:, i, :], ACT.Copy, scale=rootc[:, i:i + 1]
                               ).then_inc(sem("otok1"), 1)

        @block.vector
        def _(dve):
            def clear_total(name):
                dve.memset(nt[:, 2, :], 0.0).then_inc(sem("total"), 1)
                if name == "n3":
                    dve.memset(nt[:, 1, :], 0.0).then_inc(sem("total_f"), 1)

            def add_square(name, m, n=None):
                n = m if n is None else n
                dve.wait_ge(sem("norm_sq"), before(name) + m + 1)
                dve.wait_ge(sem("total"), before(name) + m + 1)
                sq = nsq[:, n % 2, :]
                if name == "n3":
                    dve.wait_ge(sem("total_f"), m + 1)
                    dve.tensor_tensor(nt[:, 1, :], nt[:, 1, :], sq, ALU.add).then_inc(sem("total_f"), 1)
                    dve.scalar_tensor_tensor(nt[:, 2, :], sq, gsq[:, m:m + 1], nt[:, 2, :], ALU.mult, ALU.add
                                             ).then_inc(sem("total"), 1)
                else:
                    dve.tensor_tensor(nt[:, 2, :], nt[:, 2, :], sq, ALU.add).then_inc(sem("total"), 1)

            def norm(name, gain, shift):
                if name == "n3":
                    dve.wait_ge(sem("sum_f"), 1)
                    dve.tensor_scalar(nrs[:], ps[:, TR, :], EPS / D, EPS * EPS, ALU.mult, ALU.add
                                      ).then_inc(sem("both_sums"), 1)
                    dve.wait_ge(sem("both_sums"), 1)
                    dve.wait_ge(sem("norm_sum"), NORMS.index(name) + 1)
                    dve.scalar_tensor_tensor(nrs[:], ps[:, SA, :], 1.0 / D, nrs[:], ALU.mult, ALU.add
                                             ).then_inc(sem("both_sums"), 1)
                if name == "n3":
                    dve.wait_ge(sem("norm_root"), ROOTED.index(name) + 1)
                    dve.reciprocal(nrs[:], nrs[:]).then_inc(sem("norm_rinv"), 1)
                    dve.wait_ge(sem("norm_rinv"), INVERTED.index(name) + 1)

                def lo(m):
                    dve.wait_ge(sem("norm_hi"), before(name) + m + 1)
                    if name == "n3":
                        dve.scalar_tensor_tensor(u_lo[:, m, :], nt[:, m % 3, :], ada[:, shift + m:shift + m + 1],
                                                 u_hi[:, m, :], ALU.add, ALU.subtract).then_inc(sem("norm_u"), 1)
                    else:
                        dve.tensor_tensor(u_lo[:, m, :], nt[:, m % 3, :], u_hi[:, m, :], ALU.subtract
                                          ).then_inc(sem("norm_u"), 1)

                for m in range(KC):
                    if m >= 3:
                        dve.wait_ge(sem("norm_u"), before(name) + m - 2)
                    if name == "n3":
                        dve.scalar_tensor_tensor(nt[:, m % 3, :], xres[:, m, :], gain(m), nrs[:], ALU.mult, ALU.mult
                                                 ).then_inc(sem("norm_t"), 1)
                    else:
                        dve.wait_ge(sem("norm_shift"), m + 1)
                        dve.scalar_tensor_tensor(nt[:, m % 3, :], xres[:, m, :], gain(m), nsq[:, m % 2, :],
                                                 ALU.mult, ALU.add).then_inc(sem("norm_t"), 1)
                    if m >= 1:
                        lo(m - 1)
                lo(KC - 1)

            def col(name):
                return lambda m: vec[:, VAT[name] + m:VAT[name] + m + 1]

            for s in range(SLOTS):
                dve.sem_inc(bank_free[s], 1)
            for b in range(2):
                dve.sem_inc(sem(f"ada_used{b}"), 1)
            dve.sem_inc(sem("acc_done"), 1)
            dve.wait_ge(sem("small_in"), 16)
            dve.tensor_copy(identb[:], ident).then_inc(sem("masks"), 1)
            dve.tensor_copy(causalb[:], small[:, TAT["causal"]:TAT["causal"] + P]).then_inc(sem("masks"), 1)
            dve.memset(prod[:, 0:2], 0.0).then_inc(sem("prod_zero"), 1)
            dve.wait_ge(sem("gain_turned"), 1)
            dve.tensor_copy(vec[:, 0:KC], ps[:, KC - 1, 0:KC]).then_inc(sem("gain_ready"), 1)
            dve.wait_ge(sem("gain_ready"), 1)

            def gained_lo(name, m, at):
                dve.wait_ge(sem("norm_hi"), before(name) + m + 1)
                dve.scalar_tensor_tensor(u_lo[:, m, :], xres[:, m, :], col(at)(m), u_hi[:, m, :],
                                         ALU.mult, ALU.subtract).then_inc(sem("norm_u"), 1)

            clear_total("n1")
            for m in range(KC):
                dve.wait_ge(sem("x_turned"), m + 1)
                dve.tensor_copy(xres[:, m, :], ps[:, m, :]).then_inc(sem("x_ready"), 1)
                if m > 0:
                    gained_lo("n1", m - 1, "norm1_g")
            gained_lo("n1", KC - 1, "norm1_g")
            for m in range(KC - 1):
                add_square("n1", m)
            dve.wait_ge(sem("norm_root"), 1)
            dve.reciprocal(r1[:], r1[:]).then_inc(sem("norm_rinv"), 1)
            dve.wait_ge(sem("norm_rinv"), 1)
            dve.wait_ge(sem("rope_in"), 16)

            def v_in(j):
                dve.wait_ge(used[0], st_ret.turn(0, j) + 1)
                wait(dve, sem("vf_turned"), j)
                dve.tensor_tensor(vf[:], ps[:, 0, :], r1[:], ALU.mult).then_inc(bank_free[0], 1)
                dve.wait_ge(bank_free[0], st_ret.turn(0, j) + 1)
                dve.sem_inc(sem("vf_ready"), 1)

            v_in(0)
            dve.tensor_tensor(cosr, cosr, r1[:], ALU.mult).then_inc(sem("rope_r"), 1)
            dve.tensor_tensor(sinr, sinr, r1[:], ALU.mult).then_inc(sem("rope_r"), 1)
            dve.wait_ge(sem("rope_r"), 2)
            dve.wait_ge(sem("decay_in"), 16)
            dve.wait_ge(sem("vec_ready"), 1)

            def rotate(s, j, dst):
                dve.wait_ge(used[s], st_ret.turn(s, j) + 1)
                h = P // 2
                dve.wait_ge(sem("rotated"), 2 * j + s - 1) if not (isinstance(j, int) and 2 * j + s - 1 <= 0) else None
                dve.tensor_tensor(nt[0:h, 2, :], ps[h:P, s, :], sinr[h:P, :], ALU.mult).then_inc(sem("swapped"), 1)
                dve.tensor_tensor(nt[h:P, 2, :], ps[0:h, s, :], sinr[0:h, :], ALU.mult).then_inc(sem("swapped"), 1)
                dve.tensor_tensor(dst[:], ps[:, s, :], cosr, ALU.mult).then_inc(bank_free[s], 1)
                dve.wait_ge(sem("swapped"), 4 * j + 2 * s)
                dve.wait_ge(bank_free[s], st_ret.turn(s, j) + 1)
                dve.tensor_tensor(dst[:], dst[:], nt[:, 2, :], ALU.add).then_inc(sem("rotated"), 1)
                dve.wait_ge(sem("rotated"), 2 * j + s)
                dve.sem_inc(sem("qk_ready"), 1)

            def ret_decay(p):
                for b in range(NT):
                    dve.wait_ge(sem("ret_s"), NT * p + b + 1)
                    n = T - b * P
                    dve.tensor_tensor(sdec[:, b:b + 1, 0:n], ps[:, SA + b % 2:SA + b % 2 + 1, 0:n],
                                      decay[:, ds(p, 1), 0:n], ALU.mult).then_inc(sem("sdec_ready"), 1)

            def ret_norm(p):
                dve.wait_ge(sem("ret_root"), p + 1)
                dve.reciprocal(nrs[:], nrs[:]).then_inc(sem("ret_rinv"), 1)
                dve.wait_ge(sem("ret_rinv"), p + 1)
                dve.wait_ge(sem("osb_ready"), p + 1)
                dve.scalar_tensor_tensor(nt[:, 0, :], osb[:], vec[:, ds(VAT["ret_norm_g"] + p, 1)], nrs[:],
                                         ALU.mult, ALU.mult).then_inc(sem("ret_t"), 1)
                dve.wait_ge(sem("ret_t"), p + 1)
                dve.wait_ge(sem("silu_ready"), p + 1)
                dve.tensor_tensor(nt[:, 1, :], nt[:, 0, :], silu[:], ALU.mult).then_inc(sem("ret_y"), 1)

            def ret_lo(p):
                dve.wait_ge(sem("ret_hi"), p + 1)
                dve.tensor_tensor(y_lo[:, ds(NQ + p, 1), :], nt[:, 1:2, :], y_hi[:, ds(NQ + p, 1), :], ALU.subtract
                                  ).then_inc(sem("yret_ready"), 1)

            def gate_in(j):
                dve.wait_ge(used[3], st_ret.turn(3, j) + 1)
                wait(dve, sem("ret_y"), j)
                dve.tensor_tensor(silu[:], ps[:, 3, :], r1[:], ALU.mult).then_inc(bank_free[3], 1)
                dve.wait_ge(bank_free[3], st_ret.turn(3, j) + 1)
                dve.sem_inc(sem("gate_in"), 1)

            def silus(j):
                dve.wait_ge(sem("sg_ready"), j + 1)
                dve.tensor_tensor(silu[:], silu[:], sg[:], ALU.mult).then_inc(sem("silu_ready"), 1)

            rotate(1, 0, qf)
            rotate(2, 0, kf)
            gate_in(0)
            silus(0)
            with dve.Fori(1, NQ) as j:
                v_in(j)
                ret_decay(j - 1)
                rotate(1, j, qf)
                rotate(2, j, kf)
                ret_norm(j - 1)
                gate_in(j)
                ret_lo(j - 1)
                silus(j)

            def conv_in(j):
                dve.wait_ge(used[0], st_conv.turn(0, j) + 1)
                wait(dve, sem("prod_ready"), j)
                dve.tensor_tensor(ccs[:], ps[:, 0, :], r1sq[:], ALU.mult).then_inc(bank_free[0], 1)
                dve.wait_ge(used[1], st_conv.turn(1, j) + 1)
                dve.wait_ge(bank_free[0], st_conv.turn(0, j) + 1)
                wait(dve, sem("conv_y3"), j)
                dve.tensor_tensor(prod[:, 2:T + 2], ps[:, 1, :], ccs[:], ALU.mult).then_inc(sem("prod_ready"), 1)
                dve.wait_ge(sem("prod_ready"), j + 1)
                dve.sem_inc(bank_free[1], 1)

            def conv(j):
                taps = [vec[:, ds(VAT["conv_w"] + t * NQ + j, 1)] for t in range(3)]
                wait(dve, sem("conv_t"), j)
                dve.tensor_scalar(ycv[:], prod[:, 2:T + 2], taps[2], None, ALU.mult).then_inc(sem("conv_taps"), 1)
                dve.wait_ge(sem("conv_taps"), 2 * j + 1)
                dve.scalar_tensor_tensor(ycv[:], prod[:, 1:T + 1], taps[1], ycv[:], ALU.mult, ALU.add
                                         ).then_inc(sem("conv_taps"), 1)
                dve.wait_ge(sem("conv_taps"), 2 * j + 2)
                dve.scalar_tensor_tensor(ycv[:], prod[:, 0:T], taps[0], ycv[:], ALU.mult, ALU.add
                                         ).then_inc(sem("conv_y3"), 1)
                dve.wait_ge(sem("conv_y3"), j + 1)
                dve.wait_ge(used[2], st_conv.turn(2, j) + 1)
                dve.tensor_tensor(ycv[:], ps[:, 2, :], ycv[:], ALU.mult).then_inc(bank_free[2], 1)
                dve.wait_ge(bank_free[2], st_conv.turn(2, j) + 1)
                dve.tensor_tensor(ycv[:], ycv[:], r1[:], ALU.mult).then_inc(sem("ycv_done"), 1)

            def conv_norm(p):
                dve.wait_ge(sem("conv_root"), p + 1)
                dve.reciprocal(sg[:], sg[:]).then_inc(sem("conv_rinv"), 1)
                dve.wait_ge(sem("conv_rinv"), p + 1)
                dve.scalar_tensor_tensor(nt[:, 0, :], ycv[:], vec[:, ds(VAT["conv_norm_g"] + p, 1)], sg[:],
                                         ALU.mult, ALU.mult).then_inc(sem("conv_t"), 1)
                dve.wait_ge(sem("conv_hi"), p + 1)
                dve.tensor_tensor(y_lo[:, ds(p, 1), :], nt[:, 0:1, :], y_hi[:, ds(p, 1), :], ALU.subtract
                                  ).then_inc(sem("ycv_ready"), 1)

            ret_decay(NQ - 1)
            dve.wait_ge(sem("vf_turned"), NQ)
            dve.tensor_tensor(r1sq[:], r1[:], r1[:], ALU.mult).then_inc(sem("r1sq"), 1)
            dve.wait_ge(sem("r1sq"), 1)
            conv_in(0)
            ret_norm(NQ - 1)
            ret_lo(NQ - 1)
            dve.wait_ge(sem("prod_zero"), 1)
            conv(0)
            with dve.Fori(1, NQ) as j:
                conv_in(j)
                conv_norm(j - 1)
                conv(j)
            conv_norm(NQ - 1)
            dve.wait_ge(sem("ycv_ready"), NQ)
            dve.sem_inc(sem("mix_done"), 1)

            def add(st, n, s, i, m, scale, done):
                dve.wait_ge(used[s], st.turn(s, n) + 1)
                dve.wait_ge(bank_free[s], st.turn(s, n))
                dve.scalar_tensor_tensor(xres[:, ds(m, 1), :], ps[:, s:s + 1, :], scale, xres[:, ds(m, 1), :],
                                         ALU.mult, ALU.add).then_inc(sem(done), 1)
                dve.wait_ge(sem(done), i + 1)
                dve.sem_inc(bank_free[s], 1)

            def wout(st, scale, done, next_norm, gained=False):
                clear_total(next_norm)
                for i in range(KC // 4):
                    for s in range(4):
                        m = i * 4 + s
                        add(st, i, s, m, m, scale(m), done)
                        if gained:
                            gained_lo("n2", m, "norm2_g")
                        if i * 4 + s < KC - 1:
                            add_square(next_norm, i * 4 + s)

            wout(st_out, lambda m: 1.0, "x_mixed", "n2", gained=True)

            def ada_piece(q, d, i, b):
                n = q * 4 + 2 * d + i
                dve.wait_ge(sem(f"ada_in{b}"), 16 * (n + 1))
                dve.wait_ge(sem("acc_done"), 2 * n + b + 1)
                a = acc[:, ds(i * 3 * D + b * 3 * D // 2, 3 * D // 2)]
                c = vec[:, ds(VAT["c_2"] + 2 * q + d, 1)]
                if isinstance(q, int) and q == 0 and d == 0:
                    dve.tensor_scalar(a, adaw[:, b, :], c, None, ALU.mult).then_inc(sem("acc_done"), 1)
                else:
                    dve.scalar_tensor_tensor(a, adaw[:, b, :], c, a, ALU.mult, ALU.add).then_inc(sem("acc_done"), 1)
                dve.wait_ge(sem("acc_done"), 2 * n + b + 2)
                dve.sem_inc(sem(f"ada_used{b}"), 1)

            def modulation(half):
                a, c = half * 3 * KC, slice(half * 3 * KC, (half + 1) * 3 * KC)
                gain, g_at = (gain1, VAT["g_norm1_2"]) if half == 0 else (gain2, VAT["g_norm2_2"])
                dve.wait_ge(sem("ada_sum"), half + 1)
                dve.tensor_tensor(ada[:, c], ps[:, SB, c], vec[:, VAT["b_ada_2"] + a:VAT["b_ada_2"] + a + 3 * KC],
                                  ALU.add).then_inc(sem("ada_ready"), 1)
                dve.wait_ge(sem("ada_ready"), half + 1)
                dve.scalar_tensor_tensor(gain[:], ada[:, a + KC:a + 2 * KC], 1.0, vec[:, g_at:g_at + KC],
                                         ALU.add, ALU.mult).then_inc(sem("gains"), 1)
                if half == 0:
                    dve.wait_ge(sem("gains"), 1)
                    dve.tensor_tensor(gain1[:], gain1[:], vec[:, VAT["final_norm_g"]:VAT["final_norm_g"] + KC],
                                      ALU.mult).then_inc(sem("gains"), 1)

            def mlp(st, name, scale, with_ada, next_norm, factor=None):
                def up(q):
                    with dve.Fori(0, 2) as i:
                        for s in range(4):
                            if factor is not None and s == 0:
                                wait(dve, sem("mlp_x"), q * KC + mlp_before(name))
                            dve.wait_ge(bank_free[s], st.turn(s, q * 4 + i) + 1)
                            dve.tensor_tensor(nt[:, s % 2, :], nsq[:, s % 2, :], nsq[:, s % 2, :], ALU.mult
                                              ).then_inc(sem("mlp_sq"), 1)
                            dve.wait_ge(sem("mlp_sq"), q * KC + i * 4 + (mlp_before(name) + s + 1))
                            dve.wait_ge(sem("mlp_hi"), q * KC + i * 4 + (mlp_before(name) + s + 1))
                            m = ds(i * 4 + s, 1)
                            dve.tensor_tensor(y_lo[:, m, :], nt[:, s % 2:s % 2 + 1, :], y_hi[:, m, :], ALU.subtract
                                              ).then_inc(sem("mlp_h"), 1)
                            dve.wait_ge(sem("mlp_h"), q * KC + i * 4 + (mlp_before(name) + s + 1))
                            if with_ada and s % 2:
                                ada_piece(q, 0, i, s // 2)

                def down(q, i, last=False):
                    for s in range(4):
                        if with_ada and s % 2:
                            ada_piece(q, 1, i, s // 2)
                        if with_ada and last and i == 1 and s == 3:
                            modulation(0)
                        n, m = q * KC + i * 4 + (mlp_before(name) + s), i * 4 + s
                        if factor is None:
                            add(st, q * 4 + 2 + i, s, n, m, scale(m), "mlp_x")
                        else:
                            dve.wait_ge(used[s], st.turn(s, q * 4 + 2 + i) + 1)
                            wait(dve, sem("mlp_x"), n)
                            dve.tensor_tensor(nt[:, 0, :], ps[:, s, :], factor[:], ALU.mult
                                              ).then_inc(bank_free[s], 1)
                            dve.wait_ge(bank_free[s], st.turn(s, q * 4 + 2 + i) + 1)
                            if scale is None:
                                dve.tensor_tensor(xres[:, ds(m, 1), :], nt[:, 0:1, :], xres[:, ds(m, 1), :], ALU.add
                                                  ).then_inc(sem("mlp_x"), 1)
                            else:
                                dve.scalar_tensor_tensor(xres[:, ds(m, 1), :], nt[:, 0:1, :], scale(m),
                                                         xres[:, ds(m, 1), :], ALU.mult, ALU.add
                                                         ).then_inc(sem("mlp_x"), 1)
                        if last and i * 4 + s < KC - 1:
                            add_square(next_norm, i * 4 + s)

                if factor is None:
                    first = 0
                else:
                    first = 1
                    up(0)
                    dve.wait_ge(sem("norm_sum"), NORMS.index({"mlp": "n2", "mlp2": "n4"}[name]) + 1)
                    dve.tensor_scalar(factor[:], ps[:, SA, :], 1.0 / D, EPS, ALU.mult, ALU.add
                                      ).then_inc(sem("mean_sq"), 1)
                    dve.wait_ge(sem("mean_sq"), MLPS.index(name) + 1)
                    dve.reciprocal(factor[:], factor[:]).then_inc(sem("factor"), 1)
                    dve.wait_ge(sem("factor"), MLPS.index(name) + 1)
                    for i in range(2):
                        down(0, i)
                with dve.Fori(first, NF - 1) as q:
                    up(q)
                    with dve.Fori(0, 2) as i:
                        down(q, i)
                up(NF - 1)
                clear_total(next_norm)
                for i in range(2):
                    down(NF - 1, i, True)

            dve.wait_ge(sem("brow_out"), 16 * NQ)
            dve.tensor_tensor(gsq[:], vec[:, VAT["final_norm_g"]:VAT["final_norm_g"] + KC],
                              vec[:, VAT["final_norm_g"]:VAT["final_norm_g"] + KC], ALU.mult).then_inc(sem("gsq"), 1)
            dve.wait_ge(sem("gsq"), 1)
            dve.tensor_scalar(gones[:], ones[:], gsq[:, KC - 1:KC], None, ALU.mult).then_inc(sem("gones"), 1)
            mlp(st_mlp, "mlp", None, True, "n3", factor=nrs)
            dve.wait_ge(sem("gains"), 2)
            norm("n3", lambda m: gain1[:, m:m + 1], shift=0)
            modulation(1)
            dve.wait_ge(sem("root_f"), 1)
            dve.reciprocal(nsq[:, 0, :], nsq[:, 0, :]).then_inc(sem("rinv_f"), 1)
            dve.wait_ge(sem("rinv_f"), 1)
            for m in range(KC):
                g = VAT["final_norm_g"] + m
                dve.scalar_tensor_tensor(xres[:, m, :], xres[:, m, :], vec[:, g:g + 1], nsq[:, 0, :],
                                         ALU.mult, ALU.mult).then_inc(sem("x_final"), 1)

            dve.wait_ge(sem("bfor_in"), 16)
            dve.wait_ge(sem("masks"), 2)
            dve.tensor_copy(sel[:, 0, 0:P], causalb[:]).then_inc(sem("sel_ready"), 1)
            dve.wait_ge(sem("fw_ready"), 1)
            dve.wait_ge(sem("norm_u"), before("n3") + KC)
            f = fw[0:HEADS, :]
            dve.tensor_scalar(nt[0:HEADS, 1, :], f, bfor[:, 0:1], None, ALU.add).then_inc(sem("fgate_z"), 1)
            dve.tensor_scalar(nt[0:HEADS, 2, :], f, bfor[:, 0:1], 0.0, ALU.add, ALU.min).then_inc(sem("fgate_z"), 1)
            dve.wait_ge(sem("fgate_z"), 2)
            dve.scalar_tensor_tensor(nt[0:HEADS, 1, :], nt[0:HEADS, 2, :], -2.0, nt[0:HEADS, 1, :],
                                     ALU.mult, ALU.add).then_inc(sem("fgate_abs"), 1)
            dve.memset(nrs[0:HEADS, :], 1.0).then_inc(sem("fgate_abs"), 1)
            dve.wait_ge(sem("wi_turned"), 1)
            for i in range(NT):
                last = dve.tensor_scalar(wtok[:, IDX_HEADS * i:IDX_HEADS * (i + 1)],
                                         ps[:, TR, i * 64 + 32:i * 64 + 32 + IDX_HEADS], IDX_HEADS ** -0.5, None, ALU.mult)
            last.then_inc(sem("wtok_ready"), 1)
            dve.wait_ge(sem("fgate_ln"), 1)
            dve.tensor_tensor(nt[0:HEADS, 2, :], nt[0:HEADS, 2, :], nt[0:HEADS, 1, :], ALU.subtract
                              ).then_inc(sem("fgate_log"), 1)
            dve.wait_ge(sem("fgate_log"), 1)
            dve.wait_ge(sem("fgate_abs"), 2)
            dve.tensor_tensor_scan(nt[0:HEADS, 0, :], nrs[0:HEADS, :], nt[0:HEADS, 2, :], 0.0, ALU.mult, ALU.add
                                   ).then_inc(sem("fgate_log"), 1)
            dve.wait_ge(sem("fgate_log"), 2)
            dve.tensor_scalar(nt[0:HEADS, 1, :], nt[0:HEADS, 0, :], -(HD ** 0.5), None, ALU.mult
                              ).then_inc(sem("forget_ready"), 1)
            dve.wait_ge(sem("wtok_ready"), 1)
            for n in range(IDX_HEADS * (NT - 1)):
                i, h = n // IDX_HEADS + 1, n % IDX_HEADS
                keys = (i + 1) * P
                w = wtok[:, IDX_HEADS * i + h:IDX_HEADS * i + h + 1]
                dve.wait_ge(sem("relu_ready"), n + 1)
                wk = work[:, i - 1, 0:keys]
                if h == 0:
                    dve.tensor_scalar(wk, nsq[:, n % 2, 0:keys], w, 0.0, ALU.mult, ALU.add).then_inc(sem("idx_acc"), 1)
                else:
                    dve.wait_ge(sem("idx_acc"), n)
                    dve.scalar_tensor_tensor(wk, nsq[:, n % 2, 0:keys], w, wk, ALU.mult, ALU.add
                                             ).then_inc(sem("idx_acc"), 1)
                if h == IDX_HEADS - 1:
                    dve.wait_ge(sem("idx_acc"), n + 1)
                    d = work[:, i - 1, keys - P:keys]
                    dve.tensor_tensor(d, d, causalb[:], ALU.add).then_inc(sem("iscore"), 1)

            def logits(p, n, tab_at):
                keys = (n // 2 + 1) * P
                dve.wait_ge(sem("att_s"), 8 * p + n + 1)
                if n >= 2:
                    dve.wait_ge(sem("att_t"), 8 * p + n - 1)
                else:
                    wait(dve, sem("att_t"), 8 * p)
                dve.tensor_tensor_reduce(prob[:, n % 2, 0:keys], ps[:, SA + n % 2, 0:keys],
                                         tab_at(p, n % 2, keys), -(HD ** -0.5), -MASKED, ALU.add, ALU.min,
                                         mneg[:, n:n + 1]).then_inc(sem("att_logit"), 1)
            def weights(p, n):
                keys = (n // 2 + 1) * P
                dve.wait_ge(sem("att_exp"), 8 * p + n + 1)
                dve.reciprocal(rinv[:, n:n + 1], rowsum[:, n:n + 1]).then_inc(sem("att_rinv"), 1)
                dve.wait_ge(sem("att_rinv"), 8 * p + n + 1)
                dve.tensor_scalar(prob[:, n % 2, 0:keys], prob[:, n % 2, 0:keys], rinv[:, n:n + 1], None, ALU.mult
                                  ).then_inc(sem("att_prob"), 1)
            def turned(p, n):
                i, keys = n // 2, (n // 2 + 1) * P
                dve.wait_ge(sem("att_t"), 8 * p + n + 1)
                if n % 2 == 0:
                    wait(dve, sem("att_o"), NT * p + i - 1)
                dve.tensor_copy(probt[:, 2 * (i % 2) + n % 2, 0:keys], ps[:, TURNS[n % 2], 0:keys]
                                ).then_inc(sem("att_probt"), 1)
            def y_lows(p):
                dve.wait_ge(sem("att_hi"), p + 1)
                dve.tensor_tensor(y_lo[:, ds(p, 1), :], ps[:, OU:OU + 1, :], y_hi[:, ds(p, 1), :], ALU.subtract
                                  ).then_inc(sem("att_y"), 1)
            def fox_tab(p, hh, keys):
                return ftab[:, 2 * p + hh, 0:keys]
            def dsa_tab(p, hh, keys):
                return btab[:, 2 * (p - NQ) + hh, T - keys:T]

            plan = selection_plan((0, 2, 0, 2, 0, 1, 0, 2, 4) * NQ)

            def rounds(part):
                for i, n in plan[part]:
                    wk = work[:, i - 1, 0:(i + 1) * P]
                    r = (TOPK // 8) * (i - 1) + n
                    dve.max(top8[:], wk).then_inc(sem("selection"), 1)
                    dve.wait_ge(sem("selection"), 2 * r + 1)
                    dve.match_replace(wk, top8[:], wk, TAKEN).then_inc(sem("selection"), 1)
                    dve.wait_ge(sem("selection"), 2 * r + 2)
                    if n == TOPK // 8 - 1:
                        dve.tensor_scalar(sel[:, i, 0:(i + 1) * P], wk, 0.5 * (MASKED + TAKEN), MASKED,
                                          ALU.is_gt, ALU.mult).then_inc(sem("sel_ready"), 1)

            def att(p, tab_at, select=False):
                for a in range(4):
                    if a > 0:
                        turned(p, 2 * a - 2)
                    logits(p, 2 * a, tab_at)
                    if a > 0:
                        turned(p, 2 * a - 1)
                    logits(p, 2 * a + 1, tab_at)
                    if select:
                        rounds(9 * p + 2 * a)
                    weights(p, 2 * a)
                    weights(p, 2 * a + 1)
                    if select:
                        rounds(9 * p + 2 * a + 1)
                turned(p, 6)
                turned(p, 7)
                if select:
                    rounds(9 * p + 8)
                y_lows(p)

            dve.wait_ge(sem("iscore"), NT - 1)
            dve.wait_ge(sem("ftab_in"), 16)
            for p in range(NQ):
                att(p, fox_tab, True)
            dve.wait_ge(sem("btab_in"), 16)
            for p in range(NQ, 2 * NQ):
                att(p, dsa_tab)

            def merge_branches(m):
                dve.wait_ge(used[2], st_bra.turn(2, m) + 1)
                dve.wait_ge(sem("gate_ready"), 2 * m + 2)
                dve.tensor_tensor(nt[:, 0, :], ps[:, 2, :], nsq[:, 0, :], ALU.mult).then_inc(sem("gated"), 1)
                dve.tensor_tensor(nt[:, 1, :], ps[:, SA, :], nsq[:, 1, :], ALU.mult).then_inc(sem("gated"), 1)
                dve.wait_ge(sem("gated"), 2 * m + 2)
                dve.sem_inc(bank_free[2], 1)
                dve.tensor_tensor(nt[:, 2, :], nt[:, 0, :], nt[:, 1, :], ALU.add).then_inc(sem("merged"), 1)
                dve.wait_ge(sem("m_hi"), m + 1)
                dve.tensor_tensor(m_lo[:, ds(m, 1), :], nt[:, 2:3, :], m_hi[:, ds(m, 1), :], ALU.subtract
                                  ).then_inc(sem("m_ready"), 1)

            with dve.Fori(0, KC) as m:
                merge_branches(m)
            dve.wait_ge(sem("m_ready"), KC)
            wout(st_out2, lambda m: ada[:, ds(2 * KC + m, 1)], "x_mixed2", "n4")
            norm("n4", lambda m: gain2[:, m:m + 1], shift=3 * KC)
            mlp(st_mlp2, "mlp2", lambda m: ada[:, ds(5 * KC + m, 1)], False, "n5", factor=nrs)
            dve.wait_ge(sem("norm_root"), ROOTED.index("n5") + 1)
            dve.reciprocal(rootc[:], rootc[:]).then_inc(sem("norm_rinv"), 1)
            dve.wait_ge(sem("norm_rinv"), INVERTED.index("n5") + 1)
            dve.wait_ge(sem("o_first"), 1)
            for i in range(NT):
                dve.tensor_scalar(otok[:, i, 0:T], ps[:, 4 + i, :], rootc[:, i:i + 1], None, ALU.mult
                                  ).then_inc(sem("otok0"), 1)
    return nc


_INS = ["x", "norm1_g", "w_in", "conv_w", "conv_norm_g", "ret_norm_g", "w_out", "norm2_g", "w_up", "w_down",
        "final_norm_g", "c_2", "w_ada_2", "b_ada_2", "g_norm1_2", "w_in_2", "b_forget_2", "rel_bias_2",
        "w_branch_fox_2", "w_branch_dsa_2", "w_out_2", "g_norm2_2", "w_mlp1_2", "w_mlp2_2", "g_final_2"]


def kernel(**inputs):
    import concourse.bacc as bacc
    from concourse.bass_utils import run_bass_kernel_spmd

    nc = bacc.Bacc("TRN2", target_bir_lowering=False, num_devices=1)
    arrays = {"tab": tables()}
    for name in _INS:
        arrays[name] = np.ascontiguousarray(inputs[name])
    args = {n: nc.dram_tensor(n, a.shape, mybir.dt.from_np(a.dtype), kind="ExternalInput").ap()
            for n, a in arrays.items()}
    args["out"] = nc.dram_tensor("out", (1, T, D), F32, kind="ExternalOutput").ap()
    build(nc, **args)
    r = run_bass_kernel_spmd(nc, [arrays], core_ids=[0])
    return r.results[0]["out"]
```
